# Optimizing a Trainium2 kernel written in Bass

```python
import jax, jax.numpy as jnp
from jax import lax
import numpy as np

D_MODEL = 1024
BATCH = 1
SEQ = 512
DEPTH = 2
DEC_BATCH = 8
DEC_SEQ = 4
PAST_LEN = 4096
PAGE_SIZE = 128

N_MIXERS = 2
N_GLA = (DEPTH + 1) // 2
N_HGRN = DEPTH // 2
CHUNK = 64
GLA_HEADS = 4
GLA_KEY_DIM = D_MODEL // 2
GLA_VAL_DIM = D_MODEL
GLA_DK = GLA_KEY_DIM // GLA_HEADS
GLA_DV = GLA_VAL_DIM // GLA_HEADS
GLA_GATE_RANK = 16
GLA_GATE_NORM = 16.0
HGRN_EXPAND = 128
HGRN_HEADS = D_MODEL // HGRN_EXPAND
HGRN_F_DIM = D_MODEL
HGRN_I_DIM = D_MODEL
HGRN_DF = HGRN_F_DIM // HGRN_HEADS
HGRN_DI = HGRN_I_DIM // HGRN_HEADS
D_FF = 2816
PLE_DIM = 256
RMS_EPS = 1e-6

kernel_name = 'hybrid_gla_hgrn2_macaron_step'

def rms_norm(x, w):
    xf = x.astype(jnp.float32)
    y = xf * lax.rsqrt(jnp.mean(xf * xf, axis=-1, keepdims=True) + RMS_EPS)
    return (y * w.astype(jnp.float32)).astype(x.dtype)

def swiglu(h, w_gu, w_down):
    gate, up = jnp.split(h @ w_gu, 2, axis=-1)
    return (jax.nn.silu(gate) * up) @ w_down

def chunked_gated_linear_recurrence(q, k, v, g, s0, scale):
    B, T, H, K = q.shape
    V = v.shape[-1]
    c = min(CHUNK, T)
    n = -(-T // c)
    pad = n * c - T
    f32 = jnp.float32
    q, k, v, g = (a.astype(f32) for a in (q, k, v, g))
    if pad:
        pw = ((0, 0), (0, pad), (0, 0), (0, 0))
        q, k, v, g = (jnp.pad(a, pw) for a in (q, k, v, g))
    to_chunks = lambda a: jnp.moveaxis(a.reshape(B, n, c, H, a.shape[-1]), 1, 0)
    mask = jnp.tril(jnp.ones((c, c), dtype=bool))[None, :, :, None, None]

    def step(S, inp):
        qc, kc, vc, gc = inp
        b = jnp.cumsum(gc, axis=1)
        rel = b[:, :, None] - b[:, None, :]
        decay = jnp.exp(jnp.where(mask, rel, -jnp.inf))
        attn = jnp.einsum('bthk,bshk,btshk->bhts', qc, kc, decay) * scale
        o_intra = jnp.einsum('bhts,bshv->bthv', attn, vc)
        o_inter = jnp.einsum('bthk,bhkv->bthv', qc * jnp.exp(b), S) * scale
        b_last = b[:, -1]
        k_dec = kc * jnp.exp(b_last[:, None] - b)
        S_new = S * jnp.exp(b_last)[..., None] + jnp.einsum('bshk,bshv->bhkv', k_dec, vc)
        return S_new, o_intra + o_inter

    S, o = lax.scan(step, s0.astype(f32), (to_chunks(q), to_chunks(k), to_chunks(v), to_chunks(g)))
    o = jnp.moveaxis(o, 0, 1).reshape(B, n * c, H, V)[:, :T]
    return o, S.astype(s0.dtype)

def gla_mixer(u, w_in, w_gk_up, b_gk, gn, w_out, s0):
    B, T, _ = u.shape
    z = u @ w_in
    cuts = np.cumsum([GLA_KEY_DIM, GLA_KEY_DIM, GLA_VAL_DIM, GLA_VAL_DIM]).tolist()
    q, k, v, g, r = jnp.split(z, cuts, axis=-1)
    gk = jax.nn.log_sigmoid((r @ w_gk_up + b_gk).astype(jnp.float32)) / GLA_GATE_NORM
    heads = lambda a, d: a.reshape(B, T, GLA_HEADS, d)
    o, s = chunked_gated_linear_recurrence(heads(q, GLA_DK), heads(k, GLA_DK), heads(v, GLA_DV),
                                           heads(gk, GLA_DK), s0, GLA_DK ** -0.5)
    o = rms_norm(o.astype(u.dtype), gn) * jax.nn.silu(heads(g, GLA_DV))
    return o.reshape(B, T, GLA_VAL_DIM) @ w_out, s

def hgrn2_mixer(u, w_in, gn, w_out, lb, s0):
    B, T, _ = u.shape
    z = u @ w_in
    cuts = [HGRN_F_DIM, 2 * HGRN_F_DIM, 2 * HGRN_F_DIM + HGRN_I_DIM]
    q, f, i, g = jnp.split(z, cuts, axis=-1)
    q = jax.nn.silu(q)
    f = f.astype(jnp.float32)
    log_f = jnp.logaddexp(jnp.log(lb), jnp.log1p(-lb) + jax.nn.log_sigmoid(f))
    k = (1.0 - lb) * jax.nn.sigmoid(-f)
    heads = lambda a, d: a.reshape(B, T, HGRN_HEADS, d)
    o, s = chunked_gated_linear_recurrence(heads(q, HGRN_DF), heads(k, HGRN_DF), heads(i, HGRN_DI),
                                           heads(log_f, HGRN_DF), s0, 1.0)
    o = rms_norm(o.astype(u.dtype), gn) * jax.nn.silu(heads(g, HGRN_DI))
    return o.reshape(B, T, HGRN_I_DIM) @ w_out, s

def trunk(x, p, st_gla, st_hgrn, ffn1_norm, ffn1_w_gu, ffn1_w_down, mix_norm,
          gla_w_in, gla_w_gk_up, gla_b_gk, gla_gn, gla_w_out,
          hgrn_w_in, hgrn_gn, hgrn_w_out, hgrn_lower_bounds,
          ffn2_norm, ffn2_w_gu, ffn2_w_down, ple_norm, ple_w_gate, ple_w_proj, final_norm):
    lbs = jax.nn.softmax(hgrn_lower_bounds.astype(jnp.float32), axis=0)
    lbs = jnp.cumsum(lbs, axis=0) - lbs[0]
    new_gla, new_hgrn = [], []
    h = x
    for li in range(DEPTH):
        h = h + 0.5 * swiglu(rms_norm(h, ffn1_norm[li]), ffn1_w_gu[li], ffn1_w_down[li])
        u = rms_norm(h, mix_norm[li])
        j = li // N_MIXERS
        if li % N_MIXERS == 0:
            m, s = gla_mixer(u, gla_w_in[j], gla_w_gk_up[j], gla_b_gk[j], gla_gn[j], gla_w_out[j], st_gla[j])
            new_gla.append(s)
        else:
            m, s = hgrn2_mixer(u, hgrn_w_in[j], hgrn_gn[j], hgrn_w_out[j], lbs[li], st_hgrn[j])
            new_hgrn.append(s)
        h = h + m
        h = h + 0.5 * swiglu(rms_norm(h, ffn2_norm[li]), ffn2_w_gu[li], ffn2_w_down[li])
        gate = jax.nn.sigmoid(rms_norm(h, ple_norm[li]) @ ple_w_gate[li])
        h = h + gate * (p[li] @ ple_w_proj[li])
    return rms_norm(h, final_norm), jnp.stack(new_gla), jnp.stack(new_hgrn)

def setup_inputs(seed: int = 0) -> dict:
    key = jax.random.key(seed)
    ks = iter(jax.random.split(key, 40))
    nrm = lambda shape, scale: jax.random.normal(next(ks), shape, jnp.float32) * scale
    gain = lambda shape: 1.0 + nrm(shape, 0.02)
    D = D_MODEL
    gla_in_w = 2 * GLA_KEY_DIM + 2 * GLA_VAL_DIM + GLA_GATE_RANK
    hgrn_in_w = 2 * HGRN_F_DIM + 2 * HGRN_I_DIM
    return {
        'x_prompt': nrm((BATCH, SEQ, D), 1.0),
        'x_sample': nrm((DEC_BATCH, DEC_SEQ, D), 1.0),
        'state_gla': nrm((N_GLA, DEC_BATCH, GLA_HEADS, GLA_DK, GLA_DV), 0.5),
        'state_hgrn': nrm((N_HGRN, DEC_BATCH, HGRN_HEADS, HGRN_DF, HGRN_DI), 0.5),
        'p_prompt': nrm((DEPTH, BATCH, SEQ, PLE_DIM), 1.0),
        'p_sample': nrm((DEPTH, DEC_BATCH, DEC_SEQ, PLE_DIM), 1.0),
        'ffn1_norm': gain((DEPTH, D)),
        'ffn1_w_gu': nrm((DEPTH, D, 2 * D_FF), D ** -0.5),
        'ffn1_w_down': nrm((DEPTH, D_FF, D), D_FF ** -0.5),
        'mix_norm': gain((DEPTH, D)),
        'gla_w_in': nrm((N_GLA, D, gla_in_w), D ** -0.5),
        'gla_w_gk_up': nrm((N_GLA, GLA_GATE_RANK, GLA_KEY_DIM), GLA_GATE_RANK ** -0.5),
        'gla_b_gk': nrm((N_GLA, GLA_KEY_DIM), 0.1),
        'gla_gn': gain((N_GLA, GLA_DV)),
        'gla_w_out': nrm((N_GLA, GLA_VAL_DIM, D), GLA_VAL_DIM ** -0.5),
        'hgrn_w_in': nrm((N_HGRN, D, hgrn_in_w), D ** -0.5),
        'hgrn_gn': gain((N_HGRN, HGRN_DI)),
        'hgrn_w_out': nrm((N_HGRN, HGRN_I_DIM, D), HGRN_I_DIM ** -0.5),
        'hgrn_lower_bounds': nrm((DEPTH, HGRN_F_DIM), 0.1),
        'ffn2_norm': gain((DEPTH, D)),
        'ffn2_w_gu': nrm((DEPTH, D, 2 * D_FF), D ** -0.5),
        'ffn2_w_down': nrm((DEPTH, D_FF, D), D_FF ** -0.5),
        'ple_norm': gain((DEPTH, D)),
        'ple_w_gate': nrm((DEPTH, D, D), D ** -0.5),
        'ple_w_proj': nrm((DEPTH, PLE_DIM, D), PLE_DIM ** -0.5),
        'final_norm': gain((D,)),
    }

def reference(x_prompt, x_sample, state_gla, state_hgrn, p_prompt, p_sample,
              ffn1_norm, ffn1_w_gu, ffn1_w_down, mix_norm,
              gla_w_in, gla_w_gk_up, gla_b_gk, gla_gn, gla_w_out,
              hgrn_w_in, hgrn_gn, hgrn_w_out, hgrn_lower_bounds,
              ffn2_norm, ffn2_w_gu, ffn2_w_down, ple_norm, ple_w_gate, ple_w_proj, final_norm):
    weights = (ffn1_norm, ffn1_w_gu, ffn1_w_down, mix_norm,
               gla_w_in, gla_w_gk_up, gla_b_gk, gla_gn, gla_w_out,
               hgrn_w_in, hgrn_gn, hgrn_w_out, hgrn_lower_bounds,
               ffn2_norm, ffn2_w_gu, ffn2_w_down, ple_norm, ple_w_gate, ple_w_proj, final_norm)
    bp = x_prompt.shape[0]
    zero_gla = jnp.zeros((N_GLA, bp, GLA_HEADS, GLA_DK, GLA_DV), jnp.float32)
    zero_hgrn = jnp.zeros((N_HGRN, bp, HGRN_HEADS, HGRN_DF, HGRN_DI), jnp.float32)
    y_prompt, gla_prompt, hgrn_prompt = trunk(x_prompt, p_prompt, zero_gla, zero_hgrn, *weights)
    y_sample, gla_sample, hgrn_sample = trunk(x_sample, p_sample, state_gla, state_hgrn, *weights)
    return (y_prompt, y_sample, gla_prompt, gla_sample, hgrn_prompt, hgrn_sample)


_drawn_inputs = setup_inputs


def setup_inputs(seed=0):
    import zlib

    import numpy as np

    out = dict(_drawn_inputs(seed))
    spreads = {}
    factors = {'ffn1_norm': 3.729,
     'gla_gn': 15.034,
     'hgrn_gn': 57.296,
     'ffn2_norm': 6.566,
     'ple_norm': 64.0,
     'final_norm': 7.773}
    for name, (base, spread) in spreads.items():
        noise = np.random.default_rng([zlib.crc32(name.encode()), seed]).standard_normal(out[name].shape)
        drawn = base * np.exp(spread * noise) if base else spread * noise
        out[name] = __import__('jax').numpy.asarray(drawn.astype(out[name].dtype))
    for name, factor in factors.items():
        out[name] = (out[name] * factor).astype(out[name].dtype)
    return out
```

```python
from contextlib import ExitStack

import concourse.bass as bass
from concourse import mybir

ALU = mybir.AluOpType
ACT = mybir.ActivationFunctionType
F32 = mybir.dt.float32
F32R = mybir.dt.float32r
U32 = mybir.dt.uint32

P = 128
D = 1024
KT_D = D // P
T_PROMPT = 512
N_SEQ, T_SEQ = 8, 4
T_SAMPLE = N_SEQ * T_SEQ
T = T_PROMPT + T_SAMPLE
HALF = T // 2
F_FF = 2816
NF = F_FF // P
PLE = 256
EPS = 1e-6

RING = 4
UNIT = 1024
DOWN_KT = [(0, 8), (8, 16), (16, 22)]
UP_UNITS = 2 * NF
DOWN_UNITS = 3 * KT_D
FFN_UNITS = UP_UNITS + DOWN_UNITS

CHUNK = 128
NCH = T_PROMPT // CHUNK
LEVELS = 7
LASTTILE = T - P
SROW = P - T_SAMPLE
VCOLS = 512

GLA_UNITS = [13, 12]
HGRN_UNITS = [16, 16]
OUT_UNITS = 8
PLE_GATE_UNITS, PLE_PROJ_UNITS = 8, 2
START = {}
_n = 0
for _l in range(2):
    START["ffn", 2 * _l] = _n
    _n += FFN_UNITS
    for _g, _u in enumerate((GLA_UNITS, HGRN_UNITS)[_l]):
        START["mix", 2 * _l + _g] = _n
        _n += _u
    START["out", _l] = _n
    _n += OUT_UNITS
    START["ffn", 2 * _l + 1] = _n
    _n += FFN_UNITS
    START["ple", _l] = _n
    _n += PLE_GATE_UNITS + PLE_PROJ_UNITS
N_UNITS = _n


class Group:

    def __init__(self, gi):
        self.gi = gi
        self.gla = gi < 2
        self.layer = 0 if self.gla else 1
        self.g = gi % 2
        self.NH = 2 if self.gla else 4
        self.V = VCOLS // self.NH
        self.h0 = self.g * self.NH
        self.start = START["mix", gi]
        self.has_r = gi == 0
        self.nfeat = 2 * self.NH + self.has_r
        self.vt_per_head = self.V // P
        self.gate_scale = 1.0 / 16.0 if self.gla else 1.0
        self.q_scale = float(P) ** -0.5 if self.gla else 1.0
        self.feat0 = [0, 9, 17, 29][gi]
        self.v_unit = self.start + self.nfeat
        self.g_unit = self.v_unit + 4
        self.norm = 1 if self.gla else 5

    def feat_bank(self, j):
        if j >= self.nfeat:
            return [6, 0, 2, 6][j - self.nfeat]
        if j < 2:
            return 2 * j
        return 6 if (self.nfeat - 1 - j) % 2 == 0 else 4


GROUPS = [Group(gi) for gi in range(4)]
N_FEAT = 41


def build(nc, a, o):
    with ExitStack() as ctx:
        _build(nc, a, o, ctx)


def _build(nc, a, o, ctx):
    def sb(name, shape, dt=F32, where=ctx):
        return where.enter_context(nc.sbuf_tensor(name, shape, dt))

    ps = ctx.enter_context(nc.psum_tensor("ps", [P, 8, 512], F32))
    psf = ps[:].rearrange("p b n -> p (b n)")

    H = sb("h_resid", [P, KT_D, T])
    UH = sb("u_high", [P, KT_D, T], F32R)
    UL = sb("u_low", [P, KT_D, T], F32R)
    RAW = sb("w_raw", [P, RING, UNIT])
    WH = sb("w_high", [P, RING, UNIT], F32R)
    WL = sb("w_low", [P, RING, UNIT], F32R)
    ident = sb("ident", [P, P])
    ones = sb("ones", [P, P])
    masks = sb("masks", [P, LEVELS, 64])
    seqmask = sb("seqmask", [P, N_SEQ])
    gains = sb("gains", [P, 9, KT_D])
    gn = sb("gn", [P, 3])
    bgk = sb("bgk", [P, 4])
    lbr = sb("lbr", [P, 2, KT_D])
    lbd = sb("lbd", [P, 6, KT_D])
    consts = sb("consts", [P, 2])
    rstd = sb("rstd", [P, T])
    rstdT = sb("rstd_tok", [P, 5])
    ssq = sb("ssq", [P, T])
    tG = sb("t_gate", [P, T])
    tU = sb("t_up", [P, T])
    DEC = sb("decay_chunk", [P, 4, NCH])
    DECS = sb("decay_seq", [P, 4, N_SEQ])

    with ExitStack() as region:
        HH = sb("hid_high", [P, NF, T], F32R, region)
        HL = sb("hid_low", [P, NF, T], F32R, region)
    with ExitStack() as region:
        XIN = sb("x_tok", [P, 5, D], F32, region)
    with ExitStack() as region:
        YF = sb("y_feat", [P, KT_D, T], F32, region)
        YT = sb("y_tok", [P, 5, D], F32, region)
    with ExitStack() as region:
        PIN = sb("p_tok", [P, 5, PLE], F32, region)
        PH = sb("p_high", [P, 2, T], F32R, region)
        PL = sb("p_low", [P, 2, T], F32R, region)
        PT = sb("p_feat", [P, 2, T], F32, region)
        GT = sb("ple_gate", [P, KT_D, T], F32, region)
    with ExitStack() as region:
        OH = sb("o_high", [P, KT_D, T], F32R, region)
        OL = sb("o_low", [P, KT_D, T], F32R, region)
    with ExitStack() as region:
        Q = sb("q", [P, 4, T], F32, region)
        K = sb("k", [P, 4, T], F32, region)
        G = sb("gate_sum", [P, 4, T], F32, region)
        V = sb("v_tok", [P, 5, VCOLS], F32, region)
        AT = sb("attn", [P, 16, P], F32, region)
        ATS = sb("attn_s", [P, 4, T_SAMPLE], F32, region)
        OG = sb("out_gate", [P, KT_D, T], F32, region)
        KTb = sb("k_tilde", [P, 2, 4 * T], F32, region)
        QTb = sb("q_tilde", [P, 2, 2 * T], F32, region)
        EX = sb("ex", [P, 4 * T], F32, region)
    with ExitStack() as region:
        for nm, w in (("al_q", 4 * T), ("al_k", 4 * T), ("al_g", 4 * T), ("al_v", 5 * VCOLS), ("al_at", 16 * P),
                      ("al_ats", 4 * T_SAMPLE), ("al_og", KT_D * T)):
            sb(nm, [P, w], F32, region)
        KD = sb("kdec_tok", [P, 16, P], F32, region)
        ST = sb("states", [P, 4, VCOLS], F32, region)
        sb("al_pad", [P, 2 * 4 * T - 16 * P - 4 * VCOLS], F32, region)
        S0 = sb("states_s", [P, N_SEQ, VCOLS], F32, region)
    KDS = tG
    KMASK = G

    names = (
        "raw0 raw1 raw2 raw3 hi_made lo_made mm_units "
        "pc masks_made const_dma x_in w_gkup_in p_in s0_in out_y out_state st_stored "
        "dve_const pool_const ident_made x_turned h_done uh_done sq_done u_done ssq_added norm_mm ln_done rstd_done "
        "tg_done up_evicted silu_done hid_mul hid_hi hid_done "
        "feat_out v_out lb_a lb_b lb_c lb_done r_used gk_mm x_made gate_abs gate_exp gate_ln ls_made c_made kx_made "
        "gd_made gd_abs gd_exp gd_ln k_made gate_made q_made kt_zero diff_made ek_made eq_made kt_made qt_made "
        "lvl_mm lvl_out diag_mm diag_out sdiag_out slvl_out chunk_exp qin_made ksuf_made ksuf_exp kdec_made dec_made "
        "kd_turned kd_out u_mm s_made kmask_made kmask_used us_mm snew_made o_mm os_mm o_out osq_made "
        "var_mm var_ln ors_made o_norm og_silu og_made out_hi out_lo "
        "ple_t ple_sig p_turned p_feat p_hi p_lo ple_mm ple_x y_made y_turned y_out_a y_out_v"
    ).split()
    s = {n: ctx.enter_context(nc.semaphore(n)) for n in names}
    raw_sem = [s["raw0"], s["raw1"], s["raw2"], s["raw3"]]

    def pair(b):
        return ps[:, b:b + 2, 0:HALF]

    def halves(ap):
        return ap.rearrange("p (a b) -> p a b", a=2)

    def tile_of(t3, m):
        if isinstance(m, int):
            return halves(t3[:, m, :])
        return t3[:, bass.ds(m, 1), :].rearrange("p o (a b) -> p (o a) b", a=2)

    def flat_of(t3, m):
        if isinstance(m, int):
            return t3[:, m, :]
        return t3[:, bass.ds(m, 1), :].rearrange("p o t -> p (o t)")

    w_gu = [a["ffn1_w_gu"], a["ffn2_w_gu"]]
    w_dn = [a["ffn1_w_down"], a["ffn2_w_down"]]

    RT = OG[:, KT_D - 1, :]
    LLB, L1M = lbd[:, 3, :], lbd[:, 1, :]
    WUP = KTb[:, 1, 0:512]

    def KM(b):
        return G[:].rearrange("p h t -> p (h t)")[:, (b % 4) * 512:(b % 4 + 1) * 512]

    def blocks(ap, gr, L, all_tokens):
        if all_tokens:
            v = ap[:, 0:gr.NH, :].rearrange("p h (n l) -> p (h n) l", l=2 * L)
            return v[:, :, 0:L], v[:, :, L:2 * L], v[:, :, L - 1:L]
        v = ap[:, 0:gr.NH, 0:T_PROMPT].rearrange("p h (n l) -> p h n l", l=2 * L)
        return v[:, :, :, 0:L], v[:, :, :, L:2 * L], v[:, :, :, L - 1:L]

    def compact(ap2, gr, L, all_tokens):
        v = ap2[:, 0:gr.NH * HALF].rearrange("p (h t) -> p h t", t=HALF)
        if all_tokens:
            return v.rearrange("p h (n l) -> p (h n) l", l=L)
        return v[:, :, 0:T_PROMPT // 2].rearrange("p h (n l) -> p h n l", l=L)

    block = ctx.enter_context(nc.Block())

    @block.sync
    def _(sp):
        def load_unit(base, i, j, src, nkt, width, free=True):
            n = base + j
            slot = n % RING
            if free and (not isinstance(i, int) or n + i >= RING):
                sp.wait_ge(s["lo_made"], i + (n - RING + 1))
            sp.dma_start(RAW[:, slot, 0:nkt * width].rearrange("p (k n) -> p k n", k=nkt), src)\
              .then_inc(raw_sem[slot], 16)

        def cols(w, k0, k1, c0, n):
            v = w.rearrange("(k p) n -> p k n", p=P)
            return v[:, k0:k1, bass.ds(c0, n)]

        def ffn(F):
            l, base = F // 2, START["ffn", F]
            gu, dn = w_gu[F % 2][l], w_dn[F % 2][l]

            def up_body(i, off):
                for j in range(4):
                    f2, up = j // 2, j % 2
                    load_unit(base, off, j, cols(gu, 0, KT_D, i * (2 * P) + (f2 * P + up * F_FF), P), KT_D, P)

            if F == 0:
                for j in range(RING):
                    if j == 2:
                        early_loads()
                    load_unit(0, 0, j, cols(gu, 0, KT_D, (j // 2) * P + (j % 2) * F_FF, P), KT_D, P)
            else:
                up_body(0, 0)
            with sp.Fori(1, NF // 2) as i:
                up_body(i, i * 4)
            with sp.Fori(0, 2) as i:
                for m4 in range(4):
                    for u, (k0, k1) in enumerate(DOWN_KT):
                        load_unit(base + UP_UNITS, i * 12, m4 * 3 + u, cols(dn, k0, k1, i * (4 * P) + m4 * P, P), k1 - k0, P)

        def early_loads():
            sp.dma_start(XIN[:, 0:4, :], a["x_prompt"][0].rearrange("(c p) d -> p c d", p=P)).then_inc(s["x_in"], 16)
            sp.dma_start(XIN[0:T_SAMPLE, 4, :], a["x_sample"].rearrange("b t d -> (b t) d")).then_inc(s["x_in"], 16)

        def mix_loads(gr):
            w = a["gla_w_in"][0] if gr.gla else a["hgrn_w_in"][0]
            n = gr.start
            q0 = gr.h0 * P
            k0 = (512 if gr.gla else 1024) + gr.h0 * P
            v0 = (1024 if gr.gla else 2048) + gr.g * VCOLS
            g0 = (2048 if gr.gla else 3072) + gr.g * VCOLS
            starts = ([3088 - P] if gr.has_r else []) + [q0 + P * h for h in range(gr.NH)] + [k0 + P * h for h in range(gr.NH)]
            for c in starts:
                load_unit(n, 0, 0, cols(w, 0, KT_D, c, P), KT_D, P)
                n += 1
            for u in range(4):
                load_unit(n, 0, 0, cols(w, 2 * u, 2 * u + 2, v0, VCOLS), 2, VCOLS)
                n += 1
            for t in range(4):
                load_unit(n, 0, 0, cols(w, 0, KT_D, g0 + P * t, P), KT_D, P)
                n += 1

        def small_loads():
            for e, (nm, l) in enumerate([("ffn1_norm", 0), ("mix_norm", 0), ("ffn2_norm", 0), ("ple_norm", 0),
                                         ("ffn1_norm", 1), ("mix_norm", 1), ("ffn2_norm", 1), ("ple_norm", 1)]):
                sp.dma_start(gains[:, e, :], a[nm][l].rearrange("(m p) -> p m", p=P)).then_inc(s["const_dma"], 16)
            sp.dma_start(gains[:, 8, :], a["final_norm"].rearrange("(m p) -> p m", p=P)).then_inc(s["const_dma"], 16)
            sp.dma_start(gn[:, 0:2], a["gla_gn"][0].rearrange("(m p) -> p m", p=P)).then_inc(s["const_dma"], 16)
            sp.dma_start(gn[:, 2:3], a["hgrn_gn"][0].rearrange("(m p) -> p m", p=P)).then_inc(s["const_dma"], 16)
            sp.dma_start(bgk[:, :], a["gla_b_gk"][0].rearrange("(m p) -> p m", p=P)).then_inc(s["const_dma"], 16)
            for l in range(2):
                sp.dma_start(lbr[:, l, :], a["hgrn_lower_bounds"][l].rearrange("(m p) -> p m", p=P)).then_inc(s["const_dma"], 16)

        with nc.allow_non_contiguous_dma(reason="gains and biases, one value to a partition"):
            small_loads()
        for l in range(2):
            ffn(2 * l)
            for g in range(2):
                gr = GROUPS[2 * l + g]
                mix_loads(gr)
                if g == 1:
                    w = (a["gla_w_out"] if l == 0 else a["hgrn_w_out"])[0]
                    for m in range(4):
                        load_unit(START["out", l] + m, 0, 0, cols(w, 0, KT_D, m * P, P), KT_D, P)
            for m in range(4, 8):
                load_unit(START["out", l] + m, 0, 0, cols(w, 0, KT_D, m * P, P), KT_D, P)
            ffn(2 * l + 1)
            for m in range(4):
                load_unit(START["ple", l] + m, 0, 0, cols(a["ple_w_gate"][l], 0, KT_D, m * P, P), KT_D, P)
            sp.wait_ge(s["h_done"], 8 * (4 * l + 3) + 8)
            sp.dma_start(PIN[:, 0:4, :], a["p_prompt"][l, 0].rearrange("(c p) d -> p c d", p=P)).then_inc(s["p_in"], 16)
            sp.dma_start(PIN[0:T_SAMPLE, 4, :], a["p_sample"][l].rearrange("b t d -> (b t) d")).then_inc(s["p_in"], 16)
            for m in range(4, 8):
                load_unit(START["ple", l] + m, 0, 0, cols(a["ple_w_gate"][l], 0, KT_D, m * P, P), KT_D, P)
            for u in range(2):
                load_unit(START["ple", l] + 8 + u, 0, 0, cols(a["ple_w_proj"][l], 0, 2, u * 512, 512), 2, 512)
        for c in range(5):
            sp.wait_ge(s["y_out_a" if c % 2 else "y_out_v"], c // 2 + 1)
            if c < 4:
                sp.dma_start(o["y_p"][0, c * P:(c + 1) * P, :], YT[:, c, :]).then_inc(s["out_y"], 16)
            else:
                sp.dma_start(o["y_s"].rearrange("b t d -> (b t) d"), YT[0:T_SAMPLE, 4, :]).then_inc(s["out_y"], 16)
        sp.wait_ge(s["out_y"], 16 * 5)
        sp.wait_ge(s["out_state"], 16 * 9 * 4)

    @block.tensor
    def _(pe):
        def weights(slot, k, kind, m0=0, mw=P, kw=P):
            w = WH if kind == "h" else WL
            return w[:, slot, k * kw + m0:k * kw + m0 + mw]

        def unit_ready(n):
            pe.wait_ge(s["lo_made"], n + 1)

        def products(slot, nk, k0, kt_total, bank, xh, xl, m0=0, kw=P, before=None):
            for k in range(nk):
                kk = k0 + k
                if before is not None:
                    before(kk)
                for part, (wk, x) in enumerate((("h", xh), ("h", xl), ("l", xh))):
                    for hf in range(2):
                        mm = pe.matmul(ps[:, bank + hf, 0:HALF], weights(slot, k, wk, m0, P, kw),
                                       x[:, kk, hf * HALF:(hf + 1) * HALF],
                                       start=(kk == 0 and part == 0), stop=(kk == kt_total - 1 and part == 2))
            return mm

        def wait_u(e):
            def before(kk):
                pe.wait_ge(s["u_done"], 8 * e + kk + 1)
            return before

        def norm(e, by_token=False):
            pe.wait_ge(s["ssq_added"], 8 * e + 8)
            pe.wait_ge(s["h_done"], 8 * e + 7)
            for hf in range(2):
                mm = pe.matmul(ps[:, 4 + hf, 0:HALF], ones[:, :], ssq[:, hf * HALF:(hf + 1) * HALF], start=True, stop=True)
            if by_token:
                for c in range(5):
                    t0 = c * P if c < 4 else LASTTILE
                    mm = pe.matmul(ps[:, 4, 300 + c:301 + c], ssq[:, t0:t0 + P], ones[:, 0:1], start=True, stop=True)
            mm.then_inc(s["norm_mm"], 1)

        def ffn(F):
            base, e = START["ffn", F], 2 * F

            def chunk(f, n, slot, first):
                bank = 4 * (slot // 2)
                if first and bank == 0:
                    pe.wait_ge(s["h_done"], 8 * e + 6)
                elif first:
                    pe.wait_ge(s["h_done"], 8 * e + 8)
                    pe.wait_ge(s["rstd_done"], e + 1)
                else:
                    pe.wait_ge(s["up_evicted"], f + (NF * F - 1))
                for up in range(2):
                    unit_ready(n + up)
                    products((base + slot + up) % RING, KT_D, 0, KT_D, bank + 2 * up, UH, UL,
                             before=wait_u(e) if first and bank == 0 else None).then_inc(s["mm_units"], 1)
                    if first and bank == 0 and up == 0:
                        norm(e)

            for c in range(2):
                chunk(c, base + 2 * c, 2 * c, True)
            with pe.Fori(1, NF // 2) as i:
                for c in range(2):
                    chunk(i * 2 + c, i * 4 + (base + 2 * c), 2 * c, False)
            base += UP_UNITS
            def down_tile(i, m4, first):
                if first:
                    pe.wait_ge(s["up_evicted"], NF * F + (NF - 1 if m4 < 2 else NF))
                else:
                    pe.wait_ge(s["h_done"], 8 * (e + 1) + m4 + 1)
                for u, (k0, k1) in enumerate(DOWN_KT):
                    n = m4 * 3 + u
                    unit_ready(i * 12 + (base + n))

                    def before(kk):
                        if first and m4 == 0:
                            pe.wait_ge(s["hid_done"], NF * F + kk + 1)
                    products((base + n) % RING, k1 - k0, k0, NF, 2 * m4, HH, HL, before=before).then_inc(s["mm_units"], 1)

            for m4 in range(4):
                down_tile(0, m4, True)
            for m4 in range(4):
                down_tile(1, m4, False)

        def features(gr):
            e = gr.norm
            j = 0
            n = gr.start
            def feature_tile(j, n):
                b = gr.feat_bank(j)
                if j < 2 and gr.g == 0:
                    pe.wait_ge(s["h_done"], 8 * e + 6)
                elif gr.g == 0 and j == 2:
                    pe.wait_ge(s["h_done"], 8 * e + 8)
                    pe.wait_ge(s["rstd_done"], e + 1)
                    pe.wait_ge(s["feat_out"], gr.feat0 + j - 1)
                elif j == gr.nfeat:
                    pe.wait_ge(s["feat_out"], gr.feat0 + j)
                elif j == gr.nfeat + 1:
                    pe.wait_ge(s["v_out"], 5 * gr.gi + 5)
                elif j == gr.nfeat + 3:
                    pe.wait_ge(s["feat_out"], gr.feat0 + j - 2)
                elif 2 <= j < gr.nfeat:
                    pe.wait_ge(s["feat_out"], gr.feat0 + j - 1)
                elif gr.g == 1 and j == 0:
                    pe.wait_ge(s["ors_made"], gr.gi)
                unit_ready(n)
                products(n % RING, KT_D, 0, KT_D, b, UH, UL,
                         before=wait_u(e) if j == 0 and gr.g == 0 else None).then_inc(s["mm_units"], 1)
                if j == 0 and gr.g == 0:
                    norm(e, True)
            for j in range(gr.nfeat):
                feature_tile(j, n)
                n += 1
            pe.wait_ge(s["feat_out"], gr.feat0 + gr.nfeat - 1)
            for u in range(4):
                unit_ready(n)
                for c in range(5):
                    t0 = c * P if c < 4 else LASTTILE
                    for k in range(2):
                        kk = 2 * u + k
                        for part, (x, w) in enumerate(((UH, WH), (UL, WH), (UH, WL))):
                            mm = pe.matmul(ps[:, c, :], x[:, kk, t0:t0 + P], w[:, n % RING, k * 512:(k + 1) * 512],
                                           start=(kk == 0 and part == 0), stop=(kk == KT_D - 1 and part == 2))
                mm.then_inc(s["mm_units"], 1)
                n += 1
            for j in range(gr.nfeat, gr.nfeat + 4):
                feature_tile(j, n)
                n += 1

        def gk(gr):
            pe.wait_ge(s["w_gkup_in"], 16)
            pe.wait_ge(s["feat_out"], gr.feat0 + gr.nfeat + 4)
            for h in range(4):
                for hf in range(2):
                    mm = pe.matmul(ps[:, 2 * h + hf, 0:HALF], WUP[:, h * P:(h + 1) * P],
                                   RT[:, hf * HALF:(hf + 1) * HALF], start=True, stop=True)
            mm.then_inc(s["gk_mm"], 1)

        def mix(gr):
            gi, NH = gr.gi, gr.NH
            if gr.has_r:
                pe.wait_ge(s["x_made"], 1)
            if not gr.gla:
                pe.wait_ge(s["q_made"], gi - 1)
                pe.wait_ge(s["k_made"], gi - 1)
            pe.wait_ge(s["feat_out"], gr.feat0 + gr.nfeat + 4)
            for h in range(NH):
                for c in range(NCH):
                    x = h * NCH + c
                    mm = pe.matmul(ps[:, 4 + x // 4, (x % 4) * P:(x % 4 + 1) * P], K[:, h, c * P:(c + 1) * P],
                                   Q[:, h, c * P:(c + 1) * P], start=True, stop=True)
            mm.then_inc(s["diag_mm"], 1)
            for l in range(LEVELS):
                n = LEVELS * gi + l
                pe.wait_ge(s["kt_made"], n + 1)
                pe.wait_ge(s["qt_made"], n + 1)
                if l >= 2:
                    pe.wait_ge(s["lvl_out"], n - 1)
                for h in range(NH):
                    for c in range(NCH):
                        x = h * NCH + c
                        mm = pe.matmul(ps[:, 2 * (l % 2) + x // 8, (x % 8) * 64:(x % 8 + 1) * 64],
                                       KTb[:, l % 2, h * T + c * P:h * T + (c + 1) * P],
                                       QTb[:, l % 2, h * HALF + c * 64:h * HALF + (c + 1) * 64], start=True, stop=True)
                if l < 2:
                    pe.wait_ge(s["diag_out"], gi + 1)
                    for h in range(NH):
                        mm = pe.matmul(ps[:, 4 + l, h * 16:(h + 1) * 16], KTb[:, l % 2, h * T + LASTTILE:(h + 1) * T],
                                       QTb[:, l % 2, h * HALF + 256:(h + 1) * HALF], start=True, stop=True)
                mm.then_inc(s["lvl_mm"], 1)
                if l == 0:
                    for h in range(NH):
                        mm = pe.matmul(ps[:, 6, h * 32:(h + 1) * 32], K[:, h, LASTTILE:T], Q[:, h, T_PROMPT:T],
                                       start=True, stop=True)
                    mm.then_inc(s["diag_mm"], 1)
            pe.wait_ge(s["kdec_made"], gi + 1)
            pe.wait_ge(s["lvl_out"], LEVELS * (gi + 1))
            pe.wait_ge(s["slvl_out"], 2 * (gi + 1))
            for h in range(NH):
                for c in range(NCH):
                    x = h * NCH + c
                    pe.transpose(ps[:, x // 4, (x % 4) * P:(x % 4 + 1) * P], K[:, h, c * P:(c + 1) * P], ident[:, :])
            for h in range(NH):
                mm = pe.transpose(ps[:, 4, h * P:(h + 1) * P], K[:, h, LASTTILE:T], ident[:, :])
            mm.then_inc(s["kd_turned"], 1)
            for c in range(NCH):
                pe.wait_ge(s["kd_out"], 2 * gi + 2)
                for h in range(NH):
                    mm = pe.matmul(ps[:, c, h * gr.V:(h + 1) * gr.V], KD[:, h * NCH + c, :],
                                   V[:, c, h * gr.V:(h + 1) * gr.V], start=True, stop=True)
                mm.then_inc(s["u_mm"], 1)
            for j in range(4):
                h = j // gr.vt_per_head
                for c in range(NCH):
                    pe.matmul(ps[:, 4 + j, c * P:(c + 1) * P], V[:, c, j * P:(j + 1) * P], AT[:, h * NCH + c, :],
                              start=(c == 0), stop=False, skip_group_check=True)
            pe.wait_ge(s["qin_made"], gi + 1)
            for c in range(1, NCH):
                pe.wait_ge(s["s_made"], 4 * gi + c)
                for j in range(4):
                    h = j // gr.vt_per_head
                    mm = pe.matmul(ps[:, 4 + j, c * P:(c + 1) * P], ST[:, c - 1, j * P:(j + 1) * P],
                                   Q[:, h, c * P:(c + 1) * P], start=False, stop=(c == NCH - 1), skip_group_check=True)
            mm.then_inc(s["o_mm"], 1)
            pe.wait_ge(s["s_made"], 4 * gi + 4)
            pe.wait_ge(s["s0_in"], 16 * N_SEQ * (gi + 1))
            for j in range(4):
                h = j // gr.vt_per_head
                pe.matmul(ps[:, 0, j * 32:(j + 1) * 32], V[:, 4, j * P:(j + 1) * P], ATS[:, h, :],
                          start=(j == 0), stop=False, skip_group_check=True)
            for j in range(4):
                h = j // gr.vt_per_head
                for b in range(N_SEQ):
                    mm = pe.matmul(ps[:, 0, j * 32 + 4 * b:j * 32 + 4 * b + 4], S0[:, b, j * P:(j + 1) * P],
                                   Q[:, h, T_PROMPT + 4 * b:T_PROMPT + 4 * b + 4],
                                   start=False, stop=(j == 3 and b == N_SEQ - 1), skip_group_check=True)
            mm.then_inc(s["os_mm"], 1)
            for b in range(N_SEQ):
                pe.wait_ge(s["kmask_made"], N_SEQ * gi + b + 1)
                if b >= 3:
                    pe.wait_ge(s["snew_made"], N_SEQ * gi + b - 2)
                for h in range(NH):
                    mm = pe.matmul(ps[:, 1 + b % 3, h * gr.V:(h + 1) * gr.V], KM(b)[:, h * P:(h + 1) * P],
                                   V[:, 4, h * gr.V:(h + 1) * gr.V], start=True, stop=True)
                mm.then_inc(s["us_mm"], 1)
            pe.wait_ge(s["osq_made"], gi + 1)
            pe.wait_ge(s["snew_made"], N_SEQ * (gi + 1))
            for h in range(NH):
                for hf in range(2):
                    for t in range(gr.vt_per_head):
                        mm = pe.matmul(ps[:, 2 * h + hf, 0:HALF], ones[:, :],
                                       K[:, h * gr.vt_per_head + t, hf * HALF:(hf + 1) * HALF],
                                       start=(t == 0), stop=(t == gr.vt_per_head - 1))
            mm.then_inc(s["var_mm"], 1)

        def out_proj(l):
            n = START["out", l]
            e = 4 * l + 2
            for m in range(KT_D):
                if m == 0:
                    pe.wait_ge(s["ors_made"], 2 * l + 2)
                if m >= 4:
                    pe.wait_ge(s["h_done"], 8 * e + m - 3)
                unit_ready(n)

                def before(kk):
                    if m == 0:
                        pe.wait_ge(s["out_lo"], 8 * l + kk + 1)
                products(n % RING, KT_D, 0, KT_D, 2 * (m % 4), OH, OL, before=before).then_inc(s["mm_units"], 1)
                n += 1

        def ple(l):
            n = START["ple", l]
            e = 4 * l + 3
            for m in range(KT_D):
                if m == 0:
                    pe.wait_ge(s["h_done"], 8 * e + 6)
                elif m == 2:
                    pe.wait_ge(s["h_done"], 8 * e + 8)
                    pe.wait_ge(s["rstd_done"], e + 1)
                elif m >= 4:
                    pe.wait_ge(s["ple_t"], 8 * l + m - 3)
                unit_ready(n)
                products(n % RING, KT_D, 0, KT_D, 2 * (m % 4), UH, UL, before=wait_u(e) if m == 0 else None)\
                    .then_inc(s["mm_units"], 1)
                if m == 0:
                    norm(e)
                n += 1
            pe.wait_ge(s["p_in"], 32 * (l + 1))
            for kt in range(2):
                pe.wait_ge(s["ple_t"], 8 * l + 5 + kt)
                mm = turn(PIN, kt, 2 * kt)
                mm.then_inc(s["p_turned"], 1)
            for m in range(KT_D):
                if m == 0:
                    pe.wait_ge(s["p_feat"], 2 * l + 2)
                    pe.wait_ge(s["p_lo"], 2 * l + 2)
                if m in (2, 3):
                    pe.wait_ge(s["ple_t"], 8 * l + m + 5)
                if m >= 4:
                    pe.wait_ge(s["h_done"], 8 * (e + 1) + m - 3)
                if m % 4 == 0:
                    unit_ready(n)
                mm = products(n % RING, 2, 0, 2, 2 * (m % 4), PH, PL, m0=(m % 4) * P, kw=512)
                if m % 4 == 3:
                    mm.then_inc(s["mm_units"], 1)
                    n += 1
                else:
                    mm.then_inc(s["ple_mm"], 1)

        def turn(src, m, bank):
            for c in range(5):
                rows = P if c < 4 else T_SAMPLE
                mm = pe.transpose(psf[:, bank * 512 + c * P:bank * 512 + c * P + rows],
                                  src[0:rows, c, m * P:(m + 1) * P], ident[0:rows, 0:rows])
            return mm

        pe.wait_ge(s["ident_made"], 1)
        pe.wait_ge(s["dve_const"], 1)
        pe.wait_ge(s["x_in"], 32)
        for m in range(KT_D):
            if m >= 4:
                pe.wait_ge(s["h_done"], m - 3)
            turn(XIN, m, 2 * (m % 4)).then_inc(s["x_turned"], 1)
        for l in range(2):
            ffn(2 * l)
            for g in range(2):
                gr = GROUPS[2 * l + g]
                features(gr)
                if gr.has_r:
                    gk(gr)
                mix(gr)
            out_proj(l)
            ffn(2 * l + 1)
            ple(l)
        norm(8)
        for c in range(5):
            cols = P if c < 4 else T_SAMPLE
            if c == 2:
                pe.wait_ge(s["rstd_done"], 9)
            if c == 4:
                pe.wait_ge(s["y_out_v"], 1)
            for m in range(KT_D):
                if c == 0:
                    pe.wait_ge(s["y_made"], m + 1)
                mm = pe.transpose(psf[0:cols, (2 * (c % 4)) * 512 + m * P:(2 * (c % 4)) * 512 + (m + 1) * P],
                                  YF[:, m, c * P:c * P + cols], ident[:, :])
            mm.then_inc(s["y_turned"], 1)

    @block.scalar
    def _(act):
        def high(base, i, j=0):
            n = base + j
            slot = n % RING
            act.wait_ge(raw_sem[slot], q16(i, n))
            if not isinstance(i, int) or n >= RING:
                act.wait_ge(s["mm_units"], i + (n - RING + 1))
            act.activation(WH[:, slot, :], RAW[:, slot, :], ACT.Copy).then_inc(s["hi_made"], 1)

        def q16(i, n):
            return (i // 4) * 16 + 16 * (n // RING + 1) if isinstance(i, int) else i * 4 + 16 * (n // RING + 1)

        def tile_out(e, m, mc):
            act.wait_ge(s["h_done"], m + (8 * e + 1))
            if not isinstance(m, int) or 8 * e + m >= 2:
                act.wait_ge(s["ssq_added"], m + (8 * e - 1))
            if not isinstance(m, int):
                act.wait_ge(s["pool_const"], 1)
            if e < 8:
                act.activation(flat_of(UH, m), flat_of(H, m), ACT.Copy,
                               scale=gain_of(e, m)).then_inc(s["uh_done"], 1)
            act.activation((tG, tU)[mc % 2][:, :], flat_of(H, m), ACT.Square).then_inc(s["sq_done"], 1)

        def gain_of(e, m):
            return gains[:, e, m:m + 1] if isinstance(m, int) else \
                gains[:, e, bass.ds(m, 1)]

        def norm(e, by_token=False):
            act.wait_ge(s["norm_mm"], e + 1)
            if by_token:
                act.activation(rstdT[:, :], ps[:, 4, 300:305], ACT.Ln, bias=consts[:, 0:1], scale=1.0 / D).then_inc(s["ln_done"], 1)
            act.activation(halves(rstd[:, :]), pair(4), ACT.Ln, bias=consts[:, 0:1], scale=1.0 / D).then_inc(s["ln_done"], 1)
            done = e + 1 + (e > 0) + (e > 4) + (e == 1) * 0
            act.wait_ge(s["ln_done"], done)
            if by_token:
                act.activation(rstdT[:, :], rstdT[:, :], ACT.Exp, scale=-0.5)
            act.activation(rstd[:, :], rstd[:, :], ACT.Exp, scale=-0.5).then_inc(s["rstd_done"], 1)

        def ffn(F):
            base, e = START["ffn", F], 2 * F

            def chunk(i4, f, j, first=False):
                high(base, i4, j + 2)
                high(base, i4, j + 3)
                if first:
                    norm(e)
                act.wait_ge(s["tg_done"], f + (NF * F + 1))
                act.activation(tG[:, :], tG[:, :], ACT.Silu).then_inc(s["silu_done"], 1)
                act.wait_ge(s["hid_mul"], f + (NF * F + 1))
                act.wait_ge(s["pool_const"], 1)
                act.activation(flat_of(HH, f), tU[:, :], ACT.Copy).then_inc(s["hid_hi"], 1)

            chunk(0, 0, 0, True)
            chunk(0, 1, 2)
            with act.Fori(1, NF // 2) as i:
                for c in range(2):
                    chunk(i * 4, i * 2 + c, 2 * c)
            base += UP_UNITS
            with act.Fori(0, 2) as i:
                for m4 in range(4):
                    for u in range(3):
                        high(base, i * 12, 3 * m4 + u + 2)
                    tile_out(e + 1, i * 4 + m4, m4)

        def ahead(n):
            if n + 2 < N_UNITS:
                high(n + 2, 0)

        def features(gr):
            n = gr.start
            for j in range(gr.nfeat):
                ahead(n)
                if j == 0 and gr.g == 0:
                    norm(gr.norm, True)
                n += 1
            gate(gr)
            for u in range(4):
                ahead(n)
                n += 1
            act.wait_ge(s["mm_units"], n)
            act.wait_ge(s["rstd_done"], gr.norm + 1)
            for c in range(5):
                act.activation(V[:, c, :], ps[:, c, :], ACT.Copy, scale=rstdT[:, c:c + 1]).then_inc(s["v_out"], 1)
            for j in range(4):
                ahead(n)
                n += 1

        def gate(gr):
            if gr.gla:
                return
            k = gr.gi - 1
            ex = EX[:, :]
            kk = K[:].rearrange("p h t -> p (h t)")
            act.wait_ge(s["feat_out"], gr.feat0 + gr.nfeat)
            act.activation(Q[:], Q[:], ACT.Silu).then_inc(s["q_made"], 1)
            log_sigmoid_tail(gr, kk)
            act.wait_ge(s["kx_made"], k)
            act.activation(kk, kk, ACT.Exp).then_inc(s["k_made"], 1)
            act.wait_ge(s["gd_made"], k)
            act.activation(ex, ex, ACT.Abs).then_inc(s["gd_abs"], 1)
            act.wait_ge(s["gd_abs"], k)
            act.activation(ex, ex, ACT.Exp, scale=-1.0).then_inc(s["gd_exp"], 1)
            act.wait_ge(s["gd_exp"], k)
            act.activation(ex, ex, ACT.Ln, bias=consts[:, 1:2]).then_inc(s["gd_ln"], 1)

        def log_sigmoid_tail(gr, x):
            k = gr.gi + 1
            ex = EX[:, 0:gr.NH * T]
            if gr.gi:
                act.wait_ge(s["out_state"], 16 * 9 * gr.gi)
            act.activation(ex, x, ACT.Abs).then_inc(s["gate_abs"], 1)
            act.wait_ge(s["gate_abs"], k)
            act.activation(ex, ex, ACT.Exp, scale=-1.0).then_inc(s["gate_exp"], 1)
            act.wait_ge(s["gate_exp"], k)
            act.activation(ex, ex, ACT.Ln, bias=consts[:, 1:2]).then_inc(s["gate_ln"], 1)

        def mix(gr):
            gi, NH = gr.gi, gr.NH
            gs = gr.gate_scale
            if gr.gla:
                act.wait_ge(s["x_made"], gi + 1)
                log_sigmoid_tail(gr, G[:, 0:2, :].rearrange("p h t -> p (h t)"))
            for l in range(LEVELS):
                n, L = LEVELS * gi + l, 1 << l
                both = l < 2
                _, g2, _ = blocks(G, gr, L, both)
                act.wait_ge(s["diff_made"], n + 1)
                dk = compact(EX[:, 0:2 * T], gr, L, both)
                act.activation(dk, dk, ACT.Exp, scale=gs).then_inc(s["ek_made"], 1)
                if l:
                    act.wait_ge(s["qt_made"], n)
                act.activation(compact(EX[:, 2 * T:4 * T], gr, L, both), g2, ACT.Exp, scale=gs).then_inc(s["eq_made"], 1)
            act.wait_ge(s["kt_made"], LEVELS * (gi + 1))
            act.wait_ge(s["qt_made"], LEVELS * (gi + 1))
            act.wait_ge(s["gate_made"], (LEVELS + 1) * (gi + 1))
            gf = G[:, 0:NH, :].rearrange("p h t -> p (h t)")
            act.activation(EX[:, 0:NH * T], gf, ACT.Exp, scale=gs).then_inc(s["chunk_exp"], 1)
            ends = G[:, 0:NH, 0:T_PROMPT].rearrange("p h (c t) -> p h c t", t=CHUNK)[:, :, :, CHUNK - 1]
            act.activation(DEC[:, 0:NH, :], ends, ACT.Exp, scale=gs).then_inc(s["dec_made"], 1)
            ends = G[:, 0:NH, T_PROMPT:T].rearrange("p h (c t) -> p h c t", t=T_SEQ)[:, :, :, T_SEQ - 1]
            act.activation(DECS[:, 0:NH, :], ends, ACT.Exp, scale=gs).then_inc(s["dec_made"], 1)
            act.wait_ge(s["ksuf_made"], 2 * gi + 2)
            act.activation(EX[:, 0:NH * T], EX[:, 0:NH * T], ACT.Exp, scale=gs).then_inc(s["ksuf_exp"], 1)
            act.wait_ge(s["feat_out"], gr.feat0 + gr.nfeat + 4)
            act.activation(OG[:, 4 * gr.g:4 * gr.g + 4, :], OG[:, 4 * gr.g:4 * gr.g + 4, :], ACT.Silu).then_inc(s["og_silu"], 1)
            act.wait_ge(s["kd_turned"], gi + 1)
            act.activation(KD[:, 0:NH * NCH, :].rearrange("p x k -> p (x k)"), psf[:, 0:NH * NCH * P], ACT.Copy).then_inc(s["kd_out"], 1)
            act.wait_ge(s["o_out"], 2 * gi + 2)
            act.activation(K[:], Q[:], ACT.Square).then_inc(s["osq_made"], 1)
            act.wait_ge(s["var_mm"], gi + 1)
            src = psf[:, 0:NH * 1024].rearrange("p (x n) -> p x n", n=512)[:, :, 0:HALF]
            dst = G[:, 0:NH, :].rearrange("p h (a b) -> p (h a) b", b=HALF)
            act.activation(dst, src, ACT.Ln, bias=consts[:, 0:1], scale=1.0 / gr.V).then_inc(s["var_ln"], 1)
            act.wait_ge(s["var_ln"], gi + 1)
            act.activation(dst, dst, ACT.Exp, scale=-0.5).then_inc(s["ors_made"], 1)

        def out_proj(l):
            e = 4 * l + 2
            for kk in range(KT_D):
                act.wait_ge(s["og_made"], 8 * l + 8)
                act.activation(OH[:, kk, :], OG[:, kk, :], ACT.Copy).then_inc(s["out_hi"], 1)
            for m in range(KT_D):
                ahead(START["out", l] + m)
                tile_out(e, m, m)

        def ple(l):
            e = 4 * l + 3
            for m in range(KT_D):
                ahead(START["ple", l] + m)
                if m == 0:
                    norm(e)
                act.wait_ge(s["ple_t"], 8 * l + m + 1)
                act.activation(GT[:, m, :], GT[:, m, :], ACT.Sigmoid).then_inc(s["ple_sig"], 1)
            for kt in range(2):
                act.wait_ge(s["p_feat"], 2 * l + kt + 1)
                act.activation(PH[:, kt, :], PT[:, kt, :], ACT.Copy).then_inc(s["p_hi"], 1)
            for m in range(KT_D):
                if m % 4 == 3:
                    ahead(START["ple", l] + 8 + m // 4)
                tile_out(e + 1, m, m)

        act.wait_ge(s["pool_const"], 1)
        high(0, 0)
        high(1, 0)
        act.wait_ge(s["lb_a"], 1)
        act.activation(lbd[:, 1, :], lbd[:, 0, :], ACT.Abs).then_inc(s["lb_b"], 1)
        act.wait_ge(s["lb_b"], 1)
        act.activation(lbd[:, 2, :], lbd[:, 1, :], ACT.Exp, scale=-1.0).then_inc(s["lb_b"], 1)
        act.wait_ge(s["lb_b"], 2)
        act.activation(lbd[:, 5, :], lbd[:, 2, :], ACT.Ln, bias=consts[:, 1:2]).then_inc(s["lb_c"], 1)
        for m in range(KT_D):
            tile_out(0, m, m)
        for l in range(2):
            ffn(2 * l)
            for g in range(2):
                features(GROUPS[2 * l + g])
                mix(GROUPS[2 * l + g])
            out_proj(l)
            ffn(2 * l + 1)
            ple(l)
        norm(8)
        for c in range(1, 5, 2):
            rows = P if c < 4 else T_SAMPLE
            act.wait_ge(s["y_turned"], c + 1)
            act.activation(YT[0:rows, c, :], psf[0:rows, 2 * (c % 4) * 512:2 * (c % 4) * 512 + D], ACT.Copy).then_inc(s["y_out_a"], 1)


    @block.vector
    def _(dve):
        def low(base, i, j=0):
            n = base + j
            slot = n % RING
            dve.wait_ge(s["hi_made"], i + (n + 1))
            dve.tensor_tensor(WL[:, slot, :], RAW[:, slot, :], WH[:, slot, :].bitcast(F32), ALU.subtract)\
               .then_inc(s["lo_made"], 1)

        def ahead(n):
            if n + 2 < N_UNITS:
                low(n + 2, 0)

        def tile_low(e, m):
            if e == 8:
                return
            dve.wait_ge(s["uh_done"], m + (8 * e + 1))
            sc = gains[:, e, m:m + 1] if isinstance(m, int) else gains[:, e, bass.ds(m, 1)]
            dve.scalar_tensor_tensor(out=flat_of(UL, m), in0=flat_of(H, m), scalar=sc,
                                     in1=flat_of(UH, m).bitcast(F32), op0=ALU.mult, op1=ALU.subtract)\
               .then_inc(s["u_done"], 1)

        def ffn(F):
            base, e = START["ffn", F], 2 * F

            def chunk(i4, f, j):
                bank = 2 * j
                if not isinstance(f, int) or NF * F + f > 0:
                    dve.wait_ge(s["hid_done"], f + NF * F)
                low(base, i4, j + 2)
                low(base, i4, j + 3)
                dve.wait_ge(s["mm_units"], i4 + (base + j + 2))
                dve.wait_ge(s["rstd_done"], e + 1)
                dve.tensor_tensor(halves(tG[:, :]), pair(bank), halves(rstd[:, :]), ALU.mult).then_inc(s["tg_done"], 1)
                dve.tensor_tensor(halves(tU[:, :]), pair(bank + 2), halves(rstd[:, :]), ALU.mult).then_inc(s["up_evicted"], 1)
                dve.wait_ge(s["hid_hi"], f + (NF * F + 1))
                dve.tensor_tensor(flat_of(HL, f), tU[:, :], flat_of(HH, f).bitcast(F32), ALU.subtract)\
                   .then_inc(s["hid_done"], 1)

            for c in range(2):
                chunk(0, c, 2 * c)
            with dve.Fori(1, NF // 2) as i:
                for c in range(2):
                    chunk(i * 4, i * 2 + c, 2 * c)
            base += UP_UNITS
            with dve.Fori(0, 2) as i:
                for m4 in range(4):
                    for u in range(3):
                        low(base, i * 12, 3 * m4 + u + 2)
                    m = i * 4 + m4
                    dve.wait_ge(s["mm_units"], i * 12 + (base + 3 * m4 + 3))
                    dve.scalar_tensor_tensor(out=tile_of(H, m), in0=pair(2 * m4), scalar=0.5, in1=tile_of(H, m),
                                             op0=ALU.mult, op1=ALU.add).then_inc(s["h_done"], 1)
                    tile_low(e + 1, m)

        def feature_out(gr, j, n, dst, scale=None):
            dve.wait_ge(s["mm_units"], n + 1)
            dve.wait_ge(s["rstd_done"], gr.norm + 1)
            src = pair(gr.feat_bank(j))
            if scale is None:
                dve.tensor_tensor(halves(dst), src, halves(rstd[:, :]), ALU.mult).then_inc(s["feat_out"], 1)
            else:
                dve.scalar_tensor_tensor(out=halves(dst), in0=src, scalar=scale, in1=halves(rstd[:, :]),
                                         op0=ALU.mult, op1=ALU.mult).then_inc(s["feat_out"], 1)

        def features(gr):
            n = gr.start
            dests = ([(RT, None)] if gr.has_r else []) + \
                [(Q[:, h, :], gr.q_scale if gr.gla else None) for h in range(gr.NH)] + \
                [(K[:, h, :], None) for h in range(gr.NH)]
            for j, (dst, scale) in enumerate(dests):
                ahead(n)
                feature_out(gr, j, n, dst, scale)
                n += 1
            if gr.gi == 1:
                dve.tensor_copy(G[:, 0:2, :], OG[:, 6:8, :]).then_inc(s["x_made"], 1)
                dve.wait_ge(s["x_made"], 2)
            gate(gr)
            for u in range(4):
                ahead(n)
                n += 1
            for j in range(4):
                ahead(n)
                feature_out(gr, gr.nfeat + j, n, OG[:, 4 * gr.g + j, :])
                n += 1

        def gate(gr):
            if gr.gla:
                return
            k = gr.gi - 1
            gf = G[:].rearrange("p h t -> p (h t)")
            kf = K[:].rearrange("p h t -> p (h t)")
            dve.wait_ge(s["gate_ln"], gr.gi + 1)
            dve.scalar_tensor_tensor(out=gf, in0=kf, scalar=0.0, in1=EX[:, :], op0=ALU.min, op1=ALU.subtract)\
               .then_inc(s["ls_made"], 1)
            dve.wait_ge(s["ls_made"], k)
            for h in range(4):
                ins = dve.tensor_scalar(G[:, h, :], G[:, h, :], L1M[:, gr.h0 + h:gr.h0 + h + 1], None, ALU.add)
            ins.then_inc(s["c_made"], 1)
            dve.wait_ge(s["c_made"], k)
            dve.tensor_tensor(kf, gf, kf, ALU.subtract).then_inc(s["kx_made"], 1)
            for h in range(4):
                ins = dve.tensor_scalar(EX[:, h * T:(h + 1) * T], G[:, h, :], LLB[:, gr.h0 + h:gr.h0 + h + 1], None, ALU.subtract)
            ins.then_inc(s["gd_made"], 1)
            dve.wait_ge(s["gd_ln"], k)
            for h in range(4):
                ins = dve.scalar_tensor_tensor(out=G[:, h, :], in0=G[:, h, :], scalar=LLB[:, gr.h0 + h:gr.h0 + h + 1],
                                               in1=EX[:, h * T:(h + 1) * T], op0=ALU.max, op1=ALU.add)
            ins.then_inc(s["gate_made"], 1)

        def mix(gr):
            gi, NH = gr.gi, gr.NH
            if gr.has_r:
                dve.wait_ge(s["gk_mm"], 1)
                for h in range(4):
                    dst = G[:, h, :] if h < 2 else OG[:, 4 + h, :]
                    ins = dve.tensor_scalar(halves(dst), pair(2 * h), bgk[:, h:h + 1], None, ALU.add)
                ins.then_inc(s["x_made"], 1)
            if gr.gla:
                dve.wait_ge(s["gate_ln"], gi + 1)
                gf = G[:, 0:2, :].rearrange("p h t -> p (h t)")
                dve.scalar_tensor_tensor(out=gf, in0=gf, scalar=0.0, in1=EX[:, 0:2 * T], op0=ALU.min, op1=ALU.subtract)\
                   .then_inc(s["gate_made"], 1)

            def level_out(l):
                n, L = LEVELS * gi + l, 1 << l
                dve.wait_ge(s["lvl_mm"], n + 1)
                if l == 0:
                    dve.wait_ge(s["diag_out"], gi + 1)
                    dve.wait_ge(s["sdiag_out"], gi + 1)
                else:
                    dve.wait_ge(s["lvl_out"], n)
                if l == 1:
                    dve.wait_ge(s["slvl_out"], 2 * gi + 1)
                X = NH * NCH
                dst = AT[:, 0:X, :].rearrange("p x (n l) -> p x n l", l=2 * L)[:, :, :, L:2 * L]
                data = psf[:, 1024 * (l % 2):1024 * (l % 2) + 64 * X].rearrange("p (x n l) -> p x n l", x=X, l=L)
                msk = masks[:, l, :].bitcast(U32).rearrange("p (o n l) -> p o n l", o=1, l=L).to_broadcast([P, X, 64 // L, L])
                dve.copy_predicated(dst, msk, data).then_inc(s["lvl_out"], 1)
                if l < 2:
                    dst = ATS[:, 0:NH, :].rearrange("p x (n l) -> p x n l", l=2 * L)[:, :, :, L:2 * L]
                    data = ps[:, 4 + l, 0:16 * NH].rearrange("p (x n l) -> p x n l", x=NH, l=L)
                    msk = masks[:, l, 48:64].bitcast(U32).rearrange("p (o n l) -> p o n l", o=1, l=L)\
                        .to_broadcast([P, NH, 16 // L, L])
                    dve.copy_predicated(dst, msk, data).then_inc(s["slvl_out"], 1)

            for l in range(LEVELS):
                n, L = LEVELS * gi + l, 1 << l
                both = l < 2
                g1, g2, tot = blocks(G, gr, L, both)
                dk = compact(EX[:, 0:2 * T], gr, L, both)
                dve.wait_ge(s["gate_made"], (LEVELS + 1) * gi + l + 1)
                dve.tensor_tensor(dk, tot.to_broadcast(g1.shape), g1, ALU.subtract).then_inc(s["diff_made"], 1)
                if l == 0:
                    dve.wait_ge(s["diag_mm"], 2 * gi + 1)
                    X = NH * NCH
                    dve.tensor_tensor(AT[:, 0:X, :], psf[:, 2048:2048 + X * P].rearrange("p (x n) -> p x n", x=X),
                                      ident[:, :].rearrange("p (o n) -> p o n", o=1).to_broadcast([P, X, P]),
                                      ALU.mult).then_inc(s["diag_out"], 1)
                dve.wait_ge(s["ek_made"], n + 1)
                if l >= 2:
                    dve.wait_ge(s["lvl_mm"], n - 1)
                if l == 0:
                    dve.wait_ge(s["kt_zero"], gi + 1)
                    if not gr.gla:
                        dve.wait_ge(s["k_made"], gi - 1)
                k1, _, _ = blocks(K, gr, L, both)
                kt = KTb[:, l % 2, 0:NH * T].rearrange("p (h t) -> p h t", t=T)
                kt1, _, _ = blocks(kt, gr, L, both)
                dve.tensor_tensor(kt1, k1, dk, ALU.mult).then_inc(s["kt_made"], 1)
                dve.wait_ge(s["eq_made"], n + 1)
                dve.tensor_tensor(g2, g2, tot.to_broadcast(g2.shape), ALU.add).then_inc(s["gate_made"], 1)
                if l == 1:
                    dve.wait_ge(s["diag_mm"], 2 * gi + 2)
                    dve.tensor_tensor(ATS[:, 0:NH, :], ps[:, 6, 0:NH * 32].rearrange("p (x n) -> p x n", x=NH),
                                      ident[:, SROW:P].rearrange("p (o n) -> p o n", o=1).to_broadcast([P, NH, 32]),
                                      ALU.mult).then_inc(s["sdiag_out"], 1)
                if l == 0:
                    continue
                level_out(l - 1)
            dve.wait_ge(s["chunk_exp"], gi + 1)
            dve.wait_ge(s["diag_mm"], 2 * gi + 2)
            ex3 = EX[:, 0:NH * T].rearrange("p (h t) -> p h t", t=T)
            dve.tensor_tensor(Q[:, 0:NH, :], Q[:, 0:NH, :], ex3, ALU.mult).then_inc(s["qin_made"], 1)
            dve.wait_ge(s["qin_made"], gi + 1)
            for t0, t1, L in ((0, T_PROMPT, CHUNK), (T_PROMPT, T, T_SEQ)):
                g4 = G[:, 0:NH, t0:t1].rearrange("p h (n l) -> p h n l", l=L)
                e4 = ex3[:, :, t0:t1].rearrange("p h (n l) -> p h n l", l=L)
                dve.tensor_tensor(e4, g4[:, :, :, L - 1:L].to_broadcast(g4.shape), g4, ALU.subtract).then_inc(s["ksuf_made"], 1)
            level_out(LEVELS - 1)
            dve.wait_ge(s["ksuf_exp"], gi + 1)
            dve.tensor_tensor(K[:, 0:NH, :], K[:, 0:NH, :], ex3, ALU.mult).then_inc(s["kdec_made"], 1)
            dve.wait_ge(s["kd_turned"], gi + 1)
            dve.tensor_copy(KDS[:, 0:NH * P], ps[:, 4, 0:NH * P]).then_inc(s["kd_out"], 1)
            dve.wait_ge(s["dec_made"], 2 * gi + 2)
            dve.wait_ge(s["u_mm"], 4 * gi + 1)
            dve.tensor_copy(ST[:, 0, :], ps[:, 0, :]).then_inc(s["s_made"], 1)
            for c in range(1, NCH):
                dve.wait_ge(s["u_mm"], 4 * gi + c + 1)
                dve.wait_ge(s["s_made"], 4 * gi + c)
                for h in range(NH):
                    hv = slice(h * gr.V, (h + 1) * gr.V)
                    ins = dve.scalar_tensor_tensor(out=ST[:, c, hv], in0=ST[:, c - 1, hv], scalar=DEC[:, h, c:c + 1],
                                                   in1=ps[:, c, hv], op0=ALU.mult, op1=ALU.add)
                ins.then_inc(s["s_made"], 1)

            def kmask(b):
                if b >= 4:
                    dve.wait_ge(s["us_mm"], N_SEQ * gi + b - 3)
                if b == 0:
                    dve.wait_ge(s["kd_out"], 2 * gi + 2)
                dve.tensor_scalar(KM(b)[:, 0:NH * P], KDS[:, 0:NH * P], seqmask[:, b:b + 1], None, ALU.mult)\
                   .then_inc(s["kmask_made"], 1)

            for b in range(3):
                kmask(b)
            dve.wait_ge(s["os_mm"], gi + 1)
            dve.tensor_copy(Q[:, :, 0:T_PROMPT], ps[:, 4:8, :]).then_inc(s["o_out"], 1)
            dve.tensor_copy(Q[:, :, T_PROMPT:T], ps[:, 0, 0:P].rearrange("p (j t) -> p j t", j=4)).then_inc(s["o_out"], 1)
            for b in range(N_SEQ):
                if b + 3 < N_SEQ:
                    kmask(b + 3)
                dve.wait_ge(s["us_mm"], N_SEQ * gi + b + 1)
                for h in range(NH):
                    hv = slice(h * gr.V, (h + 1) * gr.V)
                    ins = dve.scalar_tensor_tensor(out=S0[:, b, hv], in0=S0[:, b, hv], scalar=DECS[:, h, b:b + 1],
                                                   in1=ps[:, 1 + b % 3, hv], op0=ALU.mult, op1=ALU.add)
                ins.then_inc(s["snew_made"], 1)
            dve.wait_ge(s["ors_made"], gi + 1)
            for j in range(4):
                dve.tensor_tensor(Q[:, j, :], Q[:, j, :], G[:, j // gr.vt_per_head, :], ALU.mult).then_inc(s["o_norm"], 1)
            dve.wait_ge(s["og_silu"], gi + 1)
            for j in range(4):
                dve.wait_ge(s["o_norm"], 4 * gi + j + 1)
                col = j % 2 if gr.gla else 2
                og = OG[:, 4 * gr.g + j, :]
                dve.scalar_tensor_tensor(out=og, in0=og, scalar=gn[:, col:col + 1], in1=Q[:, j, :],
                                         op0=ALU.mult, op1=ALU.mult).then_inc(s["og_made"], 1)
            dve.wait_ge(s["og_made"], 4 * gi + 4)

        def out_proj(l):
            e = 4 * l + 2
            for kk in range(KT_D):
                dve.wait_ge(s["out_hi"], 8 * l + kk + 1)
                dve.tensor_tensor(OL[:, kk, :], OG[:, kk, :], OH[:, kk, :].bitcast(F32), ALU.subtract).then_inc(s["out_lo"], 1)
            for m in range(KT_D):
                ahead(START["out", l] + m)
                dve.wait_ge(s["mm_units"], START["out", l] + m + 1)
                dve.tensor_tensor(tile_of(H, m), pair(2 * (m % 4)), tile_of(H, m), ALU.add).then_inc(s["h_done"], 1)
                tile_low(e, m)

        def ple(l):
            e, n = 4 * l + 3, START["ple", l]
            for m in range(KT_D):
                ahead(n + m)
                dve.wait_ge(s["mm_units"], n + m + 1)
                dve.wait_ge(s["rstd_done"], e + 1)
                dve.tensor_tensor(halves(GT[:, m, :]), pair(2 * (m % 4)), halves(rstd[:, :]), ALU.mult).then_inc(s["ple_t"], 1)
            for kt in range(2):
                dve.wait_ge(s["p_turned"], 2 * l + kt + 1)
                dve.tensor_copy(PT[:, kt, :], psf[:, 1024 * kt:1024 * kt + T]).then_inc(s["p_feat"], 1)
            for kt in range(2):
                dve.wait_ge(s["p_hi"], 2 * l + kt + 1)
                dve.tensor_tensor(PL[:, kt, :], PT[:, kt, :], PH[:, kt, :].bitcast(F32), ALU.subtract).then_inc(s["p_lo"], 1)
            for m in range(KT_D):
                if m % 4 == 3:
                    ahead(n + 8 + m // 4)
                    dve.wait_ge(s["mm_units"], n + 8 + m // 4 + 1)
                else:
                    dve.wait_ge(s["ple_mm"], 6 * l + 3 * (m // 4) + m % 4 + 1)
                dve.wait_ge(s["ple_sig"], 8 * l + m + 1)
                dve.tensor_tensor(halves(GT[:, m, :]), pair(2 * (m % 4)), halves(GT[:, m, :]), ALU.mult).then_inc(s["ple_x"], 1)
                dve.wait_ge(s["ple_x"], 8 * l + m + 1)
                dve.tensor_tensor(H[:, m, :], H[:, m, :], GT[:, m, :], ALU.add).then_inc(s["h_done"], 1)
                tile_low(e + 1, m)

        dve.memset(ones[:, :], 1.0).then_inc(s["dve_const"], 1)
        low(0, 0)
        low(1, 0)
        dve.wait_ge(s["const_dma"], 16 * 14)
        dve.tensor_tensor(lbd[:, 0, :], lbr[:, 0, :], lbr[:, 1, :], ALU.subtract).then_inc(s["lb_a"], 1)
        dve.wait_ge(s["lb_a"], 1)
        dve.tensor_scalar(lbd[:, 4, :], lbd[:, 0, :], -1.0, None, ALU.mult).then_inc(s["lb_a"], 1)
        dve.wait_ge(s["lb_a"], 2)
        dve.wait_ge(s["lb_c"], 1)
        dve.scalar_tensor_tensor(out=LLB, in0=lbd[:, 4, :], scalar=0.0, in1=lbd[:, 5, :], op0=ALU.min, op1=ALU.subtract)\
           .then_inc(s["lb_done"], 1)
        dve.scalar_tensor_tensor(out=L1M, in0=lbd[:, 0, :], scalar=0.0, in1=lbd[:, 5, :], op0=ALU.min, op1=ALU.subtract)\
           .then_inc(s["lb_done"], 1)
        dve.wait_ge(s["lb_done"], 2)
        for m in range(KT_D):
            dve.wait_ge(s["x_turned"], m + 1)
            dve.tensor_copy(H[:, m, :], psf[:, 1024 * (m % 4):1024 * (m % 4) + T]).then_inc(s["h_done"], 1)
            dve.wait_ge(s["h_done"], m + 1)
            tile_low(0, m)
        for l in range(2):
            ffn(2 * l)
            for g in range(2):
                features(GROUPS[2 * l + g])
                mix(GROUPS[2 * l + g])
            out_proj(l)
            ffn(2 * l + 1)
            ple(l)
        dve.wait_ge(s["rstd_done"], 9)
        for m in range(KT_D):
            dve.scalar_tensor_tensor(out=YF[:, m, :], in0=H[:, m, :], scalar=gains[:, 8, m:m + 1], in1=rstd[:, :],
                                     op0=ALU.mult, op1=ALU.mult).then_inc(s["y_made"], 1)
        for c in (0, 2, 4):
            rows = P if c < 4 else T_SAMPLE
            dve.wait_ge(s["y_turned"], c + 1)
            dve.tensor_copy(YT[0:rows, c, :], psf[0:rows, 1024 * (c % 4):1024 * (c % 4) + D]).then_inc(s["y_out_v"], 1)

    @block.gpsimd
    def _(pool):
        def square_in(e, m, mc, first):
            pool.wait_ge(s["sq_done"], m + (8 * e + 1))
            if first:
                pool.tensor_copy(ssq[:, :], (tG, tU)[mc % 2][:, :]).then_inc(s["ssq_added"], 1)
            else:
                pool.wait_ge(s["ssq_added"], m + 8 * e)
                pool.tensor_tensor(ssq[:, :], ssq[:, :], (tG, tU)[mc % 2][:, :], ALU.add).then_inc(s["ssq_added"], 1)

        def squares(e):
            for m in range(KT_D):
                square_in(e, m, m, m == 0)

        def ffn(F):
            with pool.Fori(0, NF) as f:
                pool.wait_ge(s["silu_done"], f + (NF * F + 1))
                pool.wait_ge(s["up_evicted"], f + (NF * F + 1))
                pool.tensor_tensor(tU[:, :], tG[:, :], tU[:, :], ALU.mult).then_inc(s["hid_mul"], 1)
            squares(2 * F + 1)

        def state_loads(gr):
            st = a["state_gla"] if gr.gla else a["state_hgrn"]
            pool.wait_ge(s["kdec_made"], gr.gi + 1)
            pool.wait_ge(s["lvl_mm"], LEVELS * (gr.gi + 1))
            for b in range(N_SEQ):
                pool.dma_start(S0[:, b, :].rearrange("p (h v) -> p h v", h=gr.NH),
                             st[0, b, gr.h0:gr.h0 + gr.NH].rearrange("h k v -> k h v")).then_inc(s["s0_in"], 16)

        def store_states(gr):
            out_p = o["gla_p"] if gr.gla else o["hgrn_p"]
            out_s = o["gla_s"] if gr.gla else o["hgrn_s"]
            heads = slice(gr.h0, gr.h0 + gr.NH)
            pool.wait_ge(s["s_made"], 4 * gr.gi + 4)
            pool.dma_start(out_p[0, 0, heads].rearrange("h k v -> k h v"),
                         ST[:, 3, :].rearrange("p (h v) -> p h v", h=gr.NH)).then_inc(s["out_state"], 16)
            for b in range(N_SEQ):
                pool.wait_ge(s["snew_made"], N_SEQ * gr.gi + b + 1)
                pool.dma_start(out_s[0, b, heads].rearrange("h k v -> k h v"),
                             S0[:, b, :].rearrange("p (h v) -> p h v", h=gr.NH)).then_inc(s["out_state"], 16)


        def mix(gr):
            gi, NH = gr.gi, gr.NH
            if gr.g == 0:
                pool.wait_ge(s["h_done"], 8 * gr.norm + 8)
            pool.memset(KTb[:], 0.0).then_inc(s["kt_zero"], 1)
            if gr.has_r:
                pool.wait_ge(s["kt_zero"], 1)
                pool.dma_start(KTb[P - 16:P, 1, 0:512], a["gla_w_gk_up"][0]).then_inc(s["w_gkup_in"], 16)
            for l in range(LEVELS):
                n, L = LEVELS * gi + l, 1 << l
                both = l < 2
                pool.wait_ge(s["eq_made"], n + 1)
                if l >= 2:
                    pool.wait_ge(s["lvl_mm"], n - 1)
                if l == 0:
                    pool.wait_ge(s["feat_out"], gr.feat0 + gr.nfeat)
                    if not gr.gla:
                        pool.wait_ge(s["q_made"], gi - 1)
                _, q2, _ = blocks(Q, gr, L, both)
                pool.tensor_tensor(compact(QTb[:, l % 2, :], gr, L, both), q2, compact(EX[:, 2 * T:4 * T], gr, L, both),
                                   ALU.mult).then_inc(s["qt_made"], 1)
            state_loads(gr)
            store_states(gr)
            pool.wait_ge(s["out_state"], 16 * 9 * (gi + 1))

        pool.memset(ident[:, :], 0.0).then_inc(s["pc"], 1)
        pool.memset(masks[:], 1.0).then_inc(s["pc"], 1)
        pool.memset(seqmask[:, :], 1.0).then_inc(s["pc"], 1)
        pool.memset(consts[:, 0:1], EPS).then_inc(s["pc"], 1)
        pool.memset(consts[:, 1:2], 1.0).then_inc(s["pool_const"], 1)
        pool.wait_ge(s["pc"], 4)
        pool.affine_select(out=ident[:, :], in_=ident[:, :], compare_op=ALU.not_equal, fill=1.0, base=0,
                           pattern=[[-1, P]], channel_multiplier=1).then_inc(s["ident_made"], 1)
        for l in range(LEVELS):
            L = 1 << l
            mv = masks[:, l, :].rearrange("p (n l) -> p n l", l=L)
            pool.affine_select(out=mv, in_=mv, compare_op=ALU.is_ge, fill=0.0, base=0,
                               pattern=[[-2 * L, 64 // L], [0, L]], channel_multiplier=1).then_inc(s["pc"], 1)
            pool.wait_ge(s["pc"], 5 + 2 * l)
            pool.affine_select(out=mv, in_=mv, compare_op=ALU.is_ge, fill=0.0, base=L - 1,
                               pattern=[[2 * L, 64 // L], [0, L]], channel_multiplier=-1).then_inc(s["pc"], 1)
            pool.wait_ge(s["pc"], 6 + 2 * l)
        pool.affine_select(out=seqmask[:, :], in_=seqmask[:, :], compare_op=ALU.is_ge, fill=0.0, base=-SROW,
                           pattern=[[-T_SEQ, N_SEQ]], channel_multiplier=1).then_inc(s["pc"], 1)
        pool.wait_ge(s["pc"], 5 + 2 * LEVELS)
        pool.affine_select(out=seqmask[:, :], in_=seqmask[:, :], compare_op=ALU.is_ge, fill=0.0, base=SROW + T_SEQ - 1,
                           pattern=[[T_SEQ, N_SEQ]], channel_multiplier=-1).then_inc(s["masks_made"], 1)
        squares(0)
        for l in range(2):
            ffn(2 * l)
            for g in range(2):
                mix(GROUPS[2 * l + g])
            squares(4 * l + 2)
            ffn(2 * l + 1)
            squares(4 * l + 4)


_INS = ["x_prompt", "x_sample", "state_gla", "state_hgrn", "p_prompt", "p_sample", "ffn1_norm", "ffn1_w_gu",
        "ffn1_w_down", "mix_norm", "gla_w_in", "gla_w_gk_up", "gla_b_gk", "gla_gn", "gla_w_out", "hgrn_w_in",
        "hgrn_gn", "hgrn_w_out", "hgrn_lower_bounds", "ffn2_norm", "ffn2_w_gu", "ffn2_w_down", "ple_norm",
        "ple_w_gate", "ple_w_proj", "final_norm"]
_OUTS = [("y_p", (1, T_PROMPT, D)), ("y_s", (N_SEQ, T_SEQ, D)), ("gla_p", (1, 1, 4, 128, 256)),
         ("gla_s", (1, N_SEQ, 4, 128, 256)), ("hgrn_p", (1, 1, 8, 128, 128)), ("hgrn_s", (1, N_SEQ, 8, 128, 128))]


def kernel(**inputs):
    import numpy as _np
    import concourse.bacc as _bacc
    from concourse import mybir as _mybir
    from concourse.bass_utils import run_bass_kernel_spmd as _run

    nc = _bacc.Bacc("TRN2", target_bir_lowering=False, num_devices=1)
    arrays, a, o = {}, {}, {}
    for name in _INS:
        x = _np.ascontiguousarray(inputs[name])
        arrays[f"in_{name}_dram"] = x
        a[name] = nc.dram_tensor(f"in_{name}_dram", x.shape, _mybir.dt.from_np(x.dtype), kind="ExternalInput").ap()
    for name, shape in _OUTS:
        o[name] = nc.dram_tensor(f"out_{name}_dram", shape, _mybir.dt.float32, kind="ExternalOutput").ap()
    build(nc, a, o)
    r = _run(nc, [arrays], core_ids=[0])
    return tuple(r.results[0][f"out_{name}_dram"] for name, _ in _OUTS)
```

```python
from contextlib import ExitStack

import concourse.bass as bass
from concourse import mybir

ALU = mybir.AluOpType
ACT = mybir.ActivationFunctionType
F32 = mybir.dt.float32
F32R = mybir.dt.float32r
U32 = mybir.dt.uint32

P = 128
D = 1024
KT_D = D // P
T_PROMPT = 512
N_SEQ, T_SEQ = 8, 4
T_SAMPLE = N_SEQ * T_SEQ
T = T_PROMPT + T_SAMPLE
HALF = T // 2
F_FF = 2816
NF = F_FF // P
PLE = 256
EPS = 1e-6

RING = 4
UNIT = 1024
ROW_GN = 9 * KT_D
ROW_BGK = ROW_GN + 3
ROW_LB = ROW_BGK + 4
VROWS = ROW_LB + 2 * KT_D
N_VEC_LOADS = 14
DOWN_KT = [(0, 8), (8, 16), (16, 22)]
UP_UNITS = 2 * NF
DOWN_UNITS = 3 * KT_D
FFN_UNITS = UP_UNITS + DOWN_UNITS

CHUNK = 128
NCH = T_PROMPT // CHUNK
LEVELS = 7
LASTTILE = T - P
SROW = P - T_SAMPLE
VCOLS = 512

GLA_UNITS = [13, 12]
HGRN_UNITS = [16, 16]
OUT_UNITS = 8
PLE_GATE_UNITS, PLE_PROJ_UNITS = 8, 2
START = {}
_n = 0
for _l in range(2):
    START["ffn", 2 * _l] = _n
    _n += FFN_UNITS
    for _g, _u in enumerate((GLA_UNITS, HGRN_UNITS)[_l]):
        START["mix", 2 * _l + _g] = _n
        _n += _u
    START["out", _l] = _n
    _n += OUT_UNITS
    START["ffn", 2 * _l + 1] = _n
    _n += FFN_UNITS
    START["ple", _l] = _n
    _n += PLE_GATE_UNITS + PLE_PROJ_UNITS
N_UNITS = _n


class Group:

    def __init__(self, gi):
        self.gi = gi
        self.gla = gi < 2
        self.layer = 0 if self.gla else 1
        self.g = gi % 2
        self.NH = 2 if self.gla else 4
        self.V = VCOLS // self.NH
        self.h0 = self.g * self.NH
        self.start = START["mix", gi]
        self.has_r = gi == 0
        self.nfeat = 2 * self.NH + self.has_r
        self.vt_per_head = self.V // P
        self.gate_scale = 1.0 / 16.0 if self.gla else 1.0
        self.q_scale = float(P) ** -0.5 if self.gla else 1.0
        self.feat0 = [0, 9, 17, 29][gi]
        self.g_unit = self.start + self.nfeat
        self.v_unit = self.g_unit + 4
        units = [("g", j) for j in range(4)] + [("v", u) for u in range(4)]
        if self.gla:
            levels = ["diag"] + list(range(LEVELS))
        else:
            levels = [None] * 3 + ["diag"] + list(range(LEVELS))
            units += [(None, None)] * 3
        self.steps = [(kind, j, lv) for (kind, j), lv in zip(units, levels)]
        self.norm = 1 if self.gla else 5

    def level_bank(self, l):
        return 4 + l % 2 if self.NH == 2 else (6 if l in (4, 6) else 4)

    def feat_bank(self, j):
        if j >= self.nfeat:
            return [0, 2, 0, 2][j - self.nfeat]
        if j < 2:
            return 2 * j
        return 6 if (self.nfeat - 1 - j) % 2 == 0 else 4


GROUPS = [Group(gi) for gi in range(4)]
N_STATE = [0]
for _gr in GROUPS:
    N_STATE.append(N_STATE[-1] + 1 + 2 * _gr.NH)
N_S0 = [4, 8, 16, 24]
N_HEADS = [0, 2, 4, 8, 12]
KM_BUFS = 6
V_BANKS = [0, 1, 2, 3, 7]


def build(nc, a, o):
    with ExitStack() as ctx:
        _build(nc, a, o, ctx)


def _build(nc, a, o, ctx):
    def sb(name, shape, dt=F32, where=ctx):
        return where.enter_context(nc.sbuf_tensor(name, shape, dt))

    ps = ctx.enter_context(nc.psum_tensor("ps", [P, 8, 512], F32))
    psf = ps[:].rearrange("p b n -> p (b n)")

    H = sb("h_resid", [P, KT_D, T])
    UH = sb("u_high", [P, KT_D, T], F32R)
    UL = sb("u_low", [P, KT_D, T], F32R)
    RAW = sb("w_raw", [P, RING, UNIT])
    WH = sb("w_high", [P, RING, UNIT], F32R)
    WL = sb("w_low", [P, RING, UNIT], F32R)
    ident = sb("ident", [P, P])
    ones = sb("ones", [P, P])
    masks = sb("masks", [P, LEVELS, 64])
    seqmask = sb("seqmask", [P, N_SEQ])
    vecs = sb("vectors", [P, VROWS])
    lbd = sb("lbd", [P, 6, KT_D])
    consts = sb("consts", [P, 2])
    rstd = sb("rstd", [P, T])
    rstdT = sb("rstd_tok", [P, 5])
    ssq = sb("ssq", [P, T])
    tG = sb("t_gate", [P, T])
    tU = sb("t_up", [P, T])
    DEC = sb("decay_chunk", [P, 4, NCH])
    DECS = sb("decay_seq", [P, 4, N_SEQ])

    with ExitStack() as region:
        HH = sb("hid_high", [P, NF, T], F32R, region)
        HL = sb("hid_low", [P, NF, T], F32R, region)
    with ExitStack() as region:
        XIN = sb("x_tok", [P, 5, D], F32, region)
    with ExitStack() as region:
        YF = sb("y_feat", [P, KT_D, T], F32, region)
        YT = sb("y_tok", [P, 5, D], F32, region)
    with ExitStack() as region:
        PIN = sb("p_tok", [P, 5, PLE], F32, region)
        PH = sb("p_high", [P, 2, T], F32R, region)
        PL = sb("p_low", [P, 2, T], F32R, region)
        PT = sb("p_feat", [P, 2, T], F32, region)
        GT = sb("ple_gate", [P, KT_D, T], F32, region)
    with ExitStack() as region:
        OH = sb("o_high", [P, KT_D, T], F32R, region)
        OL = sb("o_low", [P, KT_D, T], F32R, region)
    with ExitStack() as region:
        Q = sb("q", [P, 4, T], F32, region)
        K = sb("k", [P, 4, T], F32, region)
        G = sb("gate_sum", [P, 4, T], F32, region)
        V = sb("v_tok", [P, 5, VCOLS], F32, region)
        AT = sb("attn", [P, 16, P], F32, region)
        ATS = sb("attn_s", [P, 4, T_SAMPLE], F32, region)
        OG = sb("out_gate", [P, KT_D, T], F32, region)
        KTb = sb("k_tilde", [P, 2, 4 * T], F32, region)
        QTb = sb("q_tilde", [P, 2, 2 * T], F32, region)
        EX = sb("ex", [P, 4 * T], F32, region)
    with ExitStack() as region:
        for nm, w in (("al_q", 4 * T), ("al_k", 4 * T), ("al_g", 4 * T), ("al_v", 5 * VCOLS), ("al_at", 16 * P),
                      ("al_ats", 4 * T_SAMPLE), ("al_og", KT_D * T)):
            sb(nm, [P, w], F32, region)
        KD = sb("kdec_tok", [P, 16, P], F32, region)
        ST = sb("states", [P, 4, VCOLS], F32, region)
        sb("al_pad", [P, 2 * 4 * T - 16 * P - 4 * VCOLS], F32, region)
        S0 = sb("states_s", [P, N_SEQ, VCOLS], F32, region)
    with ExitStack() as region:
        for nm, w in (("al2_q", 4 * T), ("al2_k", 4 * T), ("al2_g", 4 * T), ("al2_v", 5 * VCOLS)):
            sb(nm, [P, w], F32, region)
        ORS = sb("head_rstd", [P, 4, T], F32, region)
    ROWS = rstd[0:VROWS, 0:P]
    gains = vecs[:, 0:ROW_GN].rearrange("p (e m) -> p e m", m=KT_D)
    gn = vecs[:, ROW_GN:ROW_GN + 3]
    bgk = vecs[:, ROW_BGK:ROW_BGK + 4]
    lbr = vecs[:, ROW_LB:VROWS].rearrange("p (l m) -> p l m", m=KT_D)

    names = (
        "raw0 raw1 raw2 raw3 hi_made lo_made mm_units "
        "pc masks_made const_dma x_in w_gkup_in p_in s0_in out_y out_state st_stored "
        "dve_const pool_const ident_made x_turned h_done uh_done sq_done u_done ssq_added norm_mm ln_done rstd_done "
        "tg_done up_evicted silu_done hid_mul hid_hi hid_done "
        "feat_out v_out lb_a lb_b lb_c lb_done r_used gk_mm x_made gate_abs gate_exp gate_ln ls_made c_made kx_made "
        "gd_made gd_abs gd_exp gd_ln k_made gate_made q_made kt_zero diff_made ek_made eq_made kt_made qt_made "
        "lvl_mm lvl_out diag_mm diag_out sdiag_out slvl_out chunk_exp qin_made ksuf_made ksuf_exp kdec_made dec_made "
        "kd_turned kds_turned vec_turned vec_made kd_out u_mm s_made kmask_made kmask_used us_mm snew_made o_mm os_mm o_out osq_made "
        "var_mm var_ln ors_made og_pre og_silu og_made out_hi out_lo "
        "ple_t ple_sig p_turned p_feat p_hi p_lo ple_mm ple_x y_made y_turned y_out_a y_out_v"
    ).split()
    s = {n: ctx.enter_context(nc.semaphore(n)) for n in names}
    raw_sem = [s["raw0"], s["raw1"], s["raw2"], s["raw3"]]

    def pair(b):
        return ps[:, b:b + 2, 0:HALF]

    def halves(ap):
        return ap.rearrange("p (a b) -> p a b", a=2)

    def tile_of(t3, m):
        if isinstance(m, int):
            return halves(t3[:, m, :])
        return t3[:, bass.ds(m, 1), :].rearrange("p o (a b) -> p (o a) b", a=2)

    def flat_of(t3, m):
        if isinstance(m, int):
            return t3[:, m, :]
        return t3[:, bass.ds(m, 1), :].rearrange("p o t -> p (o t)")

    w_gu = [a["ffn1_w_gu"], a["ffn2_w_gu"]]
    w_dn = [a["ffn1_w_down"], a["ffn2_w_down"]]

    RT = OG[:, KT_D - 1, :]
    EP = KTb[:, 1, :]
    LLB, L1M = lbd[:, 3, :], lbd[:, 1, :]
    WUP = KTb[:, 1, 0:512]

    def KM(b):
        i = b % KM_BUFS
        return G[:].rearrange("p h t -> p (h t)")[:, i * 512:(i + 1) * 512] if i < 4 else (tG, tU)[i - 4][:, 0:512]

    def blocks(ap, gr, L, all_tokens):
        if all_tokens:
            v = ap[:, 0:gr.NH, :].rearrange("p h (n l) -> p (h n) l", l=2 * L)
            return v[:, :, 0:L], v[:, :, L:2 * L], v[:, :, L - 1:L]
        v = ap[:, 0:gr.NH, 0:T_PROMPT].rearrange("p h (n l) -> p h n l", l=2 * L)
        return v[:, :, :, 0:L], v[:, :, :, L:2 * L], v[:, :, :, L - 1:L]

    def compact(ap2, gr, L, all_tokens):
        v = ap2[:, 0:gr.NH * HALF].rearrange("p (h t) -> p h t", t=HALF)
        if all_tokens:
            return v.rearrange("p h (n l) -> p (h n) l", l=L)
        return v[:, :, 0:T_PROMPT // 2].rearrange("p h (n l) -> p h n l", l=L)

    block = ctx.enter_context(nc.Block())

    @block.sync
    def _(sp):
        def load_unit(base, i, j, src, nkt, width, free=True):
            n = base + j
            slot = n % RING
            if free and (not isinstance(i, int) or n + i >= RING):
                sp.wait_ge(s["lo_made"], i + (n - RING + 1))
            sp.dma_start(RAW[:, slot, 0:nkt * width].rearrange("p (k n) -> p k n", k=nkt), src)\
              .then_inc(raw_sem[slot], 16)

        def cols(w, k0, k1, c0, n):
            v = w.rearrange("(k p) n -> p k n", p=P)
            return v[:, k0:k1, bass.ds(c0, n)]

        def ffn(F):
            l, base = F // 2, START["ffn", F]
            gu, dn = w_gu[F % 2][l], w_dn[F % 2][l]

            def up_body(i, off):
                for j in range(4):
                    f2, up = j // 2, j % 2
                    load_unit(base, off, j, cols(gu, 0, KT_D, i * (2 * P) + (f2 * P + up * F_FF), P), KT_D, P)

            if F == 0:
                for j in range(RING):
                    load_unit(0, 0, j, cols(gu, 0, KT_D, (j // 2) * P + (j % 2) * F_FF, P), KT_D, P)
            else:
                up_body(0, 0)
            with sp.Fori(1, NF // 2) as i:
                up_body(i, i * 4)
            with sp.Fori(0, 2) as i:
                for m4 in range(4):
                    for u, (k0, k1) in enumerate(DOWN_KT):
                        load_unit(base + UP_UNITS, i * 12, m4 * 3 + u, cols(dn, k0, k1, i * (4 * P) + m4 * P, P), k1 - k0, P)

        def early_loads():
            sp.dma_start(XIN[:, 0:4, :], a["x_prompt"][0].rearrange("(c p) d -> p c d", p=P)).then_inc(s["x_in"], 16)
            sp.dma_start(XIN[0:T_SAMPLE, 4, :], a["x_sample"].rearrange("b t d -> (b t) d")).then_inc(s["x_in"], 16)

        def state_loads(gr):
            st = a["state_gla"] if gr.gla else a["state_hgrn"]
            for half in range(2):
                if half == 0:
                    sp.wait_ge(s["lvl_mm"], LEVELS * (gr.gi + 1))
                else:
                    sp.wait_ge(s["kdec_made"], gr.gi + 1)
                for h in range(gr.NH):
                    sp.dma_start(S0[:, 4 * half:4 * half + 4, h * gr.V:(h + 1) * gr.V],
                                 st[0, 4 * half:4 * half + 4, gr.h0 + h].rearrange("b k v -> k b v")).then_inc(s["s0_in"], 16)

        def store_states(gr):
            out_p = o["gla_p"] if gr.gla else o["hgrn_p"]
            out_s = o["gla_s"] if gr.gla else o["hgrn_s"]
            sp.wait_ge(s["s_made"], 4 * gr.gi + 4)
            sp.dma_start(out_p[0, 0, gr.h0:gr.h0 + gr.NH].rearrange("h k v -> k h v"),
                         ST[:, 3, :].rearrange("p (h v) -> p h v", h=gr.NH)).then_inc(s["out_state"], 16)
            for half in range(2):
                sp.wait_ge(s["snew_made"], N_SEQ * gr.gi + 4 * half + 4)
                for h in range(gr.NH):
                    sp.dma_start(out_s[0, 4 * half:4 * half + 4, gr.h0 + h].rearrange("b k v -> k b v"),
                                 S0[:, 4 * half:4 * half + 4, h * gr.V:(h + 1) * gr.V]).then_inc(s["out_state"], 16)

        def mix_sources(gr):
            w = a["gla_w_in"][0] if gr.gla else a["hgrn_w_in"][0]
            q0 = gr.h0 * P
            k0 = (512 if gr.gla else 1024) + gr.h0 * P
            v0 = (1024 if gr.gla else 2048) + gr.g * VCOLS
            g0 = (2048 if gr.gla else 3072) + gr.g * VCOLS
            starts = ([3088 - P] if gr.has_r else []) + [q0 + P * h for h in range(gr.NH)] +                 [k0 + P * h for h in range(gr.NH)] + [g0 + P * t for t in range(4)]
            return [(cols(w, 0, KT_D, c, P), KT_D, P) for c in starts] +                 [(cols(w, 2 * u, 2 * u + 2, v0, VCOLS), 2, VCOLS) for u in range(4)]

        def out_sources(l):
            w = (a["gla_w_out"] if l == 0 else a["hgrn_w_out"])[0]
            return [(cols(w, 0, KT_D, m * P, P), KT_D, P) for m in range(KT_D)]

        def mixer(l):
            groups = GROUPS[2 * l:2 * l + 2]
            n = groups[0].start
            for i, src in enumerate([mix_sources(groups[0]), mix_sources(groups[1]), out_sources(l)]):
                for j, (ap, nkt, width) in enumerate(src):
                    if i and j == 4:
                        state_loads(groups[i - 1])
                        store_states(groups[i - 1])
                    load_unit(n, 0, 0, ap, nkt, width)
                    n += 1

        early_loads()
        for l in range(2):
            ffn(2 * l)
            mixer(l)
            ffn(2 * l + 1)
            for m in range(4):
                load_unit(START["ple", l] + m, 0, 0, cols(a["ple_w_gate"][l], 0, KT_D, m * P, P), KT_D, P)
            sp.wait_ge(s["h_done"], 8 * (4 * l + 3) + 8)
            sp.dma_start(PIN[:, 0:4, :], a["p_prompt"][l, 0].rearrange("(c p) d -> p c d", p=P)).then_inc(s["p_in"], 16)
            sp.dma_start(PIN[0:T_SAMPLE, 4, :], a["p_sample"][l].rearrange("b t d -> (b t) d")).then_inc(s["p_in"], 16)
            for m in range(4, 8):
                load_unit(START["ple", l] + m, 0, 0, cols(a["ple_w_gate"][l], 0, KT_D, m * P, P), KT_D, P)
            for u in range(2):
                load_unit(START["ple", l] + 8 + u, 0, 0, cols(a["ple_w_proj"][l], 0, 2, u * 512, 512), 2, 512)
        for c in range(5):
            sp.wait_ge(s["y_out_a" if c % 2 else "y_out_v"], c // 2 + 1)
            if c < 4:
                sp.dma_start(o["y_p"][0, c * P:(c + 1) * P, :], YT[:, c, :]).then_inc(s["out_y"], 16)
            else:
                sp.dma_start(o["y_s"].rearrange("b t d -> (b t) d"), YT[0:T_SAMPLE, 4, :]).then_inc(s["out_y"], 16)
        sp.wait_ge(s["out_y"], 16 * 5)
        sp.wait_ge(s["out_state"], 16 * N_STATE[4])

    @block.tensor
    def _(pe):
        def weights(slot, k, kind, m0=0, mw=P, kw=P):
            w = WH if kind == "h" else WL
            return w[:, slot, k * kw + m0:k * kw + m0 + mw]

        def unit_ready(n):
            pe.wait_ge(s["lo_made"], n + 1)

        def products(slot, nk, k0, kt_total, bank, xh, xl, m0=0, kw=P, before=None):
            for k in range(nk):
                kk = k0 + k
                if before is not None:
                    before(kk)
                for part, (wk, x) in enumerate((("h", xh), ("h", xl), ("l", xh))):
                    for hf in range(2):
                        mm = pe.matmul(ps[:, bank + hf, 0:HALF], weights(slot, k, wk, m0, P, kw),
                                       x[:, kk, hf * HALF:(hf + 1) * HALF],
                                       start=(kk == 0 and part == 0), stop=(kk == kt_total - 1 and part == 2))
            return mm

        def wait_u(e):
            def before(kk):
                pe.wait_ge(s["u_done"], 8 * e + kk + 1)
            return before

        def norm(e, by_token=False):
            pe.wait_ge(s["ssq_added"], 8 * e + 8)
            pe.wait_ge(s["h_done"], 8 * e + 7)
            for hf in range(2):
                mm = pe.matmul(ps[:, 4 + hf, 0:HALF], ones[:, :], ssq[:, hf * HALF:(hf + 1) * HALF], start=True, stop=True)
            if by_token:
                for c in range(5):
                    t0 = c * P if c < 4 else LASTTILE
                    mm = pe.matmul(ps[:, 4, 300 + c:301 + c], ssq[:, t0:t0 + P], ones[:, 0:1], start=True, stop=True)
            mm.then_inc(s["norm_mm"], 1)

        def ffn(F):
            base, e = START["ffn", F], 2 * F

            def chunk(f, n, slot, first):
                bank = 4 * (slot // 2)
                if first and bank == 0:
                    pe.wait_ge(s["h_done"], 8 * e + 6)
                elif first:
                    pe.wait_ge(s["h_done"], 8 * e + 8)
                    pe.wait_ge(s["rstd_done"], e + 1)
                else:
                    pe.wait_ge(s["up_evicted"], f + (NF * F - 1))
                for up in range(2):
                    unit_ready(n + up)
                    products((base + slot + up) % RING, KT_D, 0, KT_D, bank + 2 * up, UH, UL,
                             before=wait_u(e) if first and bank == 0 else None).then_inc(s["mm_units"], 1)
                    if first and bank == 0 and up == 0:
                        norm(e)

            for c in range(2):
                chunk(c, base + 2 * c, 2 * c, True)
            with pe.Fori(1, NF // 2) as i:
                for c in range(2):
                    chunk(i * 2 + c, i * 4 + (base + 2 * c), 2 * c, False)
            base += UP_UNITS
            def down_tile(i, m4, first):
                if first:
                    pe.wait_ge(s["up_evicted"], NF * F + (NF - 1 if m4 < 2 else NF))
                else:
                    pe.wait_ge(s["h_done"], 8 * (e + 1) + m4 + 1)
                for u, (k0, k1) in enumerate(DOWN_KT):
                    n = m4 * 3 + u
                    unit_ready(i * 12 + (base + n))

                    def before(kk):
                        if first and m4 == 0:
                            pe.wait_ge(s["hid_done"], NF * F + kk + 1)
                    products((base + n) % RING, k1 - k0, k0, NF, 2 * m4, HH, HL, before=before).then_inc(s["mm_units"], 1)

            for m4 in range(4):
                down_tile(0, m4, True)
            for m4 in range(4):
                down_tile(1, m4, False)

        def features(gr):
            e = gr.norm
            j = 0
            n = gr.start
            def feature_tile(j, n):
                b = gr.feat_bank(j)
                if j < 2 and gr.g == 0:
                    pe.wait_ge(s["h_done"], 8 * e + 6)
                elif gr.g == 0 and j == 2:
                    pe.wait_ge(s["h_done"], 8 * e + 8)
                    pe.wait_ge(s["rstd_done"], e + 1)
                    pe.wait_ge(s["feat_out"], gr.feat0 + j - 1)
                elif j >= gr.nfeat:
                    i = j - gr.nfeat
                    if i < 2 and gr.has_r:
                        pe.wait_ge(s["x_made"], 1)
                    else:
                        pe.wait_ge(s["feat_out"], gr.feat0 + (i + 1 if i < 2 else j - 1))
                elif 2 <= j < gr.nfeat:
                    pe.wait_ge(s["feat_out"], gr.feat0 + j - 1)
                elif gr.g == 1 and j == 0:
                    pe.wait_ge(s["var_ln"], 2 * gr.gi)
                elif gr.g == 1 and j == 1:
                    pe.wait_ge(s["snew_made"], N_SEQ * gr.gi)
                unit_ready(n)
                products(n % RING, KT_D, 0, KT_D, b, UH, UL,
                         before=wait_u(e) if j == 0 and gr.g == 0 else None).then_inc(s["mm_units"], 1)
                if j == 0 and gr.g == 0:
                    norm(e, True)
            for j in range(gr.nfeat):
                feature_tile(j, n)
                n += 1
            if gr.has_r:
                gk(gr)
            for kind, j, lv in gr.steps:
                if kind == "g":
                    feature_tile(gr.nfeat + j, n)
                    n += 1
                elif kind == "v":
                    values(gr, j, n)
                    n += 1
                if lv == "diag":
                    diagonal(gr)
                elif lv is not None:
                    level(gr, lv)

        def values(gr, u, n):
            unit_ready(n)
            for c in range(5):
                t0 = c * P if c < 4 else LASTTILE
                if u == 0 and c in (0, 2):
                    pe.wait_ge(s["feat_out"], gr.feat0 + gr.nfeat + 3 + (c == 2))
                if u == 0 and c == 4:
                    pe.wait_ge(s["diag_out"], gr.gi + 1)
                for k in range(2):
                    kk = 2 * u + k
                    for part, (x, w) in enumerate(((UH, WH), (UL, WH), (UH, WL))):
                        mm = pe.matmul(ps[:, V_BANKS[c], :], x[:, kk, t0:t0 + P], w[:, n % RING, k * 512:(k + 1) * 512],
                                       start=(kk == 0 and part == 0), stop=(kk == KT_D - 1 and part == 2))
            mm.then_inc(s["mm_units"], 1)

        def diagonal(gr):
            gi = gr.gi
            pe.wait_ge(s["feat_out"], gr.feat0 + gr.nfeat)
            if gr.has_r:
                pe.wait_ge(s["x_made"], 1)
            if not gr.gla:
                pe.wait_ge(s["q_made"], gi - 1)
                pe.wait_ge(s["k_made"], gi - 1)
            for h in range(gr.NH):
                for c in range(NCH):
                    x = h * NCH + c
                    mm = pe.matmul(ps[:, 4 + x // 4, (x % 4) * P:(x % 4 + 1) * P], K[:, h, c * P:(c + 1) * P],
                                   Q[:, h, c * P:(c + 1) * P], start=True, stop=True)
            mm.then_inc(s["diag_mm"], 1)

        def level(gr, l):
            gi, NH = gr.gi, gr.NH
            n = LEVELS * gi + l
            b0 = gr.level_bank(l)
            pe.wait_ge(s["kt_made"], n + 1)
            pe.wait_ge(s["qt_made"], n + 1)
            if l == 0:
                pe.wait_ge(s["diag_out"], gi + 1)
            elif NH == 4 and l < 4:
                pe.wait_ge(s["lvl_out"], n)
            elif NH == 4 and l == 4:
                pe.wait_ge(s["slvl_out"], 2 * gi + 2)
                pe.wait_ge(s["v_out"], 5 * gi + 5)
            elif l >= 2:
                pe.wait_ge(s["lvl_out"], n - 1)
            for h in range(NH):
                for c in range(NCH):
                    x = h * NCH + c
                    mm = pe.matmul(ps[:, b0 + x // 8, (x % 8) * 64:(x % 8 + 1) * 64],
                                   KTb[:, l % 2, h * T + c * P:h * T + (c + 1) * P],
                                   QTb[:, l % 2, h * HALF + c * 64:h * HALF + (c + 1) * 64], start=True, stop=True)
            if l == 1:
                pe.wait_ge(s["slvl_out"], 2 * gi + 1)
                pe.wait_ge(s["sdiag_out"], gi + 1)
            if l < 2:
                for h in range(NH):
                    mm = pe.matmul(ps[:, 6, (8 + 4 * l + h) * 16:(9 + 4 * l + h) * 16], KTb[:, l % 2, h * T + LASTTILE:(h + 1) * T],
                                   QTb[:, l % 2, h * HALF + 256:(h + 1) * HALF], start=True, stop=True)
            if l == 0:
                for h in range(NH):
                    mm = pe.matmul(ps[:, 6, h * 32:(h + 1) * 32], K[:, h, LASTTILE:T], Q[:, h, T_PROMPT:T],
                                   start=True, stop=True)
            mm.then_inc(s["lvl_mm"], 1)

        def gk(gr):
            pe.wait_ge(s["w_gkup_in"], 16)
            pe.wait_ge(s["feat_out"], gr.feat0 + gr.nfeat)
            for h in range(4):
                for hf in range(2):
                    mm = pe.matmul(ps[:, 2 * h + hf, 0:HALF], WUP[:, h * P:(h + 1) * P],
                                   RT[:, hf * HALF:(hf + 1) * HALF], start=True, stop=True)
            mm.then_inc(s["gk_mm"], 1)

        def mix(gr):
            gi, NH = gr.gi, gr.NH
            pe.wait_ge(s["v_out"], 5 * gi + 5)
            pe.wait_ge(s["kdec_made"], gi + 1)
            for h in range(NH):
                for c in range(NCH):
                    x = h * NCH + c
                    mm = pe.transpose(ps[:, x // 4, (x % 4) * P:(x % 4 + 1) * P], K[:, h, c * P:(c + 1) * P], ident[:, :])
            mm.then_inc(s["kd_turned"], 1)
            pe.wait_ge(s["lvl_out"], LEVELS * (gi + 1))
            for j in range(4):
                h = j // gr.vt_per_head
                for c in range(NCH):
                    pe.matmul(ps[:, 4 + j, c * P:(c + 1) * P], V[:, c, j * P:(j + 1) * P], AT[:, h * NCH + c, :],
                              start=(c == 0), stop=False, skip_group_check=True)
            pe.wait_ge(s["kd_out"], gi + 1)
            for c in range(NCH):
                for h in range(NH):
                    mm = pe.matmul(ps[:, c, h * gr.V:(h + 1) * gr.V], KD[:, h * NCH + c, :],
                                   V[:, c, h * gr.V:(h + 1) * gr.V], start=True, stop=True)
                mm.then_inc(s["u_mm"], 1)
            pe.wait_ge(s["qin_made"], gi + 1)
            pe.wait_ge(s["slvl_out"], 2 * (gi + 1))
            pe.wait_ge(s["s_made"], 4 * gi + 1)
            for j in range(4):
                h = j // gr.vt_per_head
                pe.matmul(ps[:, 0, j * 32:(j + 1) * 32], V[:, 4, j * P:(j + 1) * P], ATS[:, h, :],
                          start=(j == 0), stop=False, skip_group_check=True)
            pe.wait_ge(s["s0_in"], 16 * N_S0[gi])
            for j in range(4):
                h = j // gr.vt_per_head
                for b in range(N_SEQ):
                    mm = pe.matmul(ps[:, 0, j * 32 + 4 * b:j * 32 + 4 * b + 4], S0[:, b, j * P:(j + 1) * P],
                                   Q[:, h, T_PROMPT + 4 * b:T_PROMPT + 4 * b + 4],
                                   start=False, stop=(j == 3 and b == N_SEQ - 1), skip_group_check=True)
            mm.then_inc(s["os_mm"], 1)
            pe.wait_ge(s["s_made"], 4 * gi + 2)
            for h in range(NH):
                mm = pe.transpose(ps[:, 1, h * P:(h + 1) * P], K[:, h, LASTTILE:T], ident[:, :])
            mm.then_inc(s["kds_turned"], 1)
            pe.wait_ge(s["s_made"], 4 * gi + NCH - 1)
            for j in range(4):
                h = j // gr.vt_per_head
                for c in range(1, NCH):
                    mm = pe.matmul(ps[:, 4 + j, c * P:(c + 1) * P], ST[:, c - 1, j * P:(j + 1) * P],
                                   Q[:, h, c * P:(c + 1) * P], start=False, stop=(c == NCH - 1), skip_group_check=True)
                mm.then_inc(s["o_mm"], 1)

            def sequence(b):
                pe.wait_ge(s["kmask_made"], N_SEQ * gi + b + 1)
                if b < 2:
                    pe.wait_ge(s["s_made"], 4 * gi + NCH)
                else:
                    pe.wait_ge(s["snew_made"], N_SEQ * gi + b - 1)
                for h in range(NH):
                    mm = pe.matmul(ps[:, 2 + b % 2, h * gr.V:(h + 1) * gr.V], KM(b)[:, h * P:(h + 1) * P],
                                   V[:, 4, h * gr.V:(h + 1) * gr.V], start=True, stop=True)
                mm.then_inc(s["us_mm"], 1)

            for b in range(2):
                sequence(b)
            for h in range(NH):
                vt = gr.vt_per_head
                pe.wait_ge(s["osq_made"], 4 * gi + (h + 1) * vt)
                for t0, t1, dst in ((0, T_PROMPT, ps[:, 4 + h, :]),
                                    (T_PROMPT, T, ps[:, 0, h * T_SAMPLE:(h + 1) * T_SAMPLE])):
                    for t in range(vt):
                        mm = pe.matmul(dst, ones[:, :], K[:, h * vt + t, t0:t1], start=(t == 0), stop=(t == vt - 1))
            mm.then_inc(s["var_mm"], 1)
            for b in range(2, N_SEQ):
                sequence(b)

        def out_proj(l):
            n = START["out", l]
            e = 4 * l + 2
            for m in range(KT_D):
                if m == 0:
                    pe.wait_ge(s["var_ln"], 2 * (2 * l + 2))
                if m == 1:
                    pe.wait_ge(s["snew_made"], N_SEQ * (2 * l + 2))
                if m >= 4:
                    pe.wait_ge(s["h_done"], 8 * e + m - 3)
                unit_ready(n)

                def before(kk):
                    if m == 0:
                        pe.wait_ge(s["out_lo"], 8 * l + kk + 1)
                products(n % RING, KT_D, 0, KT_D, 2 * (m % 4), OH, OL, before=before).then_inc(s["mm_units"], 1)
                n += 1

        def ple(l):
            n = START["ple", l]
            e = 4 * l + 3
            for m in range(KT_D):
                if m == 0:
                    pe.wait_ge(s["h_done"], 8 * e + 6)
                elif m == 2:
                    pe.wait_ge(s["h_done"], 8 * e + 8)
                    pe.wait_ge(s["rstd_done"], e + 1)
                elif m >= 4:
                    pe.wait_ge(s["ple_t"], 8 * l + m - 3)
                unit_ready(n)
                products(n % RING, KT_D, 0, KT_D, 2 * (m % 4), UH, UL, before=wait_u(e) if m == 0 else None)\
                    .then_inc(s["mm_units"], 1)
                if m == 0:
                    norm(e)
                n += 1
            pe.wait_ge(s["p_in"], 32 * (l + 1))
            for kt in range(2):
                pe.wait_ge(s["ple_t"], 8 * l + 5 + kt)
                mm = turn(PIN, kt, 2 * kt)
                mm.then_inc(s["p_turned"], 1)
            for m in range(KT_D):
                if m == 0:
                    pe.wait_ge(s["p_feat"], 2 * l + 2)
                    pe.wait_ge(s["p_lo"], 2 * l + 2)
                if m in (2, 3):
                    pe.wait_ge(s["ple_t"], 8 * l + m + 5)
                if m >= 4:
                    pe.wait_ge(s["h_done"], 8 * (e + 1) + m - 3)
                if m % 4 == 0:
                    unit_ready(n)
                mm = products(n % RING, 2, 0, 2, 2 * (m % 4), PH, PL, m0=(m % 4) * P, kw=512)
                if m % 4 == 3:
                    mm.then_inc(s["mm_units"], 1)
                    n += 1
                else:
                    mm.then_inc(s["ple_mm"], 1)

        def turn(src, m, bank):
            for c in range(5):
                rows = P if c < 4 else T_SAMPLE
                mm = pe.transpose(psf[:, bank * 512 + c * P:bank * 512 + c * P + rows],
                                  src[0:rows, c, m * P:(m + 1) * P], ident[0:rows, 0:rows])
            return mm

        pe.wait_ge(s["ident_made"], 1)
        pe.wait_ge(s["dve_const"], 1)
        pe.wait_ge(s["const_dma"], 16 * N_VEC_LOADS)
        pe.transpose(ps[:, 7, 0:VROWS], ROWS, ident[0:VROWS, 0:VROWS]).then_inc(s["vec_turned"], 1)
        pe.wait_ge(s["x_in"], 32)
        for m in range(KT_D):
            if m == 3:
                pe.wait_ge(s["vec_made"], 1)
            if m >= 4:
                pe.wait_ge(s["h_done"], m - 3)
            turn(XIN, m, 2 * (m % 4)).then_inc(s["x_turned"], 1)
        for l in range(2):
            ffn(2 * l)
            for g in range(2):
                gr = GROUPS[2 * l + g]
                features(gr)
                mix(gr)
            out_proj(l)
            ffn(2 * l + 1)
            ple(l)
        norm(8)
        for c in range(5):
            cols = P if c < 4 else T_SAMPLE
            if c == 2:
                pe.wait_ge(s["rstd_done"], 9)
            if c == 4:
                pe.wait_ge(s["y_out_v"], 1)
            for m in range(KT_D):
                if c == 0:
                    pe.wait_ge(s["y_made"], m + 1)
                mm = pe.transpose(psf[0:cols, (2 * (c % 4)) * 512 + m * P:(2 * (c % 4)) * 512 + (m + 1) * P],
                                  YF[:, m, c * P:c * P + cols], ident[:, :])
            mm.then_inc(s["y_turned"], 1)

    @block.scalar
    def _(act):
        def high(base, i, j=0):
            n = base + j
            slot = n % RING
            act.wait_ge(raw_sem[slot], q16(i, n))
            if not isinstance(i, int) or n >= RING:
                act.wait_ge(s["mm_units"], i + (n - RING + 1))
            act.activation(WH[:, slot, :], RAW[:, slot, :], ACT.Copy).then_inc(s["hi_made"], 1)

        def q16(i, n):
            return (i // 4) * 16 + 16 * (n // RING + 1) if isinstance(i, int) else i * 4 + 16 * (n // RING + 1)

        def tile_out(e, m, mc):
            act.wait_ge(s["h_done"], m + (8 * e + 1))
            if not isinstance(m, int) or 8 * e + m >= 2:
                act.wait_ge(s["ssq_added"], m + (8 * e - 1))
            if not isinstance(m, int):
                act.wait_ge(s["pool_const"], 1)
            if e < 8:
                act.activation(flat_of(UH, m), flat_of(H, m), ACT.Copy,
                               scale=gain_of(e, m)).then_inc(s["uh_done"], 1)
            act.activation((tG, tU)[mc % 2][:, :], flat_of(H, m), ACT.Square).then_inc(s["sq_done"], 1)

        def gain_of(e, m):
            return gains[:, e, m:m + 1] if isinstance(m, int) else \
                gains[:, e, bass.ds(m, 1)]

        def norm(e, by_token=False):
            act.wait_ge(s["norm_mm"], e + 1)
            if by_token:
                act.activation(rstdT[:, :], ps[:, 4, 300:305], ACT.Ln, bias=consts[:, 0:1], scale=1.0 / D).then_inc(s["ln_done"], 1)
            act.activation(halves(rstd[:, :]), pair(4), ACT.Ln, bias=consts[:, 0:1], scale=1.0 / D).then_inc(s["ln_done"], 1)
            done = e + 1 + (e > 0) + (e > 4) + (e == 1) * 0
            act.wait_ge(s["ln_done"], done)
            if by_token:
                act.activation(rstdT[:, :], rstdT[:, :], ACT.Exp, scale=-0.5)
            act.activation(rstd[:, :], rstd[:, :], ACT.Exp, scale=-0.5).then_inc(s["rstd_done"], 1)

        def ffn(F):
            base, e = START["ffn", F], 2 * F

            def chunk(i4, f, j, first=False):
                high(base, i4, j + 2)
                high(base, i4, j + 3)
                if first:
                    norm(e)
                act.wait_ge(s["tg_done"], f + (NF * F + 1))
                act.activation(tG[:, :], tG[:, :], ACT.Silu).then_inc(s["silu_done"], 1)
                act.wait_ge(s["hid_mul"], f + (NF * F + 1))
                act.wait_ge(s["pool_const"], 1)
                act.activation(flat_of(HH, f), tU[:, :], ACT.Copy).then_inc(s["hid_hi"], 1)

            chunk(0, 0, 0, True)
            chunk(0, 1, 2)
            with act.Fori(1, NF // 2) as i:
                for c in range(2):
                    chunk(i * 4, i * 2 + c, 2 * c)
            base += UP_UNITS
            with act.Fori(0, 2) as i:
                for m4 in range(4):
                    for u in range(3):
                        high(base, i * 12, 3 * m4 + u + 2)
                    tile_out(e + 1, i * 4 + m4, m4)

        def ahead(n):
            if n + 2 < N_UNITS:
                high(n + 2, 0)

        def features(gr):
            n = gr.start
            for j in range(gr.nfeat):
                ahead(n)
                if j == 0 and gr.g == 0:
                    norm(gr.norm, True)
                n += 1
            if gr.gla:
                gate(gr)
            for kind, j, lv in gr.steps:
                if kind:
                    ahead(n)
                    n += 1
                if not gr.gla and kind == "g" and j == 1:
                    gate(gr)
                if not gr.gla and kind == "g" and j == 3:
                    gate_end(gr)
                if lv not in (None, "diag"):
                    level(gr, lv)
                if kind == "v" and j == 3:
                    act.wait_ge(s["mm_units"], n)
                    act.wait_ge(s["rstd_done"], gr.norm + 1)
                    for c in range(5):
                        act.activation(V[:, c, :], ps[:, V_BANKS[c], :], ACT.Copy, scale=rstdT[:, c:c + 1]).then_inc(s["v_out"], 1)

        def level(gr, l):
            gi, gs = gr.gi, gr.gate_scale
            n, L = LEVELS * gi + l, 1 << l
            both = l < 2
            _, g2, _ = blocks(G, gr, L, both)
            act.wait_ge(s["gate_made"], (LEVELS + 1) * gi + l + 1)
            if l:
                act.wait_ge(s["qt_made"], n)
            act.activation(compact(EX[:, 2 * T:4 * T], gr, L, both), g2, ACT.Exp, scale=gs).then_inc(s["eq_made"], 1)
            act.wait_ge(s["diff_made"], n + 1)
            dk = compact(EX[:, 0:2 * T], gr, L, both)
            act.activation(dk, dk, ACT.Exp, scale=gs).then_inc(s["ek_made"], 1)

        def gate(gr):
            if gr.gla:
                act.wait_ge(s["x_made"], gr.gi + 1)
                log_sigmoid_tail(gr, G[:, 0:2, :].rearrange("p h t -> p (h t)"))
                return
            k = gr.gi - 1
            ex = EX[:, :]
            kk = K[:].rearrange("p h t -> p (h t)")
            act.wait_ge(s["feat_out"], gr.feat0 + gr.nfeat)
            act.activation(Q[:], Q[:], ACT.Silu).then_inc(s["q_made"], 1)
            log_sigmoid_tail(gr, kk)

        def gate_end(gr):
            k = gr.gi - 1
            ex = EX[:, :]
            kk = K[:].rearrange("p h t -> p (h t)")
            act.wait_ge(s["kx_made"], k)
            act.activation(kk, kk, ACT.Exp).then_inc(s["k_made"], 1)
            act.wait_ge(s["gd_made"], k)
            act.activation(ex, ex, ACT.Abs).then_inc(s["gd_abs"], 1)
            act.wait_ge(s["gd_abs"], k)
            act.activation(ex, ex, ACT.Exp, scale=-1.0).then_inc(s["gd_exp"], 1)
            act.wait_ge(s["gd_exp"], k)
            act.activation(ex, ex, ACT.Ln, bias=consts[:, 1:2]).then_inc(s["gd_ln"], 1)

        def log_sigmoid_tail(gr, x):
            k = gr.gi + 1
            ex = EX[:, 0:gr.NH * T]
            if gr.gi:
                act.wait_ge(s["out_state"], 16 * N_STATE[gr.gi])
            act.activation(ex, x, ACT.Abs).then_inc(s["gate_abs"], 1)
            act.wait_ge(s["gate_abs"], k)
            act.activation(ex, ex, ACT.Exp, scale=-1.0).then_inc(s["gate_exp"], 1)
            act.wait_ge(s["gate_exp"], k)
            act.activation(ex, ex, ACT.Ln, bias=consts[:, 1:2]).then_inc(s["gate_ln"], 1)

        def mix(gr):
            gi, NH = gr.gi, gr.NH
            gs = gr.gate_scale
            act.wait_ge(s["gate_made"], (LEVELS + 1) * (gi + 1))
            act.wait_ge(s["lvl_mm"], LEVELS * (gi + 1) - 1)
            gf = G[:, 0:NH, :].rearrange("p h t -> p (h t)")
            act.activation(EP[:, 0:NH * T], gf, ACT.Exp, scale=gs).then_inc(s["chunk_exp"], 1)
            act.wait_ge(s["ksuf_made"], 2 * gi + 2)
            act.activation(EX[:, 0:NH * T], EX[:, 0:NH * T], ACT.Exp, scale=gs).then_inc(s["ksuf_exp"], 1)
            ends = G[:, 0:NH, 0:T_PROMPT].rearrange("p h (c t) -> p h c t", t=CHUNK)[:, :, :, CHUNK - 1]
            act.activation(DEC[:, 0:NH, :], ends, ACT.Exp, scale=gs).then_inc(s["dec_made"], 1)
            ends = G[:, 0:NH, T_PROMPT:T].rearrange("p h (c t) -> p h c t", t=T_SEQ)[:, :, :, T_SEQ - 1]
            act.activation(DECS[:, 0:NH, :], ends, ACT.Exp, scale=gs).then_inc(s["dec_made"], 1)
            act.wait_ge(s["feat_out"], gr.feat0 + gr.nfeat + 4)
            act.activation(OG[:, 4 * gr.g:4 * gr.g + 4, :], OG[:, 4 * gr.g:4 * gr.g + 4, :], ACT.Silu).then_inc(s["og_silu"], 1)
            act.wait_ge(s["kd_turned"], gi + 1)
            act.activation(KD[:, 0:NH * NCH, :].rearrange("p x k -> p (x k)"), psf[:, 0:NH * NCH * P], ACT.Copy).then_inc(s["kd_out"], 1)
            act.wait_ge(s["kds_turned"], gi + 1)
            act.wait_ge(s["dec_made"], 2 * gi + 2)

            def kmask(b):
                if b >= KM_BUFS:
                    act.wait_ge(s["us_mm"], N_SEQ * gi + b - KM_BUFS + 1)
                act.activation(KM(b)[:, 0:NH * P], ps[:, 1, 0:NH * P], ACT.Copy, scale=seqmask[:, b:b + 1])\
                   .then_inc(s["kmask_made"], 1)

            for b in range(KM_BUFS):
                kmask(b)
            for j in range(4):
                act.wait_ge(s["o_out"], 5 * gi + j + 2)
                act.activation(K[:, j, :], Q[:, j, :], ACT.Square).then_inc(s["osq_made"], 1)
            for b in range(KM_BUFS, N_SEQ):
                kmask(b)
            if gr.g == 1:
                out_high(gr.layer, range(4))
            act.wait_ge(s["var_mm"], gi + 1)
            act.activation(ORS[:, 0:NH, 0:T_PROMPT], ps[:, 4:4 + NH, :], ACT.Ln, bias=consts[:, 0:1], scale=1.0 / gr.V)\
               .then_inc(s["var_ln"], 1)
            act.activation(ORS[:, 0:NH, T_PROMPT:T], ps[:, 0, 0:NH * T_SAMPLE].rearrange("p (h t) -> p h t", h=NH),
                           ACT.Ln, bias=consts[:, 0:1], scale=1.0 / gr.V).then_inc(s["var_ln"], 1)
            act.wait_ge(s["var_ln"], 2 * gi + 2)
            for h in range(NH):
                act.activation(ORS[:, h, :], ORS[:, h, :], ACT.Exp, scale=-0.5).then_inc(s["ors_made"], 1)

        def out_high(l, tiles):
            for kk in tiles:
                if kk == 0:
                    act.wait_ge(s["og_pre"], 8 * l + 8)
                    act.wait_ge(s["osq_made"], 8 * l + 8)
                act.wait_ge(s["og_made"], 8 * l + kk + 1)
                act.activation(OH[:, kk, :], OG[:, kk, :], ACT.Copy).then_inc(s["out_hi"], 1)

        def out_proj(l):
            e = 4 * l + 2
            out_high(l, range(4, KT_D))
            for m in range(KT_D):
                ahead(START["out", l] + m)
                tile_out(e, m, m)

        def ple(l):
            e = 4 * l + 3
            for m in range(KT_D):
                ahead(START["ple", l] + m)
                if m == 0:
                    norm(e)
                act.wait_ge(s["ple_t"], 8 * l + m + 1)
                act.activation(GT[:, m, :], GT[:, m, :], ACT.Sigmoid).then_inc(s["ple_sig"], 1)
            for kt in range(2):
                act.wait_ge(s["p_feat"], 2 * l + kt + 1)
                act.activation(PH[:, kt, :], PT[:, kt, :], ACT.Copy).then_inc(s["p_hi"], 1)
            for m in range(KT_D):
                if m % 4 == 3:
                    ahead(START["ple", l] + 8 + m // 4)
                tile_out(e + 1, m, m)

        rows = 0
        for src in [a[nm][l] for l in range(2) for nm in ("ffn1_norm", "mix_norm", "ffn2_norm", "ple_norm")] + \
                [a["final_norm"], a["gla_gn"][0], a["hgrn_gn"][0], a["gla_b_gk"][0]] + \
                [a["hgrn_lower_bounds"][l] for l in range(2)]:
            k = src.shape[0] // P
            act.dma_start(ROWS[rows:rows + k, :], src.rearrange("(m p) -> m p", p=P)).then_inc(s["const_dma"], 16)
            rows += k
        act.wait_ge(s["pool_const"], 1)
        high(0, 0)
        high(1, 0)
        act.wait_ge(s["lb_a"], 1)
        act.activation(lbd[:, 1, :], lbd[:, 0, :], ACT.Abs).then_inc(s["lb_b"], 1)
        act.wait_ge(s["lb_b"], 1)
        act.activation(lbd[:, 2, :], lbd[:, 1, :], ACT.Exp, scale=-1.0).then_inc(s["lb_b"], 1)
        act.wait_ge(s["lb_b"], 2)
        act.activation(lbd[:, 5, :], lbd[:, 2, :], ACT.Ln, bias=consts[:, 1:2]).then_inc(s["lb_c"], 1)
        for m in range(KT_D):
            tile_out(0, m, m)
        for l in range(2):
            ffn(2 * l)
            for g in range(2):
                features(GROUPS[2 * l + g])
                mix(GROUPS[2 * l + g])
            out_proj(l)
            ffn(2 * l + 1)
            ple(l)
        norm(8)
        for c in range(1, 5, 2):
            rows = P if c < 4 else T_SAMPLE
            act.wait_ge(s["y_turned"], c + 1)
            act.activation(YT[0:rows, c, :], psf[0:rows, 2 * (c % 4) * 512:2 * (c % 4) * 512 + D], ACT.Copy).then_inc(s["y_out_a"], 1)


    @block.vector
    def _(dve):
        def low(base, i, j=0):
            n = base + j
            slot = n % RING
            dve.wait_ge(s["hi_made"], i + (n + 1))
            dve.tensor_tensor(WL[:, slot, :], RAW[:, slot, :], WH[:, slot, :].bitcast(F32), ALU.subtract)\
               .then_inc(s["lo_made"], 1)

        def ahead(n):
            if n + 2 < N_UNITS:
                low(n + 2, 0)

        def tile_low(e, m):
            if e == 8:
                return
            dve.wait_ge(s["uh_done"], m + (8 * e + 1))
            sc = gains[:, e, m:m + 1] if isinstance(m, int) else gains[:, e, bass.ds(m, 1)]
            dve.scalar_tensor_tensor(out=flat_of(UL, m), in0=flat_of(H, m), scalar=sc,
                                     in1=flat_of(UH, m).bitcast(F32), op0=ALU.mult, op1=ALU.subtract)\
               .then_inc(s["u_done"], 1)

        def ffn(F):
            base, e = START["ffn", F], 2 * F

            def chunk(i4, f, j):
                bank = 2 * j
                if not isinstance(f, int) or NF * F + f > 0:
                    dve.wait_ge(s["hid_done"], f + NF * F)
                low(base, i4, j + 2)
                low(base, i4, j + 3)
                dve.wait_ge(s["mm_units"], i4 + (base + j + 2))
                dve.wait_ge(s["rstd_done"], e + 1)
                dve.tensor_tensor(halves(tG[:, :]), pair(bank), halves(rstd[:, :]), ALU.mult).then_inc(s["tg_done"], 1)
                dve.tensor_tensor(halves(tU[:, :]), pair(bank + 2), halves(rstd[:, :]), ALU.mult).then_inc(s["up_evicted"], 1)
                dve.wait_ge(s["hid_hi"], f + (NF * F + 1))
                dve.tensor_tensor(flat_of(HL, f), tU[:, :], flat_of(HH, f).bitcast(F32), ALU.subtract)\
                   .then_inc(s["hid_done"], 1)

            for c in range(2):
                chunk(0, c, 2 * c)
            with dve.Fori(1, NF // 2) as i:
                for c in range(2):
                    chunk(i * 4, i * 2 + c, 2 * c)
            base += UP_UNITS
            with dve.Fori(0, 2) as i:
                for m4 in range(4):
                    for u in range(3):
                        low(base, i * 12, 3 * m4 + u + 2)
                    m = i * 4 + m4
                    dve.wait_ge(s["mm_units"], i * 12 + (base + 3 * m4 + 3))
                    dve.scalar_tensor_tensor(out=tile_of(H, m), in0=pair(2 * m4), scalar=0.5, in1=tile_of(H, m),
                                             op0=ALU.mult, op1=ALU.add).then_inc(s["h_done"], 1)
                    tile_low(e + 1, m)

        def feature_out(gr, j, n, dst, scale=None):
            dve.wait_ge(s["mm_units"], n + 1)
            dve.wait_ge(s["rstd_done"], gr.norm + 1)
            src = pair(gr.feat_bank(j))
            if scale is None:
                dve.tensor_tensor(halves(dst), src, halves(rstd[:, :]), ALU.mult).then_inc(s["feat_out"], 1)
            else:
                dve.scalar_tensor_tensor(out=halves(dst), in0=src, scalar=scale, in1=halves(rstd[:, :]),
                                         op0=ALU.mult, op1=ALU.mult).then_inc(s["feat_out"], 1)

        def features(gr):
            n = gr.start
            dests = ([(RT, None)] if gr.has_r else []) + \
                [(Q[:, h, :], gr.q_scale if gr.gla else None) for h in range(gr.NH)] + \
                [(K[:, h, :], None) for h in range(gr.NH)]
            for j, (dst, scale) in enumerate(dests):
                ahead(n)
                feature_out(gr, j, n, dst, scale)
                n += 1
            if gr.gi == 1:
                dve.tensor_copy(G[:, 0:2, :], OG[:, 6:8, :]).then_inc(s["x_made"], 1)
                dve.wait_ge(s["x_made"], 2)
            if gr.gla:
                gate(gr)
            for kind, j, lv in gr.steps:
                if kind:
                    ahead(n)
                    n += 1
                if lv == "diag":
                    if kind == "g":
                        feature_out(gr, gr.nfeat + j, n - 1, OG[:, 4 * gr.g + j, :])
                    if not gr.gla:
                        gate_end(gr)
                    diagonal(gr)
                    continue
                if not gr.gla and kind == "g" and j < 2:
                    if j == 1:
                        feature_out(gr, gr.nfeat, n - 2, OG[:, 4 * gr.g, :])
                        gate(gr)
                        feature_out(gr, gr.nfeat + 1, n - 1, OG[:, 4 * gr.g + 1, :])
                    continue
                if lv is not None:
                    level(gr, lv)
                if kind == "g":
                    feature_out(gr, gr.nfeat + j, n - 1, OG[:, 4 * gr.g + j, :])

        def diagonal(gr):
            dve.wait_ge(s["diag_mm"], gr.gi + 1)
            X = gr.NH * NCH
            dve.tensor_tensor(AT[:, 0:X, :], psf[:, 2048:2048 + X * P].rearrange("p (x n) -> p x n", x=X),
                              ident[:, :].rearrange("p (o n) -> p o n", o=1).to_broadcast([P, X, P]),
                              ALU.mult).then_inc(s["diag_out"], 1)

        def level_out(gr, l):
            gi, NH = gr.gi, gr.NH
            n, L = LEVELS * gi + l, 1 << l
            b0 = gr.level_bank(l)
            dve.wait_ge(s["lvl_mm"], n + 1)
            if l == 0:
                dve.tensor_tensor(ATS[:, 0:NH, :], ps[:, 6, 0:NH * 32].rearrange("p (x n) -> p x n", x=NH),
                                  ident[:, SROW:P].rearrange("p (o n) -> p o n", o=1).to_broadcast([P, NH, 32]),
                                  ALU.mult).then_inc(s["sdiag_out"], 1)
                dve.wait_ge(s["diag_out"], gi + 1)
                dve.wait_ge(s["sdiag_out"], gi + 1)
            else:
                dve.wait_ge(s["lvl_out"], n)
            if l == 1:
                dve.wait_ge(s["slvl_out"], 2 * gi + 1)
            X = NH * NCH
            dst = AT[:, 0:X, :].rearrange("p x (n l) -> p x n l", l=2 * L)[:, :, :, L:2 * L]
            data = psf[:, 512 * b0:512 * b0 + 64 * X].rearrange("p (x n l) -> p x n l", x=X, l=L)
            msk = masks[:, l, :].bitcast(U32).rearrange("p (o n l) -> p o n l", o=1, l=L).to_broadcast([P, X, 64 // L, L])
            dve.copy_predicated(dst, msk, data).then_inc(s["lvl_out"], 1)
            if l < 2:
                dst = ATS[:, 0:NH, :].rearrange("p x (n l) -> p x n l", l=2 * L)[:, :, :, L:2 * L]
                data = ps[:, 6, (8 + 4 * l) * 16:(8 + 4 * l + NH) * 16].rearrange("p (x n l) -> p x n l", x=NH, l=L)
                msk = masks[:, l, 48:64].bitcast(U32).rearrange("p (o n l) -> p o n l", o=1, l=L)\
                    .to_broadcast([P, NH, 16 // L, L])
                dve.copy_predicated(dst, msk, data).then_inc(s["slvl_out"], 1)

        def level(gr, l):
            gi, NH = gr.gi, gr.NH
            n, L = LEVELS * gi + l, 1 << l
            both = l < 2
            g1, g2, tot = blocks(G, gr, L, both)
            dk = compact(EX[:, 0:2 * T], gr, L, both)
            dve.wait_ge(s["gate_made"], (LEVELS + 1) * gi + l + 1)
            dve.tensor_tensor(dk, tot.to_broadcast(g1.shape), g1, ALU.subtract).then_inc(s["diff_made"], 1)
            dve.wait_ge(s["eq_made"], n + 1)
            if l == 0:
                dve.wait_ge(s["kt_zero"], gi + 1)
                if not gr.gla:
                    dve.wait_ge(s["k_made"], gi - 1)
            dve.wait_ge(s["diff_made"], n + 1)
            dve.tensor_tensor(g2, g2, tot.to_broadcast(g2.shape), ALU.add).then_inc(s["gate_made"], 1)
            dve.wait_ge(s["ek_made"], n + 1)
            k1, _, _ = blocks(K, gr, L, both)
            kt = KTb[:, l % 2, 0:NH * T].rearrange("p (h t) -> p h t", t=T)
            kt1, _, _ = blocks(kt, gr, L, both)
            dve.tensor_tensor(kt1, k1, dk, ALU.mult).then_inc(s["kt_made"], 1)
            dve.wait_ge(s["kt_made"], n + 1)
            if l:
                level_out(gr, l - 1)

        def gate(gr):
            gi = gr.gi
            if gr.has_r:
                dve.wait_ge(s["gk_mm"], 1)
                for h in range(4):
                    dst = G[:, h, :] if h < 2 else OG[:, 4 + h, :]
                    ins = dve.tensor_scalar(halves(dst), pair(2 * h), bgk[:, h:h + 1], None, ALU.add)
                ins.then_inc(s["x_made"], 1)
            if gr.gla:
                dve.wait_ge(s["gate_ln"], gi + 1)
                gf = G[:, 0:2, :].rearrange("p h t -> p (h t)")
                dve.scalar_tensor_tensor(out=gf, in0=gf, scalar=0.0, in1=EX[:, 0:2 * T], op0=ALU.min, op1=ALU.subtract)\
                   .then_inc(s["gate_made"], 1)
                return
            k = gr.gi - 1
            gf = G[:].rearrange("p h t -> p (h t)")
            kf = K[:].rearrange("p h t -> p (h t)")
            dve.wait_ge(s["gate_ln"], gr.gi + 1)
            dve.scalar_tensor_tensor(out=gf, in0=kf, scalar=0.0, in1=EX[:, :], op0=ALU.min, op1=ALU.subtract)\
               .then_inc(s["ls_made"], 1)
            dve.wait_ge(s["ls_made"], k)
            for h in range(4):
                ins = dve.tensor_scalar(G[:, h, :], G[:, h, :], L1M[:, gr.h0 + h:gr.h0 + h + 1], None, ALU.add)
            ins.then_inc(s["c_made"], 1)
            dve.wait_ge(s["c_made"], k)
            dve.tensor_tensor(kf, gf, kf, ALU.subtract).then_inc(s["kx_made"], 1)
            for h in range(4):
                ins = dve.tensor_scalar(EX[:, h * T:(h + 1) * T], G[:, h, :], LLB[:, gr.h0 + h:gr.h0 + h + 1], None, ALU.subtract)
            ins.then_inc(s["gd_made"], 1)

        def gate_end(gr):
            k = gr.gi - 1
            dve.wait_ge(s["gd_ln"], k)
            for h in range(4):
                ins = dve.scalar_tensor_tensor(out=G[:, h, :], in0=G[:, h, :], scalar=LLB[:, gr.h0 + h:gr.h0 + h + 1],
                                               in1=EX[:, h * T:(h + 1) * T], op0=ALU.max, op1=ALU.add)
            ins.then_inc(s["gate_made"], 1)

        def mix(gr):
            gi, NH = gr.gi, gr.NH
            dve.wait_ge(s["qt_made"], LEVELS * (gi + 1))
            dve.wait_ge(s["gate_made"], (LEVELS + 1) * (gi + 1))
            ex3 = EX[:, 0:NH * T].rearrange("p (h t) -> p h t", t=T)
            for t0, t1, L in ((0, T_PROMPT, CHUNK), (T_PROMPT, T, T_SEQ)):
                g4 = G[:, 0:NH, t0:t1].rearrange("p h (n l) -> p h n l", l=L)
                e4 = ex3[:, :, t0:t1].rearrange("p h (n l) -> p h n l", l=L)
                dve.tensor_tensor(e4, g4[:, :, :, L - 1:L].to_broadcast(g4.shape), g4, ALU.subtract).then_inc(s["ksuf_made"], 1)
            dve.wait_ge(s["ksuf_exp"], gi + 1)
            dve.tensor_tensor(K[:, 0:NH, :], K[:, 0:NH, :], ex3, ALU.mult).then_inc(s["kdec_made"], 1)
            dve.wait_ge(s["chunk_exp"], gi + 1)
            dve.tensor_tensor(Q[:, 0:NH, :], Q[:, 0:NH, :], EP[:, 0:NH * T].rearrange("p (h t) -> p h t", t=T), ALU.mult)\
               .then_inc(s["qin_made"], 1)
            level_out(gr, LEVELS - 1)
            dve.wait_ge(s["qin_made"], gi + 1)
            dve.wait_ge(s["dec_made"], 2 * gi + 2)
            dve.wait_ge(s["u_mm"], 4 * gi + 1)
            dve.tensor_copy(ST[:, 0, :], ps[:, 0, :]).then_inc(s["s_made"], 1)
            for c in range(1, NCH):
                dve.wait_ge(s["u_mm"], 4 * gi + c + 1)
                dve.wait_ge(s["s_made"], 4 * gi + c)
                for h in range(NH):
                    hv = slice(h * gr.V, (h + 1) * gr.V)
                    ins = dve.scalar_tensor_tensor(out=ST[:, c, hv], in0=ST[:, c - 1, hv], scalar=DEC[:, h, c:c + 1],
                                                   in1=ps[:, c, hv], op0=ALU.mult, op1=ALU.add)
                ins.then_inc(s["s_made"], 1)

            dve.wait_ge(s["os_mm"], gi + 1)
            dve.tensor_copy(Q[:, :, T_PROMPT:T], ps[:, 0, 0:P].rearrange("p (j t) -> p j t", j=4)).then_inc(s["o_out"], 1)
            for j in range(4):
                dve.wait_ge(s["o_mm"], 4 * gi + max(j, min(3, (j + 1) * gr.vt_per_head - 1)) + 1)
                dve.tensor_copy(Q[:, j, 0:T_PROMPT], ps[:, 4 + j, :]).then_inc(s["o_out"], 1)

            def sequence(b):
                dve.wait_ge(s["us_mm"], N_SEQ * gi + b + 1)
                for h in range(NH):
                    hv = slice(h * gr.V, (h + 1) * gr.V)
                    ins = dve.scalar_tensor_tensor(out=S0[:, b, hv], in0=S0[:, b, hv], scalar=DECS[:, h, b:b + 1],
                                                   in1=ps[:, 2 + b % 2, hv], op0=ALU.mult, op1=ALU.add)
                ins.then_inc(s["snew_made"], 1)

            dve.wait_ge(s["og_silu"], gi + 1)
            for j in range(4):
                col = j % 2 if gr.gla else 2
                og = OG[:, 4 * gr.g + j, :]
                dve.wait_ge(s["o_out"], 5 * gi + j + 2)
                dve.scalar_tensor_tensor(out=og, in0=og, scalar=gn[:, col:col + 1], in1=Q[:, j, :],
                                         op0=ALU.mult, op1=ALU.mult).then_inc(s["og_pre"], 1)
            for b in range(N_SEQ - 2):
                sequence(b)
            for j in range(4):
                og = OG[:, 4 * gr.g + j, :]
                dve.wait_ge(s["og_pre"], 4 * gi + j + 1)
                dve.wait_ge(s["ors_made"], N_HEADS[gi] + j // gr.vt_per_head + 1)
                dve.tensor_tensor(og, og, ORS[:, j // gr.vt_per_head, :], ALU.mult).then_inc(s["og_made"], 1)
                if gr.g == 1 and j % 2:
                    dve.wait_ge(s["us_mm"], N_SEQ * (gi + 1))
                    out_low(gr.layer, (j - 1, j))
            for b in range(N_SEQ - 2, N_SEQ):
                sequence(b)
            dve.wait_ge(s["og_made"], 4 * gi + 4)

        def out_low(l, tiles):
            for kk in tiles:
                dve.wait_ge(s["out_hi"], 8 * l + kk + 1)
                dve.tensor_tensor(OL[:, kk, :], OG[:, kk, :], OH[:, kk, :].bitcast(F32), ALU.subtract).then_inc(s["out_lo"], 1)

        def out_proj(l):
            e = 4 * l + 2
            out_low(l, range(4, KT_D))
            for m in range(KT_D):
                ahead(START["out", l] + m)
                dve.wait_ge(s["mm_units"], START["out", l] + m + 1)
                dve.tensor_tensor(tile_of(H, m), pair(2 * (m % 4)), tile_of(H, m), ALU.add).then_inc(s["h_done"], 1)
                tile_low(e, m)

        def ple(l):
            e, n = 4 * l + 3, START["ple", l]
            for m in range(KT_D):
                ahead(n + m)
                dve.wait_ge(s["mm_units"], n + m + 1)
                dve.wait_ge(s["rstd_done"], e + 1)
                dve.tensor_tensor(halves(GT[:, m, :]), pair(2 * (m % 4)), halves(rstd[:, :]), ALU.mult).then_inc(s["ple_t"], 1)
            for kt in range(2):
                dve.wait_ge(s["p_turned"], 2 * l + kt + 1)
                dve.tensor_copy(PT[:, kt, :], psf[:, 1024 * kt:1024 * kt + T]).then_inc(s["p_feat"], 1)
            for kt in range(2):
                dve.wait_ge(s["p_hi"], 2 * l + kt + 1)
                dve.tensor_tensor(PL[:, kt, :], PT[:, kt, :], PH[:, kt, :].bitcast(F32), ALU.subtract).then_inc(s["p_lo"], 1)
            for m in range(KT_D):
                if m % 4 == 3:
                    ahead(n + 8 + m // 4)
                    dve.wait_ge(s["mm_units"], n + 8 + m // 4 + 1)
                else:
                    dve.wait_ge(s["ple_mm"], 6 * l + 3 * (m // 4) + m % 4 + 1)
                dve.wait_ge(s["ple_sig"], 8 * l + m + 1)
                dve.tensor_tensor(halves(GT[:, m, :]), pair(2 * (m % 4)), halves(GT[:, m, :]), ALU.mult).then_inc(s["ple_x"], 1)
                dve.wait_ge(s["ple_x"], 8 * l + m + 1)
                dve.tensor_tensor(H[:, m, :], H[:, m, :], GT[:, m, :], ALU.add).then_inc(s["h_done"], 1)
                tile_low(e + 1, m)

        dve.memset(ones[:, :], 1.0).then_inc(s["dve_const"], 1)
        dve.wait_ge(s["vec_turned"], 1)
        dve.tensor_copy(vecs[:, :], ps[:, 7, 0:VROWS]).then_inc(s["vec_made"], 1)
        low(0, 0)
        low(1, 0)
        dve.wait_ge(s["vec_made"], 1)
        dve.tensor_tensor(lbd[:, 0, :], lbr[:, 0, :], lbr[:, 1, :], ALU.subtract).then_inc(s["lb_a"], 1)
        dve.wait_ge(s["lb_a"], 1)
        dve.tensor_scalar(lbd[:, 4, :], lbd[:, 0, :], -1.0, None, ALU.mult).then_inc(s["lb_a"], 1)
        dve.wait_ge(s["lb_a"], 2)
        dve.wait_ge(s["lb_c"], 1)
        dve.scalar_tensor_tensor(out=LLB, in0=lbd[:, 4, :], scalar=0.0, in1=lbd[:, 5, :], op0=ALU.min, op1=ALU.subtract)\
           .then_inc(s["lb_done"], 1)
        dve.scalar_tensor_tensor(out=L1M, in0=lbd[:, 0, :], scalar=0.0, in1=lbd[:, 5, :], op0=ALU.min, op1=ALU.subtract)\
           .then_inc(s["lb_done"], 1)
        dve.wait_ge(s["lb_done"], 2)
        for m in range(KT_D):
            dve.wait_ge(s["x_turned"], m + 1)
            dve.tensor_copy(H[:, m, :], psf[:, 1024 * (m % 4):1024 * (m % 4) + T]).then_inc(s["h_done"], 1)
            dve.wait_ge(s["h_done"], m + 1)
            tile_low(0, m)
        for l in range(2):
            ffn(2 * l)
            for g in range(2):
                features(GROUPS[2 * l + g])
                mix(GROUPS[2 * l + g])
            out_proj(l)
            ffn(2 * l + 1)
            ple(l)
        dve.wait_ge(s["rstd_done"], 9)
        for m in range(KT_D):
            dve.scalar_tensor_tensor(out=YF[:, m, :], in0=H[:, m, :], scalar=gains[:, 8, m:m + 1], in1=rstd[:, :],
                                     op0=ALU.mult, op1=ALU.mult).then_inc(s["y_made"], 1)
        for c in (0, 2, 4):
            rows = P if c < 4 else T_SAMPLE
            dve.wait_ge(s["y_turned"], c + 1)
            dve.tensor_copy(YT[0:rows, c, :], psf[0:rows, 1024 * (c % 4):1024 * (c % 4) + D]).then_inc(s["y_out_v"], 1)

    @block.gpsimd
    def _(pool):
        def square_in(e, m, mc, first):
            pool.wait_ge(s["sq_done"], m + (8 * e + 1))
            if first:
                pool.tensor_copy(ssq[:, :], (tG, tU)[mc % 2][:, :]).then_inc(s["ssq_added"], 1)
            else:
                pool.wait_ge(s["ssq_added"], m + 8 * e)
                pool.tensor_tensor(ssq[:, :], ssq[:, :], (tG, tU)[mc % 2][:, :], ALU.add).then_inc(s["ssq_added"], 1)

        def squares(e):
            for m in range(KT_D):
                square_in(e, m, m, m == 0)

        def ffn(F):
            with pool.Fori(0, NF) as f:
                pool.wait_ge(s["silu_done"], f + (NF * F + 1))
                pool.wait_ge(s["up_evicted"], f + (NF * F + 1))
                pool.tensor_tensor(tU[:, :], tG[:, :], tU[:, :], ALU.mult).then_inc(s["hid_mul"], 1)
            squares(2 * F + 1)

        def mix(gr):
            gi, NH = gr.gi, gr.NH
            if gr.g == 0:
                pool.wait_ge(s["h_done"], 8 * gr.norm + 8)
            pool.memset(KTb[:], 0.0).then_inc(s["kt_zero"], 1)
            if gr.has_r:
                pool.wait_ge(s["kt_zero"], 1)
                pool.dma_start(KTb[P - 16:P, 1, 0:512], a["gla_w_gk_up"][0]).then_inc(s["w_gkup_in"], 16)
            for l in range(LEVELS):
                n, L = LEVELS * gi + l, 1 << l
                both = l < 2
                pool.wait_ge(s["eq_made"], n + 1)
                if l >= 2:
                    pool.wait_ge(s["lvl_mm"], n - 1)
                if l == 0:
                    pool.wait_ge(s["feat_out"], gr.feat0 + gr.nfeat)
                    if not gr.gla:
                        pool.wait_ge(s["q_made"], gi - 1)
                _, q2, _ = blocks(Q, gr, L, both)
                pool.tensor_tensor(compact(QTb[:, l % 2, :], gr, L, both), q2, compact(EX[:, 2 * T:4 * T], gr, L, both),
                                   ALU.mult).then_inc(s["qt_made"], 1)
            pool.wait_ge(s["out_state"], 16 * N_STATE[gi + 1])

        pool.memset(ident[:, :], 0.0).then_inc(s["pc"], 1)
        pool.memset(masks[:], 1.0).then_inc(s["pc"], 1)
        pool.memset(seqmask[:, :], 1.0).then_inc(s["pc"], 1)
        pool.memset(consts[:, 0:1], EPS).then_inc(s["pc"], 1)
        pool.memset(consts[:, 1:2], 1.0).then_inc(s["pool_const"], 1)
        pool.wait_ge(s["pc"], 4)
        pool.affine_select(out=ident[:, :], in_=ident[:, :], compare_op=ALU.not_equal, fill=1.0, base=0,
                           pattern=[[-1, P]], channel_multiplier=1).then_inc(s["ident_made"], 1)
        for l in range(LEVELS):
            L = 1 << l
            mv = masks[:, l, :].rearrange("p (n l) -> p n l", l=L)
            pool.affine_select(out=mv, in_=mv, compare_op=ALU.is_ge, fill=0.0, base=0,
                               pattern=[[-2 * L, 64 // L], [0, L]], channel_multiplier=1).then_inc(s["pc"], 1)
            pool.wait_ge(s["pc"], 5 + 2 * l)
            pool.affine_select(out=mv, in_=mv, compare_op=ALU.is_ge, fill=0.0, base=L - 1,
                               pattern=[[2 * L, 64 // L], [0, L]], channel_multiplier=-1).then_inc(s["pc"], 1)
            pool.wait_ge(s["pc"], 6 + 2 * l)
        pool.affine_select(out=seqmask[:, :], in_=seqmask[:, :], compare_op=ALU.is_ge, fill=0.0, base=-SROW,
                           pattern=[[-T_SEQ, N_SEQ]], channel_multiplier=1).then_inc(s["pc"], 1)
        pool.wait_ge(s["pc"], 5 + 2 * LEVELS)
        pool.affine_select(out=seqmask[:, :], in_=seqmask[:, :], compare_op=ALU.is_ge, fill=0.0, base=SROW + T_SEQ - 1,
                           pattern=[[T_SEQ, N_SEQ]], channel_multiplier=-1).then_inc(s["masks_made"], 1)
        squares(0)
        for l in range(2):
            ffn(2 * l)
            for g in range(2):
                mix(GROUPS[2 * l + g])
            squares(4 * l + 2)
            ffn(2 * l + 1)
            squares(4 * l + 4)


_INS = ["x_prompt", "x_sample", "state_gla", "state_hgrn", "p_prompt", "p_sample", "ffn1_norm", "ffn1_w_gu",
        "ffn1_w_down", "mix_norm", "gla_w_in", "gla_w_gk_up", "gla_b_gk", "gla_gn", "gla_w_out", "hgrn_w_in",
        "hgrn_gn", "hgrn_w_out", "hgrn_lower_bounds", "ffn2_norm", "ffn2_w_gu", "ffn2_w_down", "ple_norm",
        "ple_w_gate", "ple_w_proj", "final_norm"]
_OUTS = [("y_p", (1, T_PROMPT, D)), ("y_s", (N_SEQ, T_SEQ, D)), ("gla_p", (1, 1, 4, 128, 256)),
         ("gla_s", (1, N_SEQ, 4, 128, 256)), ("hgrn_p", (1, 1, 8, 128, 128)), ("hgrn_s", (1, N_SEQ, 8, 128, 128))]


def kernel(**inputs):
    import numpy as _np
    import concourse.bacc as _bacc
    from concourse import mybir as _mybir
    from concourse.bass_utils import run_bass_kernel_spmd as _run

    nc = _bacc.Bacc("TRN2", target_bir_lowering=False, num_devices=1)
    arrays, a, o = {}, {}, {}
    for name in _INS:
        x = _np.ascontiguousarray(inputs[name])
        arrays[f"in_{name}_dram"] = x
        a[name] = nc.dram_tensor(f"in_{name}_dram", x.shape, _mybir.dt.from_np(x.dtype), kind="ExternalInput").ap()
    for name, shape in _OUTS:
        o[name] = nc.dram_tensor(f"out_{name}_dram", shape, _mybir.dt.float32, kind="ExternalOutput").ap()
    build(nc, a, o)
    r = _run(nc, [arrays], core_ids=[0])
    return tuple(r.results[0][f"out_{name}_dram"] for name, _ in _OUTS)
```

```python
from contextlib import ExitStack

import concourse.bass as bass
from concourse import mybir

ALU = mybir.AluOpType
ACT = mybir.ActivationFunctionType
F32 = mybir.dt.float32
F32R = mybir.dt.float32r
U32 = mybir.dt.uint32

P = 128
D = 1024
KT_D = D // P
T_PROMPT = 512
N_SEQ, T_SEQ = 8, 4
T_SAMPLE = N_SEQ * T_SEQ
T = T_PROMPT + T_SAMPLE
HALF = T // 2
F_FF = 2816
NF = F_FF // P
PLE = 256
EPS = 1e-6

RING = 4
UNIT = 1024
ROW_GN = 9 * KT_D
ROW_BGK = ROW_GN + 3
ROW_LB = ROW_BGK + 4
VROWS = ROW_LB + 2 * KT_D
N_VEC_LOADS = 9
N_LN = 12
DOWN_KT = [(0, 8), (8, 16), (16, 22)]
UP_UNITS = 2 * NF
DOWN_UNITS = 3 * KT_D
FFN_UNITS = UP_UNITS + DOWN_UNITS

CHUNK = 128
NCH = T_PROMPT // CHUNK
LEVELS = 7
LASTTILE = T - P
SROW = P - T_SAMPLE
VCOLS = 512

GLA_UNITS = [13, 12]
HGRN_UNITS = [16, 16]
OUT_UNITS = 8
PLE_GATE_UNITS, PLE_PROJ_UNITS = 8, 2
PLE_ORDER = [0, 1, None, None, 2, 3, 4, 5, 6, 7]
START = {}
_n = 0
for _l in range(2):
    START["ffn", 2 * _l] = _n
    _n += FFN_UNITS
    for _g, _u in enumerate((GLA_UNITS, HGRN_UNITS)[_l]):
        START["mix", 2 * _l + _g] = _n
        _n += _u
    START["out", _l] = _n
    _n += OUT_UNITS
    START["ffn", 2 * _l + 1] = _n
    _n += FFN_UNITS
    START["ple", _l] = _n
    _n += PLE_GATE_UNITS + PLE_PROJ_UNITS
N_UNITS = _n


class Group:

    def __init__(self, gi):
        self.gi = gi
        self.gla = gi < 2
        self.layer = 0 if self.gla else 1
        self.g = gi % 2
        self.NH = 2 if self.gla else 4
        self.V = VCOLS // self.NH
        self.h0 = self.g * self.NH
        self.start = START["mix", gi]
        self.has_r = gi == 0
        self.nfeat = 2 * self.NH + self.has_r
        self.vt_per_head = self.V // P
        self.gate_scale = 1.0 / 16.0 if self.gla else 1.0
        self.q_scale = float(P) ** -0.5 if self.gla else 1.0
        self.feat0 = [0, 9, 17, 29][gi]
        self.g_unit = self.start + self.nfeat
        self.v_unit = self.g_unit + 4
        units = [("g", j) for j in range(4)] + [("v", u) for u in range(4)]
        if self.gla:
            levels = ["diag"] + list(range(LEVELS))
        else:
            levels = [None] * 3 + ["diag", None] + list(range(LEVELS))
            units += [(None, None)] * 4
        self.steps = [(kind, j, lv) for (kind, j), lv in zip(units, levels)]
        self.norm = 1 if self.gla else 5

    def level_bank(self, l):
        return 4 + l % 2 if self.NH == 2 else (6 if l == 5 else 4)

    def feat_bank(self, j):
        if j >= self.nfeat:
            return ([0, 2, 0, 2] if self.gla else [0, 2, 4, 0])[j - self.nfeat]
        if j < 2:
            return 2 * j
        return 6 if (self.nfeat - 1 - j) % 2 == 0 else 4


GROUPS = [Group(gi) for gi in range(4)]
N_STATE = [0]
for _gr in GROUPS:
    N_STATE.append(N_STATE[-1] + 1 + 2 * _gr.NH)
N_S0 = [4, 8, 16, 24]
N_HEADS = [0, 2, 4, 8, 12]
KM_BUFS = 6
V_BANKS = [0, 1, 2, 3, 7]


def build(nc, a, o):
    with ExitStack() as ctx:
        _build(nc, a, o, ctx)


def _build(nc, a, o, ctx):
    def sb(name, shape, dt=F32, where=ctx):
        return where.enter_context(nc.sbuf_tensor(name, shape, dt))

    ps = ctx.enter_context(nc.psum_tensor("ps", [P, 8, 512], F32))
    psf = ps[:].rearrange("p b n -> p (b n)")

    H = sb("h_resid", [P, KT_D, T])
    UH = sb("u_high", [P, KT_D, T], F32R)
    UL = sb("u_low", [P, KT_D, T], F32R)
    RAW = sb("w_raw", [P, RING, UNIT])
    WH = sb("w_high", [P, RING, UNIT], F32R)
    WL = sb("w_low", [P, RING, UNIT], F32R)
    ident = sb("ident", [P, P])
    ones = sb("ones", [P, P])
    masks = sb("masks", [P, LEVELS, 64])
    seqmask = sb("seqmask", [P, N_SEQ])
    vecs = sb("vectors", [P, VROWS])
    lbd = sb("lbd", [P, 6, KT_D])
    consts = sb("consts", [P, 2])
    rstd = sb("rstd", [P, T])
    rstdT = sb("rstd_tok", [P, 5])
    ssq = sb("ssq", [P, T])
    tG = sb("t_gate", [P, T])
    tU = sb("t_up", [P, T])
    DEC = sb("decay_chunk", [P, 4, NCH])
    DECS = sb("decay_seq", [P, 4, N_SEQ])

    with ExitStack() as region:
        HH = sb("hid_high", [P, NF, T], F32R, region)
        HL = sb("hid_low", [P, NF, T], F32R, region)
    with ExitStack() as region:
        XIN = sb("x_tok", [P, 5, D], F32, region)
    with ExitStack() as region:
        YF = sb("y_feat", [P, KT_D, T], F32, region)
        YT = sb("y_tok", [P, 5, D], F32, region)
    with ExitStack() as region:
        PIN = sb("p_tok", [P, 5, PLE], F32, region)
        PH = sb("p_high", [P, 2, T], F32R, region)
        PL = sb("p_low", [P, 2, T], F32R, region)
        PT = sb("p_feat", [P, 2, T], F32, region)
        GT = sb("ple_gate", [P, KT_D, T], F32, region)
        PX = sb("ple_proj", [P, KT_D, T], F32, region)
    with ExitStack() as region:
        OH = sb("o_high", [P, KT_D, T], F32R, region)
        OL = sb("o_low", [P, KT_D, T], F32R, region)
    with ExitStack() as region:
        Q = sb("q", [P, 4, T], F32, region)
        K = sb("k", [P, 4, T], F32, region)
        G = sb("gate_sum", [P, 4, T], F32, region)
        V = sb("v_tok", [P, 5, VCOLS], F32, region)
        AT = sb("attn", [P, 16, P], F32, region)
        ATS = sb("attn_s", [P, 4, T_SAMPLE], F32, region)
        OG = sb("out_gate", [P, KT_D, T], F32, region)
        KTb = sb("k_tilde", [P, 2, 4 * T], F32, region)
        QTb = sb("q_tilde", [P, 2, 2 * T], F32, region)
        EX = sb("ex", [P, 4 * T], F32, region)
    with ExitStack() as region:
        for nm, w in (("al_q", 4 * T), ("al_k", 4 * T), ("al_g", 4 * T), ("al_v", 5 * VCOLS), ("al_at", 16 * P),
                      ("al_ats", 4 * T_SAMPLE), ("al_og", KT_D * T)):
            sb(nm, [P, w], F32, region)
        KD = sb("kdec_tok", [P, 16, P], F32, region)
        ST = sb("states", [P, 4, VCOLS], F32, region)
        sb("al_pad", [P, 2 * 4 * T - 16 * P - 4 * VCOLS], F32, region)
        S0 = sb("states_s", [P, N_SEQ, VCOLS], F32, region)
    with ExitStack() as region:
        for nm, w in (("al2_q", 4 * T), ("al2_k", 4 * T), ("al2_g", 4 * T), ("al2_v", 5 * VCOLS)):
            sb(nm, [P, w], F32, region)
        ORS = sb("head_rstd", [P, 4, T], F32, region)
    ROWS = rstd[0:VROWS, 0:P]
    gains = vecs[:, 0:ROW_GN].rearrange("p (e m) -> p e m", m=KT_D)

    def gain_row(e):
        return 2 * (e % 4) + e // 4 if e < 8 else 8

    gn = vecs[:, ROW_GN:ROW_GN + 3]
    bgk = vecs[:, ROW_BGK:ROW_BGK + 4]
    lbr = vecs[:, ROW_LB:VROWS].rearrange("p (l m) -> p l m", m=KT_D)

    names = (
        "raw0 raw1 raw2 raw3 hi_made lo_made mm_units pc masks_made const_dma x_in w_gkup_in p_in s0_in out_y "
        "out_state dve_const pool_const ident_made x_turned h_done uh_done sq_done u_done ssq_added norm_mm "
        "ln_done rstd_done tg_done up_evicted silu_done hid_mul hid_hi hid_done feat_out v_out lb_a lb_b lb_c "
        "lb_done gk_mm x_out x_made gate_abs gate_exp gate_ln ls_made c_made kx_made gd_made gd_abs gd_exp "
        "gd_ln k_made gate_made q_made kt_zero diff_made ek_made eq_made kt_made qt_made lvl_mm lvl_out "
        "diag_mm diag_out sdiag_out slvl_out chunk_exp qin_made ksuf_made ksuf_exp kdec_made dec_made "
        "kd_turned kds_turned vec_turned vec_made kd_out u_mm s_made kmask_made us_mm snew_made o_mm os_mm "
        "o_out osq_made var_mm var_ln ors_made og_pre og_silu og_made og_made_p out_hi out_lo ple_t ple_sig "
        "p_turned p_feat p_hi p_lo p_out ple_mm ple_x y_made y_turned y_out_a y_out_v"
    ).split()
    s = {n: ctx.enter_context(nc.semaphore(n)) for n in names}
    raw_sem = [s["raw0"], s["raw1"], s["raw2"], s["raw3"]]

    def pair(b):
        return ps[:, b:b + 2, 0:HALF]

    def halves(ap):
        return ap.rearrange("p (a b) -> p a b", a=2)

    def tile_of(t3, m):
        if isinstance(m, int):
            return halves(t3[:, m, :])
        return t3[:, bass.ds(m, 1), :].rearrange("p o (a b) -> p (o a) b", a=2)

    def flat_of(t3, m):
        if isinstance(m, int):
            return t3[:, m, :]
        return t3[:, bass.ds(m, 1), :].rearrange("p o t -> p (o t)")

    w_gu = [a["ffn1_w_gu"], a["ffn2_w_gu"]]
    w_dn = [a["ffn1_w_down"], a["ffn2_w_down"]]

    RT = OG[:, KT_D - 1, :]
    EP = KTb[:, 1, :]
    LLB, L1M = lbd[:, 3, :], lbd[:, 1, :]
    WUP = KTb[:, 1, 0:512]

    def KM(b):
        i = b % KM_BUFS
        return G[:].rearrange("p h t -> p (h t)")[:, i * 512:(i + 1) * 512] if i < 4 else (tG, tU)[i - 4][:, 0:512]

    def blocks(ap, gr, L, all_tokens):
        if all_tokens:
            v = ap[:, 0:gr.NH, :].rearrange("p h (n l) -> p (h n) l", l=2 * L)
            return v[:, :, 0:L], v[:, :, L:2 * L], v[:, :, L - 1:L]
        v = ap[:, 0:gr.NH, 0:T_PROMPT].rearrange("p h (n l) -> p h n l", l=2 * L)
        return v[:, :, :, 0:L], v[:, :, :, L:2 * L], v[:, :, :, L - 1:L]

    def compact(ap2, gr, L, all_tokens):
        v = ap2[:, 0:gr.NH * HALF].rearrange("p (h t) -> p h t", t=HALF)
        if all_tokens:
            return v.rearrange("p h (n l) -> p (h n) l", l=L)
        return v[:, :, 0:T_PROMPT // 2].rearrange("p h (n l) -> p h n l", l=L)

    def p_sample_col(kt):
        return HALF + 32 + kt * T_SAMPLE

    block = ctx.enter_context(nc.Block())

    @block.sync
    def _(sp):
        def load_unit(base, i, j, src, nkt, width):
            n = base + j
            slot = n % RING
            if not isinstance(i, int) or n + i >= RING:
                sp.wait_ge(s["lo_made"], i + (n - RING + 1))
            sp.dma_start(RAW[:, slot, 0:nkt * width].rearrange("p (k n) -> p k n", k=nkt), src)\
              .then_inc(raw_sem[slot], 16)

        def cols(w, k0, k1, c0, n):
            v = w.rearrange("(k p) n -> p k n", p=P)
            return v[:, k0:k1, bass.ds(c0, n)]

        def ffn(F):
            l, base = F // 2, START["ffn", F]
            gu, dn = w_gu[F % 2][l], w_dn[F % 2][l]

            def up_body(i, off):
                for j in range(4):
                    f2, up = j // 2, j % 2
                    load_unit(base, off, j, cols(gu, 0, KT_D, i * (2 * P) + (f2 * P + up * F_FF), P), KT_D, P)

            if F == 0:
                for j in range(RING):
                    load_unit(0, 0, j, cols(gu, 0, KT_D, (j // 2) * P + (j % 2) * F_FF, P), KT_D, P)
            else:
                up_body(0, 0)
            with sp.Fori(1, NF // 2) as i:
                up_body(i, i * 4)
            with sp.Fori(0, 2) as i:
                for m4 in range(4):
                    for u, (k0, k1) in enumerate(DOWN_KT):
                        load_unit(base + UP_UNITS, i * 12, m4 * 3 + u, cols(dn, k0, k1, i * (4 * P) + m4 * P, P), k1 - k0, P)

        def token_loads():
            sp.dma_start(XIN[:, 0:4, :], a["x_prompt"][0].rearrange("(c p) d -> p c d", p=P)).then_inc(s["x_in"], 16)
            sp.dma_start(XIN[0:T_SAMPLE, 4, :], a["x_sample"].rearrange("b t d -> (b t) d")).then_inc(s["x_in"], 16)

        def state_loads(gr):
            st = a["state_gla"] if gr.gla else a["state_hgrn"]
            for half in range(2):
                if half == 0:
                    sp.wait_ge(s["lvl_mm"], LEVELS * (gr.gi + 1))
                else:
                    sp.wait_ge(s["kdec_made"], gr.gi + 1)
                for h in range(gr.NH):
                    sp.dma_start(S0[:, 4 * half:4 * half + 4, h * gr.V:(h + 1) * gr.V],
                                 st[0, 4 * half:4 * half + 4, gr.h0 + h].rearrange("b k v -> k b v")).then_inc(s["s0_in"], 16)

        def store_states(gr):
            out_p = o["gla_p"] if gr.gla else o["hgrn_p"]
            out_s = o["gla_s"] if gr.gla else o["hgrn_s"]
            sp.wait_ge(s["s_made"], 4 * gr.gi + 4)
            sp.dma_start(out_p[0, 0, gr.h0:gr.h0 + gr.NH].rearrange("h k v -> k h v"),
                         ST[:, 3, :].rearrange("p (h v) -> p h v", h=gr.NH)).then_inc(s["out_state"], 16)
            for half in range(2):
                sp.wait_ge(s["snew_made"], N_SEQ * gr.gi + 4 * half + 4)
                for h in range(gr.NH):
                    sp.dma_start(out_s[0, 4 * half:4 * half + 4, gr.h0 + h].rearrange("b k v -> k b v"),
                                 S0[:, 4 * half:4 * half + 4, h * gr.V:(h + 1) * gr.V]).then_inc(s["out_state"], 16)

        def mix_sources(gr):
            w = a["gla_w_in"][0] if gr.gla else a["hgrn_w_in"][0]
            q0 = gr.h0 * P
            k0 = (512 if gr.gla else 1024) + gr.h0 * P
            v0 = (1024 if gr.gla else 2048) + gr.g * VCOLS
            g0 = (2048 if gr.gla else 3072) + gr.g * VCOLS
            starts = ([3088 - P] if gr.has_r else []) + [q0 + P * h for h in range(gr.NH)] + \
                [k0 + P * h for h in range(gr.NH)] + [g0 + P * t for t in range(4)]
            return [(cols(w, 0, KT_D, c, P), KT_D, P) for c in starts] + \
                [(cols(w, 2 * u, 2 * u + 2, v0, VCOLS), 2, VCOLS) for u in range(4)]

        def out_sources(l):
            w = (a["gla_w_out"] if l == 0 else a["hgrn_w_out"])[0]
            return [(cols(w, 0, KT_D, m * P, P), KT_D, P) for m in range(KT_D)]

        def mixer(l):
            groups = GROUPS[2 * l:2 * l + 2]
            n = groups[0].start
            for i, src in enumerate([mix_sources(groups[0]), mix_sources(groups[1]), out_sources(l)]):
                for j, (ap, nkt, width) in enumerate(src):
                    if i and j == 4:
                        state_loads(groups[i - 1])
                        store_states(groups[i - 1])
                    load_unit(n, 0, 0, ap, nkt, width)
                    n += 1

        def ple(l):
            n = START["ple", l]
            for i, m in enumerate(PLE_ORDER):
                if m is None:
                    u = i - 2
                    load_unit(n + i, 0, 0, cols(a["ple_w_proj"][l], 0, 2, u * 512, 512), 2, 512)
                else:
                    load_unit(n + i, 0, 0, cols(a["ple_w_gate"][l], 0, KT_D, m * P, P), KT_D, P)
                if i == 3:
                    sp.wait_ge(s["h_done"], 8 * (4 * l + 3) + 8)
                    sp.dma_start(PIN[:, 0:4, :], a["p_prompt"][l, 0].rearrange("(c p) d -> p c d", p=P)).then_inc(s["p_in"], 16)
                    sp.dma_start(PIN[0:T_SAMPLE, 4, :], a["p_sample"][l].rearrange("b t d -> (b t) d")).then_inc(s["p_in"], 16)

        token_loads()
        sp.wait_ge(s["const_dma"], 16 * N_VEC_LOADS)
        for l in range(2):
            ffn(2 * l)
            mixer(l)
            ffn(2 * l + 1)
            ple(l)
        for c in range(5):
            sp.wait_ge(s["y_out_a" if c % 2 else "y_out_v"], c // 2 + 1)
            if c < 4:
                sp.dma_start(o["y_p"][0, c * P:(c + 1) * P, :], YT[:, c, :]).then_inc(s["out_y"], 16)
            else:
                sp.dma_start(o["y_s"].rearrange("b t d -> (b t) d"), YT[0:T_SAMPLE, 4, :]).then_inc(s["out_y"], 16)
        sp.wait_ge(s["out_y"], 16 * 5)
        sp.wait_ge(s["out_state"], 16 * N_STATE[4])

    @block.tensor
    def _(pe):
        def weights(slot, k, kind, m0=0, mw=P, kw=P):
            w = WH if kind == "h" else WL
            return w[:, slot, k * kw + m0:k * kw + m0 + mw]

        def unit_ready(n):
            pe.wait_ge(s["lo_made"], n + 1)

        def products(slot, nk, k0, kt_total, bank, xh, xl, m0=0, kw=P, before=None):
            for k in range(nk):
                kk = k0 + k
                if before is not None:
                    before(kk)
                for part, (wk, x) in enumerate((("h", xh), ("h", xl), ("l", xh))):
                    for hf in range(2):
                        mm = pe.matmul(ps[:, bank + hf, 0:HALF], weights(slot, k, wk, m0, P, kw),
                                       x[:, kk, hf * HALF:(hf + 1) * HALF],
                                       start=(kk == 0 and part == 0), stop=(kk == kt_total - 1 and part == 2))
            return mm

        def wait_u(e):
            def before(kk):
                pe.wait_ge(s["u_done"], 8 * e + kk + 1)
            return before

        def norm(e, by_token=False):
            pe.wait_ge(s["ssq_added"], 8 * e + 8)
            pe.wait_ge(s["h_done"], 8 * e + 7)
            for hf in range(2):
                mm = pe.matmul(ps[:, 4 + hf, 0:HALF], ones[:, :], ssq[:, hf * HALF:(hf + 1) * HALF], start=True, stop=True)
            if by_token:
                for c in range(5):
                    t0 = c * P if c < 4 else LASTTILE
                    mm = pe.matmul(ps[:, 4, 300 + c:301 + c], ssq[:, t0:t0 + P], ones[:, 0:1], start=True, stop=True)
            mm.then_inc(s["norm_mm"], 1)

        def ffn(F):
            base, e = START["ffn", F], 2 * F

            def chunk(f, n, slot, first):
                bank = 4 * (slot // 2)
                if first and bank == 0:
                    pe.wait_ge(s["h_done"], 8 * e + 6)
                elif first:
                    pe.wait_ge(s["h_done"], 8 * e + 8)
                    pe.wait_ge(s["rstd_done"], e + 1)
                else:
                    pe.wait_ge(s["up_evicted"], f + (NF * F - 1))
                for up in range(2):
                    unit_ready(n + up)
                    products((base + slot + up) % RING, KT_D, 0, KT_D, bank + 2 * up, UH, UL,
                             before=wait_u(e) if first and bank == 0 else None).then_inc(s["mm_units"], 1)
                    if first and bank == 0 and up == 0:
                        norm(e)

            for c in range(2):
                chunk(c, base + 2 * c, 2 * c, True)
            with pe.Fori(1, NF // 2) as i:
                for c in range(2):
                    chunk(i * 2 + c, i * 4 + (base + 2 * c), 2 * c, False)
            base += UP_UNITS
            def down_tile(i, m4, first):
                if first:
                    pe.wait_ge(s["up_evicted"], NF * F + (NF - 1 if m4 < 2 else NF))
                else:
                    pe.wait_ge(s["h_done"], 8 * (e + 1) + m4 + 1)
                for u, (k0, k1) in enumerate(DOWN_KT):
                    n = m4 * 3 + u
                    unit_ready(i * 12 + (base + n))

                    def before(kk):
                        if first and m4 == 0:
                            pe.wait_ge(s["hid_done"], NF * F + kk + 1)
                    products((base + n) % RING, k1 - k0, k0, NF, 2 * m4, HH, HL, before=before).then_inc(s["mm_units"], 1)

            for m4 in range(4):
                down_tile(0, m4, True)
            for m4 in range(4):
                down_tile(1, m4, False)

        def features(gr):
            e = gr.norm
            j = 0
            n = gr.start
            def feature_tile(j, n):
                b = gr.feat_bank(j)
                if j < 2 and gr.g == 0:
                    pe.wait_ge(s["h_done"], 8 * e + 6)
                elif gr.g == 0 and j == 2:
                    pe.wait_ge(s["h_done"], 8 * e + 8)
                    pe.wait_ge(s["rstd_done"], e + 1)
                    pe.wait_ge(s["feat_out"], gr.feat0 + j - 1)
                elif j >= gr.nfeat:
                    i = j - gr.nfeat
                    if i < 2 and gr.has_r:
                        pe.wait_ge(s["x_out"], i + 1)
                    elif i >= 2 and not gr.gla:
                        pe.wait_ge(s["feat_out"], gr.feat0 + (7 if i == 2 else gr.nfeat + 1))
                    else:
                        pe.wait_ge(s["feat_out"], gr.feat0 + (i + 1 if i < 2 else j - 1))
                elif 2 <= j < gr.nfeat:
                    pe.wait_ge(s["feat_out"], gr.feat0 + j - 1)
                elif gr.g == 1 and j == 0:
                    pe.wait_ge(s["var_ln"], 2 * gr.gi)
                elif gr.g == 1 and j == 1:
                    pe.wait_ge(s["snew_made"], N_SEQ * gr.gi)
                unit_ready(n)
                products(n % RING, KT_D, 0, KT_D, b, UH, UL,
                         before=wait_u(e) if j == 0 and gr.g == 0 else None).then_inc(s["mm_units"], 1)
                if j == 0 and gr.g == 0:
                    norm(e, True)
            for j in range(gr.nfeat):
                feature_tile(j, n)
                n += 1
                if gr.has_r and j >= gr.nfeat - 2:
                    gk(gr, range(2) if j == gr.nfeat - 2 else (2,))
            for kind, j, lv in gr.steps:
                if kind == "g":
                    feature_tile(gr.nfeat + j, n)
                    n += 1
                elif kind == "v":
                    values(gr, j, n)
                    n += 1
                if lv == "diag":
                    if gr.has_r:
                        gk(gr, (3,))
                    diagonal(gr)
                elif lv is not None:
                    level(gr, lv)

        def values(gr, u, n):
            unit_ready(n)
            for c in range(5):
                t0 = c * P if c < 4 else LASTTILE
                if u == 0 and c in (0, 2):
                    pe.wait_ge(s["feat_out"], gr.feat0 + gr.nfeat + (3 + (c == 2) if gr.gla else 4))
                if u == 0 and c == 4:
                    pe.wait_ge(s["diag_out"], gr.gi + 1)
                for k in range(2):
                    kk = 2 * u + k
                    for part, (x, w) in enumerate(((UH, WH), (UL, WH), (UH, WL))):
                        mm = pe.matmul(ps[:, V_BANKS[c], :], x[:, kk, t0:t0 + P], w[:, n % RING, k * 512:(k + 1) * 512],
                                       start=(kk == 0 and part == 0), stop=(kk == KT_D - 1 and part == 2))
            mm.then_inc(s["mm_units"], 1)

        def diagonal(gr):
            gi = gr.gi
            pe.wait_ge(s["feat_out"], gr.feat0 + gr.nfeat + (0 if gr.gla else 3))
            if gr.has_r:
                pe.wait_ge(s["x_out"], 4)
            if not gr.gla:
                pe.wait_ge(s["q_made"], gi - 1)
                pe.wait_ge(s["k_made"], gi - 1)
            for h in range(gr.NH):
                for c in range(NCH):
                    x = h * NCH + c
                    mm = pe.matmul(ps[:, 4 + x // 4, (x % 4) * P:(x % 4 + 1) * P], K[:, h, c * P:(c + 1) * P],
                                   Q[:, h, c * P:(c + 1) * P], start=True, stop=True)
            mm.then_inc(s["diag_mm"], 1)

        def level(gr, l):
            gi, NH = gr.gi, gr.NH
            n = LEVELS * gi + l
            b0 = gr.level_bank(l)
            if l:
                pe.wait_ge(s["kt_made"], (LEVELS - 1) * gi + l)
            pe.wait_ge(s["qt_made"], n + 1)

            def k_of(h, t0):
                return KTb[:, l % 2, h * T + t0:h * T + t0 + P] if l else K[:, h, t0:t0 + P]

            if l == 0:
                pe.wait_ge(s["diag_out"], gi + 1)
            elif NH == 4 and l < 5:
                pe.wait_ge(s["lvl_out"], n)
            elif NH == 4 and l == 5:
                pe.wait_ge(s["slvl_out"], 2 * gi + 2)
                pe.wait_ge(s["v_out"], 5 * gi + 1)
            elif l >= 2:
                pe.wait_ge(s["lvl_out"], n - 1)
            for h in range(NH):
                for c in range(NCH):
                    x = h * NCH + c
                    mm = pe.matmul(ps[:, b0 + x // 8, (x % 8) * 64:(x % 8 + 1) * 64],
                                   k_of(h, c * P),
                                   QTb[:, l % 2, h * HALF + c * 64:h * HALF + (c + 1) * 64], start=True, stop=True)
            if l == 1:
                pe.wait_ge(s["slvl_out"], 2 * gi + 1)
                pe.wait_ge(s["sdiag_out"], gi + 1)
            if l < 2:
                for h in range(NH):
                    mm = pe.matmul(ps[:, 6, (8 + 4 * l + h) * 16:(9 + 4 * l + h) * 16], k_of(h, LASTTILE),
                                   QTb[:, l % 2, h * HALF + 256:(h + 1) * HALF], start=True, stop=True)
            if l == 0:
                for h in range(NH):
                    mm = pe.matmul(ps[:, 6, h * 32:(h + 1) * 32], K[:, h, LASTTILE:T], Q[:, h, T_PROMPT:T],
                                   start=True, stop=True)
            mm.then_inc(s["lvl_mm"], 1)

        def gk(gr, heads):
            for h in heads:
                if h == 0:
                    pe.wait_ge(s["w_gkup_in"], 16)
                pe.wait_ge(s["feat_out"], gr.feat0 + (1, 2, 4, 5)[h])
                for hf in range(2):
                    mm = pe.matmul(ps[:, 2 * h + hf, 0:HALF], WUP[:, h * P:(h + 1) * P],
                                   RT[:, hf * HALF:(hf + 1) * HALF], start=True, stop=True)
                mm.then_inc(s["gk_mm"], 1)

        def mix(gr):
            gi, NH = gr.gi, gr.NH
            pe.wait_ge(s["v_out"], 5 * gi + 5)
            pe.wait_ge(s["kdec_made"], gi + 1)
            for h in range(NH):
                for c in range(NCH):
                    x = h * NCH + c
                    mm = pe.transpose(ps[:, x // 4, (x % 4) * P:(x % 4 + 1) * P], K[:, h, c * P:(c + 1) * P], ident[:, :])
            mm.then_inc(s["kd_turned"], 1)
            pe.wait_ge(s["lvl_out"], LEVELS * (gi + 1))
            for j in range(4):
                h = j // gr.vt_per_head
                for c in range(NCH):
                    pe.matmul(ps[:, 4 + j, c * P:(c + 1) * P], V[:, c, j * P:(j + 1) * P], AT[:, h * NCH + c, :],
                              start=(c == 0), stop=False, skip_group_check=True)
            pe.wait_ge(s["kd_out"], gi + 1)
            for c in range(NCH):
                for h in range(NH):
                    mm = pe.matmul(ps[:, c, h * gr.V:(h + 1) * gr.V], KD[:, h * NCH + c, :],
                                   V[:, c, h * gr.V:(h + 1) * gr.V], start=True, stop=True)
                mm.then_inc(s["u_mm"], 1)
            pe.wait_ge(s["qin_made"], gi + 1)
            pe.wait_ge(s["slvl_out"], 2 * (gi + 1))
            pe.wait_ge(s["s_made"], 4 * gi + 1)
            for j in range(4):
                h = j // gr.vt_per_head
                pe.matmul(ps[:, 0, j * 32:(j + 1) * 32], V[:, 4, j * P:(j + 1) * P], ATS[:, h, :],
                          start=(j == 0), stop=False, skip_group_check=True)
            pe.wait_ge(s["s0_in"], 16 * N_S0[gi])
            for j in range(4):
                h = j // gr.vt_per_head
                for b in range(N_SEQ):
                    mm = pe.matmul(ps[:, 0, j * 32 + 4 * b:j * 32 + 4 * b + 4], S0[:, b, j * P:(j + 1) * P],
                                   Q[:, h, T_PROMPT + 4 * b:T_PROMPT + 4 * b + 4],
                                   start=False, stop=(j == 3 and b == N_SEQ - 1), skip_group_check=True)
            mm.then_inc(s["os_mm"], 1)
            pe.wait_ge(s["s_made"], 4 * gi + 2)
            for h in range(NH):
                mm = pe.transpose(ps[:, 1, h * P:(h + 1) * P], K[:, h, LASTTILE:T], ident[:, :])
            mm.then_inc(s["kds_turned"], 1)
            pe.wait_ge(s["s_made"], 4 * gi + NCH - 1)
            for j in range(4):
                h = j // gr.vt_per_head
                for c in range(1, NCH):
                    mm = pe.matmul(ps[:, 4 + j, c * P:(c + 1) * P], ST[:, c - 1, j * P:(j + 1) * P],
                                   Q[:, h, c * P:(c + 1) * P], start=False, stop=(c == NCH - 1), skip_group_check=True)
                mm.then_inc(s["o_mm"], 1)

            def sequence(b):
                pe.wait_ge(s["kmask_made"], N_SEQ * gi + b + 1)
                if b < 2:
                    pe.wait_ge(s["s_made"], 4 * gi + NCH)
                else:
                    pe.wait_ge(s["snew_made"], N_SEQ * gi + b - 1)
                for h in range(NH):
                    mm = pe.matmul(ps[:, 2 + b % 2, h * gr.V:(h + 1) * gr.V], KM(b)[:, h * P:(h + 1) * P],
                                   V[:, 4, h * gr.V:(h + 1) * gr.V], start=True, stop=True)
                mm.then_inc(s["us_mm"], 1)

            for b in range(2):
                sequence(b)
            for h in range(NH):
                vt = gr.vt_per_head
                pe.wait_ge(s["osq_made"], 4 * gi + (h + 1) * vt)
                for t0, t1, dst in ((0, T_PROMPT, ps[:, 4 + h, :]),
                                    (T_PROMPT, T, ps[:, 0, h * T_SAMPLE:(h + 1) * T_SAMPLE])):
                    for t in range(vt):
                        mm = pe.matmul(dst, ones[:, :], K[:, h * vt + t, t0:t1], start=(t == 0), stop=(t == vt - 1))
            mm.then_inc(s["var_mm"], 1)
            for b in range(2, N_SEQ):
                sequence(b)

        def out_proj(l):
            n = START["out", l]
            e = 4 * l + 2
            for m in range(KT_D):
                if m == 0:
                    pe.wait_ge(s["var_ln"], 2 * (2 * l + 2))
                if m == 1:
                    pe.wait_ge(s["snew_made"], N_SEQ * (2 * l + 2))
                if m >= 4:
                    pe.wait_ge(s["h_done"], 8 * e + m - 3)
                unit_ready(n)

                def before(kk):
                    if m == 0:
                        pe.wait_ge(s["out_lo"], 8 * l + kk + 1)
                products(n % RING, KT_D, 0, KT_D, 2 * (m % 4), OH, OL, before=before).then_inc(s["mm_units"], 1)
                n += 1

        def ple(l):
            n = START["ple", l]
            e = 4 * l + 3
            for i, m in enumerate(PLE_ORDER):
                unit_ready(n + i)
                if m is not None:
                    if m == 0:
                        pe.wait_ge(s["h_done"], 8 * e + 6)
                    elif 2 <= m < 6:
                        pe.wait_ge(s["p_out"], 8 * l + m + 3)
                    elif m >= 6:
                        pe.wait_ge(s["ple_t"], 8 * l + m - 3)
                    products((n + i) % RING, KT_D, 0, KT_D, 2 * (m % 4), UH, UL, before=wait_u(e) if m == 0 else None)\
                        .then_inc(s["mm_units"], 1)
                if m == 0:
                    norm(e)
                    pe.wait_ge(s["p_in"], 32 * (l + 1))
                    pe.wait_ge(s["h_done"], 8 * e + 8)
                    for kt in range(2):
                        for c in range(4):
                            pe.transpose(ps[:, 6 + kt, c * P:(c + 1) * P], PIN[:, c, kt * P:(kt + 1) * P], ident[:, :])
                        mm = pe.transpose(ps[:, 1, p_sample_col(kt):p_sample_col(kt) + T_SAMPLE],
                                          PIN[0:T_SAMPLE, 4, kt * P:(kt + 1) * P], ident[0:T_SAMPLE, 0:T_SAMPLE])
                    mm.then_inc(s["p_turned"], 1)
                if m is None:
                    for j in range(4 * (i - 2), 4 * (i - 2) + 4):
                        if j == 0:
                            pe.wait_ge(s["p_lo"], 2 * l + 2)
                            pe.wait_ge(s["rstd_done"], e + 1)
                        elif j in (2, 3):
                            pe.wait_ge(s["ple_t"], 8 * l + j - 1)
                        elif j >= 4:
                            pe.wait_ge(s["p_out"], 8 * l + j - 3)
                        mm = products((n + i) % RING, 2, 0, 2, 2 * ((j + 2) % 4), PH, PL, m0=(j % 4) * P, kw=512)
                        mm.then_inc(s["mm_units" if j % 4 == 3 else "ple_mm"], 1)

        def turn(src, m, bank):
            for c in range(5):
                rows = P if c < 4 else T_SAMPLE
                mm = pe.transpose(psf[:, bank * 512 + c * P:bank * 512 + c * P + rows],
                                  src[0:rows, c, m * P:(m + 1) * P], ident[0:rows, 0:rows])
            return mm

        pe.wait_ge(s["ident_made"], 1)
        pe.wait_ge(s["dve_const"], 1)
        pe.wait_ge(s["x_in"], 32)
        for m in range(KT_D):
            if m == 1:
                pe.wait_ge(s["const_dma"], 16 * N_VEC_LOADS)
                pe.transpose(ps[:, 7, 0:VROWS], ROWS, ident[0:VROWS, 0:VROWS]).then_inc(s["vec_turned"], 1)
            if m == 3:
                pe.wait_ge(s["vec_made"], 1)
            if m >= 4:
                pe.wait_ge(s["h_done"], m - 3)
            turn(XIN, m, 2 * (m % 4)).then_inc(s["x_turned"], 1)
        for l in range(2):
            ffn(2 * l)
            for g in range(2):
                gr = GROUPS[2 * l + g]
                features(gr)
                mix(gr)
            out_proj(l)
            ffn(2 * l + 1)
            ple(l)
        pe.wait_ge(s["ple_t"], 8 + 7)

        def turn_out(c, m):
            cols = P if c < 4 else T_SAMPLE
            pe.wait_ge(s["y_made"], m + 1)
            return pe.transpose(psf[0:cols, (2 * (c % 4)) * 512 + m * P:(2 * (c % 4)) * 512 + (m + 1) * P],
                                YF[:, m, c * P:c * P + cols], ident[:, :])

        for m in range(KT_D):
            for c in range(3):
                mm = turn_out(c, m)
                if m == KT_D - 1:
                    mm.then_inc(s["y_turned"], 1)
        pe.wait_ge(s["ssq_added"], 8 * 8 + 8)
        for c in range(5):
            cols = P if c < 4 else T_SAMPLE
            mm = pe.matmul(ps[0:cols, 6, c:c + 1], ssq[:, c * P:c * P + cols], ones[:, 0:1], start=True, stop=True)
        mm.then_inc(s["norm_mm"], 1)
        for c in range(3, 5):
            if c == 3:
                pe.wait_ge(s["ln_done"], N_LN)
            else:
                pe.wait_ge(s["y_out_v"], 1)
            for m in range(KT_D):
                mm = turn_out(c, m)
            mm.then_inc(s["y_turned"], 1)

    @block.scalar
    def _(act):
        def high(base, i, j=0):
            n = base + j
            slot = n % RING
            act.wait_ge(raw_sem[slot], q16(i, n))
            if not isinstance(i, int) or n >= RING:
                act.wait_ge(s["mm_units"], i + (n - RING + 1))
            act.activation(WH[:, slot, :], RAW[:, slot, :], ACT.Copy).then_inc(s["hi_made"], 1)

        def q16(i, n):
            return (i // 4) * 16 + 16 * (n // RING + 1) if isinstance(i, int) else i * 4 + 16 * (n // RING + 1)

        def square_out(e, m):
            act.wait_ge(s["h_done"], 8 * e + m + 1)
            act.wait_ge(s["ssq_added"], 8 * e + m - 1)
            act.activation((tG, tU)[m % 2][:, :], H[:, m, :], ACT.Square).then_inc(s["sq_done"], 1)

        def scaled_out(m):
            act.activation(YF[:, m, :], H[:, m, :], ACT.Copy, scale=gain_of(8, m)).then_inc(s["y_made"], 1)

        def high_out(e, m):
            act.activation(UH[:, m, :], H[:, m, :], ACT.Copy, scale=gain_of(e, m)).then_inc(s["uh_done"], 1)

        def tile_out(e, m, mc):
            act.wait_ge(s["h_done"], m + (8 * e + 1))
            if not isinstance(m, int) or 8 * e + m >= 2:
                act.wait_ge(s["ssq_added"], m + (8 * e - 1))
            if not isinstance(m, int):
                act.wait_ge(s["pool_const"], 1)
            if e < 8:
                act.activation(flat_of(UH, m), flat_of(H, m), ACT.Copy,
                               scale=gain_of(e, m)).then_inc(s["uh_done"], 1)
            act.activation((tG, tU)[mc % 2][:, :], flat_of(H, m), ACT.Square).then_inc(s["sq_done"], 1)

        def gain_of(e, m):
            return gains[:, gain_row(e), m:m + 1] if isinstance(m, int) else \
                gains[:, gain_row(e), bass.ds(m, 1)]

        def norm(e, by_token=False):
            act.wait_ge(s["norm_mm"], e + 1)
            if by_token:
                act.activation(rstdT[:, :], ps[:, 4, 300:305], ACT.Ln, bias=consts[:, 0:1], scale=1.0 / D).then_inc(s["ln_done"], 1)
            act.activation(halves(rstd[:, :]), pair(4), ACT.Ln, bias=consts[:, 0:1], scale=1.0 / D).then_inc(s["ln_done"], 1)
            done = e + 1 + (e > 0) + (e > 4)
            act.wait_ge(s["ln_done"], done)
            if by_token:
                act.activation(rstdT[:, :], rstdT[:, :], ACT.Exp, scale=-0.5)
            act.activation(rstd[:, :], rstd[:, :], ACT.Exp, scale=-0.5).then_inc(s["rstd_done"], 1)

        def ffn(F):
            base, e = START["ffn", F], 2 * F

            def chunk(i4, f, j, first=False):
                high(base, i4, j + 2)
                high(base, i4, j + 3)
                if first:
                    norm(e)
                act.wait_ge(s["tg_done"], f + (NF * F + 1))
                act.activation(tG[:, :], tG[:, :], ACT.Silu).then_inc(s["silu_done"], 1)
                act.wait_ge(s["hid_mul"], f + (NF * F + 1))
                act.wait_ge(s["pool_const"], 1)
                act.activation(flat_of(HH, f), tU[:, :], ACT.Copy).then_inc(s["hid_hi"], 1)

            chunk(0, 0, 0, True)
            chunk(0, 1, 2)
            with act.Fori(1, NF // 2) as i:
                for c in range(2):
                    chunk(i * 4, i * 2 + c, 2 * c)
            base += UP_UNITS
            with act.Fori(0, 2) as i:
                for m4 in range(4):
                    for u in range(3):
                        high(base, i * 12, 3 * m4 + u + 2)
                    tile_out(e + 1, i * 4 + m4, m4)

        def ahead(n):
            if n + 2 < N_UNITS:
                high(n + 2, 0)

        def features(gr):
            n = gr.start
            for j in range(gr.nfeat):
                ahead(n)
                if j == 0 and gr.g == 0:
                    norm(gr.norm, True)
                n += 1
            if gr.gla:
                gate(gr)
            for kind, j, lv in gr.steps:
                if kind:
                    ahead(n)
                    n += 1
                if not gr.gla and kind == "g" and j == 1:
                    gate(gr)
                if not gr.gla and kind == "g" and j == 3:
                    gate_end(gr)
                if lv not in (None, "diag"):
                    level(gr, lv)
                if not gr.gla and lv == 4:
                    values_out(gr, (4, 0, 1, 2, 3))

        def values_out(gr, tiles):
            act.wait_ge(s["mm_units"], gr.v_unit + 4)
            act.wait_ge(s["rstd_done"], gr.norm + 1)
            for c in tiles:
                act.activation(V[:, c, :], ps[:, V_BANKS[c], :], ACT.Copy, scale=rstdT[:, c:c + 1]).then_inc(s["v_out"], 1)

        def level(gr, l):
            gi, gs = gr.gi, gr.gate_scale
            n, L = LEVELS * gi + l, 1 << l
            both = l < 2
            _, g2, _ = blocks(G, gr, L, both)
            act.wait_ge(s["gate_made"], (LEVELS + 1) * gi + l + 1)
            if l:
                act.wait_ge(s["qt_made"], n)
            act.activation(compact(EX[:, 2 * T:4 * T], gr, L, both), g2, ACT.Exp, scale=gs).then_inc(s["eq_made"], 1)
            if l == 0:
                return
            act.wait_ge(s["diff_made"], (LEVELS - 1) * gi + l)
            dk = compact(EX[:, 0:2 * T], gr, L, both)
            act.activation(dk, dk, ACT.Exp, scale=gs).then_inc(s["ek_made"], 1)

        def gate(gr):
            if gr.gla:
                if gr.has_r:
                    act.wait_ge(s["x_out"], 2)
                else:
                    act.wait_ge(s["x_made"], 1)
                log_sigmoid_tail(gr, G[:, 0:2, :].rearrange("p h t -> p (h t)"))
                return
            kk = K[:].rearrange("p h t -> p (h t)")
            act.wait_ge(s["feat_out"], gr.feat0 + gr.nfeat)
            act.activation(Q[:], Q[:], ACT.Silu).then_inc(s["q_made"], 1)
            log_sigmoid_tail(gr, kk)

        def gate_end(gr):
            k = gr.gi - 1
            ex = EX[:, :]
            kk = K[:].rearrange("p h t -> p (h t)")
            act.wait_ge(s["kx_made"], k)
            act.activation(kk, kk, ACT.Exp).then_inc(s["k_made"], 1)
            act.wait_ge(s["gd_made"], k)
            act.activation(ex, ex, ACT.Abs).then_inc(s["gd_abs"], 1)
            act.wait_ge(s["gd_abs"], k)
            act.activation(ex, ex, ACT.Exp, scale=-1.0).then_inc(s["gd_exp"], 1)
            act.wait_ge(s["gd_exp"], k)
            act.activation(ex, ex, ACT.Ln, bias=consts[:, 1:2]).then_inc(s["gd_ln"], 1)

        def log_sigmoid_tail(gr, x):
            k = gr.gi + 1
            ex = EX[:, 0:gr.NH * T]
            if gr.gi:
                act.wait_ge(s["out_state"], 16 * N_STATE[gr.gi])
            act.activation(ex, x, ACT.Abs).then_inc(s["gate_abs"], 1)
            act.wait_ge(s["gate_abs"], k)
            act.activation(ex, ex, ACT.Exp, scale=-1.0).then_inc(s["gate_exp"], 1)
            act.wait_ge(s["gate_exp"], k)
            act.activation(ex, ex, ACT.Ln, bias=consts[:, 1:2]).then_inc(s["gate_ln"], 1)

        def mix(gr):
            gi, NH = gr.gi, gr.NH
            gs = gr.gate_scale
            act.wait_ge(s["gate_made"], (LEVELS + 1) * (gi + 1))
            act.wait_ge(s["lvl_mm"], LEVELS * (gi + 1) - 1)
            gf = G[:, 0:NH, :].rearrange("p h t -> p (h t)")
            act.activation(EP[:, 0:NH * T], gf, ACT.Exp, scale=gs).then_inc(s["chunk_exp"], 1)
            act.wait_ge(s["ksuf_made"], 2 * gi + 2)
            act.activation(EX[:, 0:NH * T], EX[:, 0:NH * T], ACT.Exp, scale=gs).then_inc(s["ksuf_exp"], 1)
            if gr.gla:
                values_out(gr, (4, 0, 1, 2, 3))
            ends = G[:, 0:NH, 0:T_PROMPT].rearrange("p h (c t) -> p h c t", t=CHUNK)[:, :, :, CHUNK - 1]
            act.activation(DEC[:, 0:NH, :], ends, ACT.Exp, scale=gs).then_inc(s["dec_made"], 1)
            ends = G[:, 0:NH, T_PROMPT:T].rearrange("p h (c t) -> p h c t", t=T_SEQ)[:, :, :, T_SEQ - 1]
            act.activation(DECS[:, 0:NH, :], ends, ACT.Exp, scale=gs).then_inc(s["dec_made"], 1)
            act.wait_ge(s["feat_out"], gr.feat0 + gr.nfeat + 4)
            act.activation(OG[:, 4 * gr.g:4 * gr.g + 4, :], OG[:, 4 * gr.g:4 * gr.g + 4, :], ACT.Silu).then_inc(s["og_silu"], 1)
            act.wait_ge(s["kd_turned"], gi + 1)
            act.activation(KD[:, 0:NH * NCH, :].rearrange("p x k -> p (x k)"), psf[:, 0:NH * NCH * P], ACT.Copy).then_inc(s["kd_out"], 1)
            act.wait_ge(s["kds_turned"], gi + 1)
            act.wait_ge(s["dec_made"], 2 * gi + 2)

            def kmask(b):
                if b >= KM_BUFS:
                    act.wait_ge(s["us_mm"], N_SEQ * gi + b - KM_BUFS + 1)
                act.activation(KM(b)[:, 0:NH * P], ps[:, 1, 0:NH * P], ACT.Copy, scale=seqmask[:, b:b + 1])\
                   .then_inc(s["kmask_made"], 1)

            for b in range(KM_BUFS):
                kmask(b)
            for j in range(4):
                act.wait_ge(s["o_out"], 5 * gi + j + 2)
                act.activation(K[:, j, :], Q[:, j, :], ACT.Square).then_inc(s["osq_made"], 1)
            for b in range(KM_BUFS, N_SEQ):
                kmask(b)
            act.wait_ge(s["var_mm"], gi + 1)
            act.activation(ORS[:, 0:NH, 0:T_PROMPT], ps[:, 4:4 + NH, :], ACT.Ln, bias=consts[:, 0:1], scale=1.0 / gr.V)\
               .then_inc(s["var_ln"], 1)
            act.activation(ORS[:, 0:NH, T_PROMPT:T], ps[:, 0, 0:NH * T_SAMPLE].rearrange("p (h t) -> p h t", h=NH),
                           ACT.Ln, bias=consts[:, 0:1], scale=1.0 / gr.V).then_inc(s["var_ln"], 1)
            act.wait_ge(s["var_ln"], 2 * gi + 2)
            for h in range(NH):
                act.activation(ORS[:, h, :], ORS[:, h, :], ACT.Exp, scale=-0.5).then_inc(s["ors_made"], 1)

        def out_high(l):
            for kk in range(KT_D):
                if kk == 0:
                    act.wait_ge(s["og_pre"], 8 * l + 8)
                    act.wait_ge(s["osq_made"], 8 * l + 8)
                act.wait_ge(s["og_made" if kk % 4 < 2 else "og_made_p"], 2 * (2 * l + kk // 4) + kk % 2 + 1)
                act.activation(OH[:, kk, :], OG[:, kk, :], ACT.Copy).then_inc(s["out_hi"], 1)

        def out_proj(l):
            e = 4 * l + 2
            out_high(l)
            for m in range(KT_D):
                ahead(START["out", l] + m)
                tile_out(e, m, m)

        def ple(l):
            e, n = 4 * l + 3, START["ple", l]
            for i, m in enumerate(PLE_ORDER):
                ahead(n + i)
                if m == 0:
                    norm(e)
                    for kt in range(2):
                        act.wait_ge(s["p_feat"], 2 * (2 * l + kt + 1))
                        act.activation(PH[:, kt, :], PT[:, kt, :], ACT.Copy).then_inc(s["p_hi"], 1)
                if m is None:
                    continue
                if m == 2:
                    square_out(e + 1, 0)
                    if l == 1:
                        scaled_out(0)
                if m >= 2:
                    square_out(e + 1, m - 1)
                    if l == 1:
                        scaled_out(m - 1)
                if m == KT_D - 1 and l == 0:
                    act.wait_ge(s["mm_units"], n + len(PLE_ORDER))
                    high_out(e + 1, 0)
                act.wait_ge(s["ple_t"], 8 * l + m + 1)
                act.activation(GT[:, m, :], GT[:, m, :], ACT.Sigmoid).then_inc(s["ple_sig"], 1)
            if l == 0:
                for m in range(1, 4):
                    high_out(e + 1, m)
            square_out(e + 1, KT_D - 1)
            if l == 0:
                for m in range(4, KT_D):
                    high_out(e + 1, m)
            else:
                scaled_out(KT_D - 1)

        rows = 0
        for src in [a[nm].rearrange("l (m p) -> (l m) p", p=P) for nm in ("ffn1_norm", "mix_norm", "ffn2_norm", "ple_norm")] + \
                [a["final_norm"].rearrange("(m p) -> m p", p=P)] + \
                [a[nm].rearrange("l (m p) -> (l m) p", p=P) for nm in ("gla_gn", "hgrn_gn", "gla_b_gk", "hgrn_lower_bounds")]:
            k = src.shape[0]
            act.dma_start(ROWS[rows:rows + k, :], src).then_inc(s["const_dma"], 16)
            rows += k
        act.wait_ge(s["pool_const"], 1)
        act.wait_ge(s["vec_made"], 1)
        for m in range(KT_D):
            tile_out(0, m, m)
            if m in (1, 4):
                high(m // 4, 0)
        act.wait_ge(s["lb_a"], 1)
        act.activation(lbd[:, 1, :], lbd[:, 0, :], ACT.Abs).then_inc(s["lb_b"], 1)
        act.wait_ge(s["lb_b"], 1)
        act.activation(lbd[:, 2, :], lbd[:, 1, :], ACT.Exp, scale=-1.0).then_inc(s["lb_b"], 1)
        act.wait_ge(s["lb_b"], 2)
        act.activation(lbd[:, 5, :], lbd[:, 2, :], ACT.Ln, bias=consts[:, 1:2]).then_inc(s["lb_c"], 1)
        for l in range(2):
            ffn(2 * l)
            for g in range(2):
                features(GROUPS[2 * l + g])
                mix(GROUPS[2 * l + g])
            out_proj(l)
            ffn(2 * l + 1)
            ple(l)
        act.wait_ge(s["norm_mm"], 9)
        act.activation(rstdT[:, 0:4], ps[:, 6, 0:4], ACT.Ln, bias=consts[:, 0:1], scale=1.0 / D).then_inc(s["ln_done"], 1)
        act.activation(rstdT[0:T_SAMPLE, 4:5], ps[0:T_SAMPLE, 6, 4:5], ACT.Ln, bias=consts[0:T_SAMPLE, 0:1], scale=1.0 / D)\
           .then_inc(s["ln_done"], 1)
        act.wait_ge(s["ln_done"], N_LN)
        act.activation(rstdT[:, 0:4], rstdT[:, 0:4], ACT.Exp, scale=-0.5).then_inc(s["rstd_done"], 1)
        act.activation(rstdT[0:T_SAMPLE, 4:5], rstdT[0:T_SAMPLE, 4:5], ACT.Exp, scale=-0.5).then_inc(s["rstd_done"], 1)
        act.wait_ge(s["rstd_done"], 10)
        for c in (1, 3):
            act.wait_ge(s["y_turned"], c + 1)
            act.activation(YT[:, c, :], psf[:, 1024 * c:1024 * c + D], ACT.Copy, scale=rstdT[:, c:c + 1]).then_inc(s["y_out_a"], 1)

    @block.vector
    def _(dve):
        def low(base, i, j=0):
            n = base + j
            slot = n % RING
            dve.wait_ge(s["hi_made"], i + (n + 1))
            dve.tensor_tensor(WL[:, slot, :], RAW[:, slot, :], WH[:, slot, :].bitcast(F32), ALU.subtract)\
               .then_inc(s["lo_made"], 1)

        def ahead(n):
            if n + 2 < N_UNITS:
                low(n + 2, 0)

        def tile_low(e, m):
            if e == 8:
                return
            dve.wait_ge(s["uh_done"], m + (8 * e + 1))
            sc = gains[:, gain_row(e), m:m + 1] if isinstance(m, int) else gains[:, gain_row(e), bass.ds(m, 1)]
            dve.scalar_tensor_tensor(out=flat_of(UL, m), in0=flat_of(H, m), scalar=sc,
                                     in1=flat_of(UH, m).bitcast(F32), op0=ALU.mult, op1=ALU.subtract)\
               .then_inc(s["u_done"], 1)

        def ffn(F):
            base, e = START["ffn", F], 2 * F

            def chunk(i4, f, j):
                bank = 2 * j
                if not isinstance(f, int) or NF * F + f > 0:
                    dve.wait_ge(s["hid_done"], f + NF * F)
                low(base, i4, j + 2)
                low(base, i4, j + 3)
                dve.wait_ge(s["mm_units"], i4 + (base + j + 2))
                dve.wait_ge(s["rstd_done"], e + 1)
                dve.tensor_tensor(halves(tG[:, :]), pair(bank), halves(rstd[:, :]), ALU.mult).then_inc(s["tg_done"], 1)
                dve.tensor_tensor(halves(tU[:, :]), pair(bank + 2), halves(rstd[:, :]), ALU.mult).then_inc(s["up_evicted"], 1)
                dve.wait_ge(s["hid_hi"], f + (NF * F + 1))
                dve.tensor_tensor(flat_of(HL, f), tU[:, :], flat_of(HH, f).bitcast(F32), ALU.subtract)\
                   .then_inc(s["hid_done"], 1)

            for c in range(2):
                chunk(0, c, 2 * c)
            with dve.Fori(1, NF // 2) as i:
                for c in range(2):
                    chunk(i * 4, i * 2 + c, 2 * c)
            base += UP_UNITS
            with dve.Fori(0, 2) as i:
                for m4 in range(4):
                    for u in range(3):
                        low(base, i * 12, 3 * m4 + u + 2)
                    m = i * 4 + m4
                    dve.wait_ge(s["mm_units"], i * 12 + (base + 3 * m4 + 3))
                    dve.scalar_tensor_tensor(out=tile_of(H, m), in0=pair(2 * m4), scalar=0.5, in1=tile_of(H, m),
                                             op0=ALU.mult, op1=ALU.add).then_inc(s["h_done"], 1)
                    tile_low(e + 1, m)

        def feature_out(gr, j, n, dst, scale=None):
            dve.wait_ge(s["mm_units"], n + 1)
            dve.wait_ge(s["rstd_done"], gr.norm + 1)
            src = pair(gr.feat_bank(j))
            if scale is None:
                dve.tensor_tensor(halves(dst), src, halves(rstd[:, :]), ALU.mult).then_inc(s["feat_out"], 1)
            else:
                dve.scalar_tensor_tensor(out=halves(dst), in0=src, scalar=scale, in1=halves(rstd[:, :]),
                                         op0=ALU.mult, op1=ALU.mult).then_inc(s["feat_out"], 1)

        def gates_out(heads):
            for h in heads:
                dve.wait_ge(s["gk_mm"], h + 1)
                dve.tensor_scalar(halves(G[:, h, :] if h < 2 else OG[:, 4 + h, :]), pair(2 * h), bgk[:, h:h + 1],
                                  None, ALU.add).then_inc(s["x_out"], 1)

        def features(gr):
            n = gr.start
            dests = ([(RT, None)] if gr.has_r else []) + \
                [(Q[:, h, :], gr.q_scale if gr.gla else None) for h in range(gr.NH)] + \
                [(K[:, h, :], None) for h in range(gr.NH)]
            for j, (dst, scale) in enumerate(dests):
                ahead(n)
                feature_out(gr, j, n, dst, scale)
                n += 1
                if gr.has_r and j >= gr.nfeat - 2:
                    gates_out(range(2) if j == gr.nfeat - 2 else (2,))
            if gr.gi == 1:
                dve.wait_ge(s["x_out"], 4)
                dve.tensor_copy(G[:, 0:2, :], OG[:, 6:8, :]).then_inc(s["x_made"], 1)
                dve.wait_ge(s["x_made"], 1)
            if gr.gla:
                gate(gr)
            for kind, j, lv in gr.steps:
                if kind:
                    ahead(n)
                    n += 1
                if lv == "diag":
                    if kind == "g":
                        feature_out(gr, gr.nfeat + j, n - 1, OG[:, 4 * gr.g + j, :])
                    if gr.has_r:
                        gates_out((3,))
                    if not gr.gla:
                        gate_end(gr)
                    diagonal(gr)
                    continue
                if not gr.gla and kind == "g" and j < 2:
                    if j == 1:
                        feature_out(gr, gr.nfeat, n - 2, OG[:, 4 * gr.g, :])
                        gate(gr)
                        feature_out(gr, gr.nfeat + 1, n - 1, OG[:, 4 * gr.g + 1, :])
                    continue
                if lv is not None:
                    level(gr, lv)
                if kind == "g":
                    feature_out(gr, gr.nfeat + j, n - 1, OG[:, 4 * gr.g + j, :])

        def diagonal(gr):
            dve.wait_ge(s["diag_mm"], gr.gi + 1)
            X = gr.NH * NCH
            dve.tensor_tensor(AT[:, 0:X, :], psf[:, 2048:2048 + X * P].rearrange("p (x n) -> p x n", x=X),
                              ident[:, :].rearrange("p (o n) -> p o n", o=1).to_broadcast([P, X, P]),
                              ALU.mult).then_inc(s["diag_out"], 1)

        def level_out(gr, l):
            gi, NH = gr.gi, gr.NH
            n, L = LEVELS * gi + l, 1 << l
            b0 = gr.level_bank(l)
            dve.wait_ge(s["lvl_mm"], n + 1)
            if l == 0:
                dve.tensor_tensor(ATS[:, 0:NH, :], ps[:, 6, 0:NH * 32].rearrange("p (x n) -> p x n", x=NH),
                                  ident[:, SROW:P].rearrange("p (o n) -> p o n", o=1).to_broadcast([P, NH, 32]),
                                  ALU.mult).then_inc(s["sdiag_out"], 1)
                dve.wait_ge(s["diag_out"], gi + 1)
                dve.wait_ge(s["sdiag_out"], gi + 1)
            else:
                dve.wait_ge(s["lvl_out"], n)
            if l == 1:
                dve.wait_ge(s["slvl_out"], 2 * gi + 1)
            X = NH * NCH
            dst = AT[:, 0:X, :].rearrange("p x (n l) -> p x n l", l=2 * L)[:, :, :, L:2 * L]
            data = psf[:, 512 * b0:512 * b0 + 64 * X].rearrange("p (x n l) -> p x n l", x=X, l=L)
            msk = masks[:, l, :].bitcast(U32).rearrange("p (o n l) -> p o n l", o=1, l=L).to_broadcast([P, X, 64 // L, L])
            dve.copy_predicated(dst, msk, data).then_inc(s["lvl_out"], 1)
            if l < 2:
                dst = ATS[:, 0:NH, :].rearrange("p x (n l) -> p x n l", l=2 * L)[:, :, :, L:2 * L]
                data = ps[:, 6, (8 + 4 * l) * 16:(8 + 4 * l + NH) * 16].rearrange("p (x n l) -> p x n l", x=NH, l=L)
                msk = masks[:, l, 48:64].bitcast(U32).rearrange("p (o n l) -> p o n l", o=1, l=L)\
                    .to_broadcast([P, NH, 16 // L, L])
                dve.copy_predicated(dst, msk, data).then_inc(s["slvl_out"], 1)

        def level(gr, l):
            gi, NH = gr.gi, gr.NH
            n, L = LEVELS * gi + l, 1 << l
            both = l < 2
            n1 = (LEVELS - 1) * gi + l
            g1, g2, tot = blocks(G, gr, L, both)
            dk = compact(EX[:, 0:2 * T], gr, L, both)
            dve.wait_ge(s["gate_made"], (LEVELS + 1) * gi + l + 1)
            if l:
                dve.tensor_tensor(dk, tot.to_broadcast(g1.shape), g1, ALU.subtract).then_inc(s["diff_made"], 1)
            dve.wait_ge(s["eq_made"], n + 1)
            dve.tensor_tensor(g2, g2, tot.to_broadcast(g2.shape), ALU.add).then_inc(s["gate_made"], 1)
            if l == 0:
                return
            dve.wait_ge(s["diff_made"], n1)
            if l == 1:
                dve.wait_ge(s["kt_zero"], gi + 1)
                if not gr.gla:
                    dve.wait_ge(s["k_made"], gi - 1)
            dve.wait_ge(s["ek_made"], n1)
            k1, _, _ = blocks(K, gr, L, both)
            kt = KTb[:, l % 2, 0:NH * T].rearrange("p (h t) -> p h t", t=T)
            kt1, _, _ = blocks(kt, gr, L, both)
            dve.tensor_tensor(kt1, k1, dk, ALU.mult).then_inc(s["kt_made"], 1)
            dve.wait_ge(s["kt_made"], n1)
            if 0 < l < LEVELS - 1:
                level_out(gr, l - 1)

        def gate(gr):
            gi = gr.gi
            if gr.gla:
                dve.wait_ge(s["gate_ln"], gi + 1)
                gf = G[:, 0:2, :].rearrange("p h t -> p (h t)")
                dve.scalar_tensor_tensor(out=gf, in0=gf, scalar=0.0, in1=EX[:, 0:2 * T], op0=ALU.min, op1=ALU.subtract)\
                   .then_inc(s["gate_made"], 1)
                return
            k = gr.gi - 1
            gf = G[:].rearrange("p h t -> p (h t)")
            kf = K[:].rearrange("p h t -> p (h t)")
            dve.wait_ge(s["gate_ln"], gr.gi + 1)
            dve.scalar_tensor_tensor(out=gf, in0=kf, scalar=0.0, in1=EX[:, :], op0=ALU.min, op1=ALU.subtract)\
               .then_inc(s["ls_made"], 1)
            dve.wait_ge(s["ls_made"], k)
            for h in range(4):
                ins = dve.tensor_scalar(G[:, h, :], G[:, h, :], L1M[:, gr.h0 + h:gr.h0 + h + 1], None, ALU.add)
            ins.then_inc(s["c_made"], 1)
            dve.wait_ge(s["c_made"], k)
            dve.tensor_tensor(kf, gf, kf, ALU.subtract).then_inc(s["kx_made"], 1)
            for h in range(4):
                ins = dve.tensor_scalar(EX[:, h * T:(h + 1) * T], G[:, h, :], LLB[:, gr.h0 + h:gr.h0 + h + 1], None, ALU.subtract)
            ins.then_inc(s["gd_made"], 1)

        def gate_end(gr):
            k = gr.gi - 1
            dve.wait_ge(s["gd_ln"], k)
            for h in range(4):
                ins = dve.scalar_tensor_tensor(out=G[:, h, :], in0=G[:, h, :], scalar=LLB[:, gr.h0 + h:gr.h0 + h + 1],
                                               in1=EX[:, h * T:(h + 1) * T], op0=ALU.max, op1=ALU.add)
            ins.then_inc(s["gate_made"], 1)

        def mix(gr):
            gi, NH = gr.gi, gr.NH
            dve.wait_ge(s["qt_made"], LEVELS * (gi + 1))
            dve.wait_ge(s["gate_made"], (LEVELS + 1) * (gi + 1))
            ex3 = EX[:, 0:NH * T].rearrange("p (h t) -> p h t", t=T)
            for t0, t1, L in ((0, T_PROMPT, CHUNK), (T_PROMPT, T, T_SEQ)):
                g4 = G[:, 0:NH, t0:t1].rearrange("p h (n l) -> p h n l", l=L)
                e4 = ex3[:, :, t0:t1].rearrange("p h (n l) -> p h n l", l=L)
                dve.tensor_tensor(e4, g4[:, :, :, L - 1:L].to_broadcast(g4.shape), g4, ALU.subtract).then_inc(s["ksuf_made"], 1)
            level_out(gr, LEVELS - 2)
            dve.wait_ge(s["ksuf_exp"], gi + 1)
            dve.tensor_tensor(K[:, 0:NH, :], K[:, 0:NH, :], ex3, ALU.mult).then_inc(s["kdec_made"], 1)
            dve.wait_ge(s["chunk_exp"], gi + 1)
            dve.tensor_tensor(Q[:, 0:NH, :], Q[:, 0:NH, :], EP[:, 0:NH * T].rearrange("p (h t) -> p h t", t=T), ALU.mult)\
               .then_inc(s["qin_made"], 1)
            level_out(gr, LEVELS - 1)
            dve.wait_ge(s["qin_made"], gi + 1)
            dve.wait_ge(s["dec_made"], 2 * gi + 2)
            dve.wait_ge(s["u_mm"], 4 * gi + 1)
            dve.tensor_copy(ST[:, 0, :], ps[:, 0, :]).then_inc(s["s_made"], 1)
            for c in range(1, NCH):
                dve.wait_ge(s["u_mm"], 4 * gi + c + 1)
                dve.wait_ge(s["s_made"], 4 * gi + c)
                for h in range(NH):
                    hv = slice(h * gr.V, (h + 1) * gr.V)
                    ins = dve.scalar_tensor_tensor(out=ST[:, c, hv], in0=ST[:, c - 1, hv], scalar=DEC[:, h, c:c + 1],
                                                   in1=ps[:, c, hv], op0=ALU.mult, op1=ALU.add)
                ins.then_inc(s["s_made"], 1)

            dve.wait_ge(s["os_mm"], gi + 1)
            dve.tensor_copy(Q[:, :, T_PROMPT:T], ps[:, 0, 0:P].rearrange("p (j t) -> p j t", j=4)).then_inc(s["o_out"], 1)
            for j in range(4):
                dve.wait_ge(s["o_mm"], 4 * gi + max(j, min(3, (j + 1) * gr.vt_per_head - 1)) + 1)
                dve.tensor_copy(Q[:, j, 0:T_PROMPT], ps[:, 4 + j, :]).then_inc(s["o_out"], 1)

            def sequence(b):
                dve.wait_ge(s["us_mm"], N_SEQ * gi + b + 1)
                for h in range(NH):
                    hv = slice(h * gr.V, (h + 1) * gr.V)
                    ins = dve.scalar_tensor_tensor(out=S0[:, b, hv], in0=S0[:, b, hv], scalar=DECS[:, h, b:b + 1],
                                                   in1=ps[:, 2 + b % 2, hv], op0=ALU.mult, op1=ALU.add)
                ins.then_inc(s["snew_made"], 1)

            dve.wait_ge(s["og_silu"], gi + 1)
            for j in range(4):
                col = j % 2 if gr.gla else 2
                og = OG[:, 4 * gr.g + j, :]
                dve.wait_ge(s["o_out"], 5 * gi + j + 2)
                dve.scalar_tensor_tensor(out=og, in0=og, scalar=gn[:, col:col + 1], in1=Q[:, j, :],
                                         op0=ALU.mult, op1=ALU.mult).then_inc(s["og_pre"], 1)
            for b in range(N_SEQ - 2):
                sequence(b)
            for j in range(2):
                og = OG[:, 4 * gr.g + j, :]
                dve.wait_ge(s["og_pre"], 4 * gi + j + 1)
                dve.wait_ge(s["ors_made"], N_HEADS[gi] + j // gr.vt_per_head + 1)
                dve.tensor_tensor(og, og, ORS[:, j // gr.vt_per_head, :], ALU.mult).then_inc(s["og_made"], 1)
            if gr.g == 1:
                dve.wait_ge(s["us_mm"], N_SEQ * (gi + 1))
                out_low(gr.layer, range(4))
            for b in range(N_SEQ - 2, N_SEQ):
                sequence(b)
            dve.wait_ge(s["og_made"], 2 * gi + 2)
            dve.wait_ge(s["og_made_p"], 2 * gi + 2)

        def out_low(l, tiles):
            for kk in tiles:
                dve.wait_ge(s["out_hi"], 8 * l + kk + 1)
                dve.tensor_tensor(OL[:, kk, :], OG[:, kk, :], OH[:, kk, :].bitcast(F32), ALU.subtract).then_inc(s["out_lo"], 1)

        def out_proj(l):
            e = 4 * l + 2
            out_low(l, range(4, KT_D))
            for m in range(KT_D):
                ahead(START["out", l] + m)
                dve.wait_ge(s["mm_units"], START["out", l] + m + 1)
                dve.tensor_tensor(tile_of(H, m), pair(2 * (m % 4)), tile_of(H, m), ALU.add).then_inc(s["h_done"], 1)
                tile_low(e, m)

        def ple(l):
            e, n = 4 * l + 3, START["ple", l]

            def residual(m):
                dve.wait_ge(s["ple_sig"], 8 * l + m + 1)
                dve.tensor_tensor(GT[:, m, :], PX[:, m, :], GT[:, m, :], ALU.mult).then_inc(s["ple_x"], 1)
                dve.wait_ge(s["ple_x"], 8 * l + m + 1)
                dve.tensor_tensor(H[:, m, :], H[:, m, :], GT[:, m, :], ALU.add).then_inc(s["h_done"], 1)

            for i, m in enumerate(PLE_ORDER):
                ahead(n + i)
                if m == 0:
                    dve.wait_ge(s["p_turned"], l + 1)
                    for kt in range(2):
                        dve.tensor_copy(PT[:, kt, 0:T_PROMPT], ps[:, 6 + kt, :]).then_inc(s["p_feat"], 1)
                        dve.tensor_copy(PT[:, kt, T_PROMPT:T], ps[:, 1, p_sample_col(kt):p_sample_col(kt) + T_SAMPLE])\
                           .then_inc(s["p_feat"], 1)
                if m is not None:
                    if m == 2:
                        residual(0)
                    if m >= 2:
                        residual(m - 1)
                    dve.wait_ge(s["mm_units"], n + i + 1)
                    dve.wait_ge(s["rstd_done"], e + 1)
                    dve.tensor_tensor(halves(GT[:, m, :]), pair(2 * (m % 4)), halves(rstd[:, :]), ALU.mult).then_inc(s["ple_t"], 1)
                    if m == 0:
                        for kt in range(2):
                            dve.wait_ge(s["p_hi"], 2 * l + kt + 1)
                            dve.tensor_tensor(PL[:, kt, :], PT[:, kt, :], PH[:, kt, :].bitcast(F32), ALU.subtract).then_inc(s["p_lo"], 1)
                    continue
                for j in range(4 * (i - 2), 4 * (i - 2) + 4):
                    if j % 4 == 3:
                        dve.wait_ge(s["mm_units"], n + i + 1)
                    else:
                        dve.wait_ge(s["ple_mm"], 6 * l + 3 * (j // 4) + j % 4 + 1)
                    dve.tensor_copy(halves(PX[:, j, :]), pair(2 * ((j + 2) % 4))).then_inc(s["p_out"], 1)
            tile_low(e + 1, 0)
            residual(KT_D - 1)
            for m in range(1, KT_D):
                tile_low(e + 1, m)

        dve.memset(ones[:, :], 1.0).then_inc(s["dve_const"], 1)

        def x_out(m):
            dve.wait_ge(s["x_turned"], m + 1)
            dve.tensor_copy(H[:, m, :], psf[:, 1024 * (m % 4):1024 * (m % 4) + T]).then_inc(s["h_done"], 1)

        x_out(0)
        dve.wait_ge(s["vec_turned"], 1)
        dve.tensor_copy(vecs[:, :], ps[:, 7, 0:VROWS]).then_inc(s["vec_made"], 1)
        for m in range(KT_D):
            if m + 1 < KT_D:
                x_out(m + 1)
            dve.wait_ge(s["h_done"], m + 1)
            tile_low(0, m)
            if m in (1, 5):
                low(m // 4, 0)
        dve.wait_ge(s["vec_made"], 1)
        dve.tensor_tensor(lbd[:, 0, :], lbr[:, 0, :], lbr[:, 1, :], ALU.subtract).then_inc(s["lb_a"], 1)
        dve.wait_ge(s["lb_a"], 1)
        dve.tensor_scalar(lbd[:, 4, :], lbd[:, 0, :], -1.0, None, ALU.mult).then_inc(s["lb_a"], 1)

        def bounds():
            dve.wait_ge(s["lb_a"], 2)
            dve.wait_ge(s["lb_c"], 1)
            dve.scalar_tensor_tensor(out=LLB, in0=lbd[:, 4, :], scalar=0.0, in1=lbd[:, 5, :], op0=ALU.min, op1=ALU.subtract)\
               .then_inc(s["lb_done"], 1)
            dve.scalar_tensor_tensor(out=L1M, in0=lbd[:, 0, :], scalar=0.0, in1=lbd[:, 5, :], op0=ALU.min, op1=ALU.subtract)\
               .then_inc(s["lb_done"], 1)
            dve.wait_ge(s["lb_done"], 2)

        for l in range(2):
            ffn(2 * l)
            if l == 1:
                bounds()
            for g in range(2):
                features(GROUPS[2 * l + g])
                mix(GROUPS[2 * l + g])
            out_proj(l)
            ffn(2 * l + 1)
            ple(l)
        dve.wait_ge(s["rstd_done"], 10)
        for c in (0, 2, 4):
            rows = P if c < 4 else T_SAMPLE
            dve.wait_ge(s["y_turned"], c + 1)
            dve.tensor_scalar(YT[0:rows, c, :], psf[0:rows, 1024 * (c % 4):1024 * (c % 4) + D], rstdT[0:rows, c:c + 1],
                              None, ALU.mult).then_inc(s["y_out_v"], 1)

    @block.gpsimd
    def _(pool):
        def square_in(e, m, mc, first):
            pool.wait_ge(s["sq_done"], m + (8 * e + 1))
            if first:
                pool.tensor_copy(ssq[:, :], (tG, tU)[mc % 2][:, :]).then_inc(s["ssq_added"], 1)
            else:
                pool.wait_ge(s["ssq_added"], m + 8 * e)
                pool.tensor_tensor(ssq[:, :], ssq[:, :], (tG, tU)[mc % 2][:, :], ALU.add).then_inc(s["ssq_added"], 1)

        def squares(e):
            for m in range(KT_D):
                square_in(e, m, m, m == 0)

        def ffn(F):
            with pool.Fori(0, NF) as f:
                pool.wait_ge(s["silu_done"], f + (NF * F + 1))
                pool.wait_ge(s["up_evicted"], f + (NF * F + 1))
                pool.tensor_tensor(tU[:, :], tG[:, :], tU[:, :], ALU.mult).then_inc(s["hid_mul"], 1)
            squares(2 * F + 1)

        def mix(gr):
            gi, NH = gr.gi, gr.NH
            if gr.g == 0:
                pool.wait_ge(s["h_done"], 8 * gr.norm + 8)
            pool.memset(KTb[:], 0.0).then_inc(s["kt_zero"], 1)
            if gr.has_r:
                pool.wait_ge(s["kt_zero"], 1)
                pool.dma_start(KTb[P - 16:P, 1, 0:512], a["gla_w_gk_up"][0]).then_inc(s["w_gkup_in"], 16)
            for l in range(LEVELS):
                n, L = LEVELS * gi + l, 1 << l
                both = l < 2
                pool.wait_ge(s["eq_made"], n + 1)
                if l >= 2:
                    pool.wait_ge(s["lvl_mm"], n - 1)
                if l == 0:
                    pool.wait_ge(s["feat_out"], gr.feat0 + gr.nfeat)
                    if not gr.gla:
                        pool.wait_ge(s["q_made"], gi - 1)
                _, q2, _ = blocks(Q, gr, L, both)
                pool.tensor_tensor(compact(QTb[:, l % 2, :], gr, L, both), q2, compact(EX[:, 2 * T:4 * T], gr, L, both),
                                   ALU.mult).then_inc(s["qt_made"], 1)
            for j in (2, 3):
                og = OG[:, 4 * gr.g + j, :]
                pool.wait_ge(s["og_pre"], 4 * gi + j + 1)
                pool.wait_ge(s["ors_made"], N_HEADS[gi] + j // gr.vt_per_head + 1)
                pool.tensor_tensor(og, og, ORS[:, j // gr.vt_per_head, :], ALU.mult).then_inc(s["og_made_p"], 1)
            pool.wait_ge(s["out_state"], 16 * N_STATE[gi + 1])

        pool.memset(ident[:, :], 0.0).then_inc(s["pc"], 1)
        pool.memset(masks[:], 1.0).then_inc(s["pc"], 1)
        pool.memset(seqmask[:, :], 1.0).then_inc(s["pc"], 1)
        pool.memset(consts[:, 0:1], EPS).then_inc(s["pc"], 1)
        pool.memset(consts[:, 1:2], 1.0).then_inc(s["pool_const"], 1)
        pool.wait_ge(s["pc"], 4)
        pool.affine_select(out=ident[:, :], in_=ident[:, :], compare_op=ALU.not_equal, fill=1.0, base=0,
                           pattern=[[-1, P]], channel_multiplier=1).then_inc(s["ident_made"], 1)
        for l in range(LEVELS):
            L = 1 << l
            mv = masks[:, l, :].rearrange("p (n l) -> p n l", l=L)
            pool.affine_select(out=mv, in_=mv, compare_op=ALU.is_ge, fill=0.0, base=0,
                               pattern=[[-2 * L, 64 // L], [0, L]], channel_multiplier=1).then_inc(s["pc"], 1)
            pool.wait_ge(s["pc"], 5 + 2 * l)
            pool.affine_select(out=mv, in_=mv, compare_op=ALU.is_ge, fill=0.0, base=L - 1,
                               pattern=[[2 * L, 64 // L], [0, L]], channel_multiplier=-1).then_inc(s["pc"], 1)
            pool.wait_ge(s["pc"], 6 + 2 * l)
        pool.affine_select(out=seqmask[:, :], in_=seqmask[:, :], compare_op=ALU.is_ge, fill=0.0, base=-SROW,
                           pattern=[[-T_SEQ, N_SEQ]], channel_multiplier=1).then_inc(s["pc"], 1)
        pool.wait_ge(s["pc"], 5 + 2 * LEVELS)
        pool.affine_select(out=seqmask[:, :], in_=seqmask[:, :], compare_op=ALU.is_ge, fill=0.0, base=SROW + T_SEQ - 1,
                           pattern=[[T_SEQ, N_SEQ]], channel_multiplier=-1).then_inc(s["masks_made"], 1)
        squares(0)
        for l in range(2):
            ffn(2 * l)
            for g in range(2):
                mix(GROUPS[2 * l + g])
            squares(4 * l + 2)
            ffn(2 * l + 1)
            squares(4 * l + 4)


_INS = ["x_prompt", "x_sample", "state_gla", "state_hgrn", "p_prompt", "p_sample", "ffn1_norm", "ffn1_w_gu",
        "ffn1_w_down", "mix_norm", "gla_w_in", "gla_w_gk_up", "gla_b_gk", "gla_gn", "gla_w_out", "hgrn_w_in",
        "hgrn_gn", "hgrn_w_out", "hgrn_lower_bounds", "ffn2_norm", "ffn2_w_gu", "ffn2_w_down", "ple_norm",
        "ple_w_gate", "ple_w_proj", "final_norm"]
_OUTS = [("y_p", (1, T_PROMPT, D)), ("y_s", (N_SEQ, T_SEQ, D)), ("gla_p", (1, 1, 4, 128, 256)),
         ("gla_s", (1, N_SEQ, 4, 128, 256)), ("hgrn_p", (1, 1, 8, 128, 128)), ("hgrn_s", (1, N_SEQ, 8, 128, 128))]


def kernel(**inputs):
    import numpy as _np
    import concourse.bacc as _bacc
    from concourse import mybir as _mybir
    from concourse.bass_utils import run_bass_kernel_spmd as _run

    nc = _bacc.Bacc("TRN2", target_bir_lowering=False, num_devices=1)
    arrays, a, o = {}, {}, {}
    for name in _INS:
        x = _np.ascontiguousarray(inputs[name])
        arrays[f"in_{name}_dram"] = x
        a[name] = nc.dram_tensor(f"in_{name}_dram", x.shape, _mybir.dt.from_np(x.dtype), kind="ExternalInput").ap()
    for name, shape in _OUTS:
        o[name] = nc.dram_tensor(f"out_{name}_dram", shape, _mybir.dt.float32, kind="ExternalOutput").ap()
    build(nc, a, o)
    r = _run(nc, [arrays], core_ids=[0])
    return tuple(r.results[0][f"out_{name}_dram"] for name, _ in _OUTS)
```
